# Optimizing a Trainium2 kernel written in Bass

```python
import math
import jax, jax.numpy as jnp
from jax import lax
import numpy as np

D_MODEL = 1024
BATCH = 1
SEQ = 128
DEPTH = 2
DEC_BATCH = 1
DEC_SEQ = 512
PAST_LEN = 128

GRID_W = 64
N_MIXERS = 3
LAYER_MIXER = tuple(i % N_MIXERS for i in range(DEPTH))
N_MLA_LAYERS = LAYER_MIXER.count(0)
N_RET_LAYERS = LAYER_MIXER.count(1)
N_FNET_LAYERS = LAYER_MIXER.count(2)

MLA_HEADS = 8
MLA_NOPE = 128
MLA_ROPE = 64
MLA_V = 128
MLA_Q_LORA = 384
MLA_KV_LORA = 256
ROPE_BASE = 10000.0
Q_BLOCK = 128
RET_HEADS = 4
RET_DK = D_MODEL // RET_HEADS
RET_DV = 2 * D_MODEL // RET_HEADS
RET_CHUNK = 128
FNET_GROUPS = 4
FNET_GROUP_DIM = D_MODEL // FNET_GROUPS
N_EXPERTS = 16
N_EXPERT_GROUPS = 4
EXPERTS_PER_GROUP = N_EXPERTS // N_EXPERT_GROUPS
TOP_K = 2
D_EXPERT = 512
MOE_BLOCK = 128
NORM_EPS = 1e-6

kernel_name = 'hybrid_mla_retention_fnet_moe_diffusion_step'

def rmsnorm(x, g=None):
    xf = x.astype(jnp.float32)
    y = xf * lax.rsqrt(jnp.mean(xf * xf, axis=-1, keepdims=True) + NORM_EPS)
    if g is not None:
        y = y * g.astype(jnp.float32)
    return y.astype(x.dtype)

def modulation(cond, w, b):
    m = jax.nn.silu(cond) @ w + b
    return jnp.split(m, 6, axis=-1)

def modulate(x, g, shift, scale):
    return rmsnorm(x, g) * (1 + scale[:, None, :]) + shift[:, None, :]

def rotate(x, cos, sin):
    half = x.shape[-1] // 2
    x1, x2 = x[..., :half], x[..., half:]
    return jnp.concatenate([x1 * cos - x2 * sin, x1 * sin + x2 * cos], axis=-1)

def axial_angles(n_tokens):
    n_rows = n_tokens // GRID_W
    row = jnp.repeat(jnp.arange(n_rows), GRID_W).astype(jnp.float32)
    col = jnp.tile(jnp.arange(GRID_W), n_rows).astype(jnp.float32)
    axis_dim = MLA_ROPE // 2
    inv = ROPE_BASE ** (-jnp.arange(0, axis_dim, 2, dtype=jnp.float32) / axis_dim)
    return row[:, None] * inv[None, :], col[:, None] * inv[None, :]

def apply_axial_rope(x, ang_r, ang_c):
    axis_dim = MLA_ROPE // 2
    shape = ang_r.shape[:1] + (1,) * (x.ndim - 3) + ang_r.shape[1:]
    def rot(part, ang):
        ang = ang.reshape(shape)
        return rotate(part, jnp.cos(ang).astype(x.dtype), jnp.sin(ang).astype(x.dtype))
    return jnp.concatenate([rot(x[..., :axis_dim], ang_r), rot(x[..., axis_dim:], ang_c)], axis=-1)

def block_attention(q, k, v):
    b, tq, h, dq = q.shape
    nb = tq // Q_BLOCK
    qb = q.reshape(b, nb, Q_BLOCK, h, dq).transpose(1, 0, 2, 3, 4)
    scale = dq ** -0.5
    def one(qblk):
        s = jnp.einsum('bqhd,bkhd->bhqk', qblk, k, preferred_element_type=jnp.float32) * scale
        p = jax.nn.softmax(s, axis=-1).astype(v.dtype)
        return jnp.einsum('bhqk,bkhd->bqhd', p, v)
    o = lax.map(one, qb)
    return o.transpose(1, 0, 2, 3, 4).reshape(b, tq, h, v.shape[-1])

def mla_project(h, w_in, q_norm_g, kv_norm_g, w_uq):
    b, t, _ = h.shape
    z = h @ w_in
    cq, ckv, kpe = jnp.split(z, [MLA_Q_LORA, MLA_Q_LORA + MLA_KV_LORA], axis=-1)
    q = (rmsnorm(cq, q_norm_g) @ w_uq).reshape(b, t, MLA_HEADS, MLA_NOPE + MLA_ROPE)
    return q, rmsnorm(ckv, kv_norm_g), kpe

def mla_keys_values(ckv, kpe, w_ukv):
    b, t, _ = ckv.shape
    kv = (ckv @ w_ukv).reshape(b, t, MLA_HEADS, MLA_NOPE + MLA_V)
    k_pe = jnp.broadcast_to(kpe[:, :, None, :], (b, t, MLA_HEADS, MLA_ROPE))
    return jnp.concatenate([kv[..., :MLA_NOPE], k_pe], axis=-1), kv[..., MLA_NOPE:]

def mla_context(h, w_in, q_norm_g, kv_norm_g, w_uq, w_ukv, w_o):
    b, t, _ = h.shape
    q, ckv, kpe = mla_project(h, w_in, q_norm_g, kv_norm_g, w_uq)
    k, v = mla_keys_values(ckv, kpe, w_ukv)
    o = block_attention(q, k, v).reshape(b, t, MLA_HEADS * MLA_V)
    return o @ w_o, jnp.concatenate([ckv, kpe], axis=-1)

def mla_latent(h, ctx_cache, w_in, q_norm_g, kv_norm_g, w_uq, w_ukv, w_o):
    b, t, _ = h.shape
    q, ckv, kpe = mla_project(h, w_in, q_norm_g, kv_norm_g, w_uq)
    ang_r, ang_c = axial_angles(t)
    q = jnp.concatenate([q[..., :MLA_NOPE], apply_axial_rope(q[..., MLA_NOPE:], ang_r, ang_c)], axis=-1)
    kpe = apply_axial_rope(kpe, ang_r, ang_c)
    k_lat, v_lat = mla_keys_values(ckv, kpe, w_ukv)
    k_ctx, v_ctx = mla_keys_values(ctx_cache[..., :MLA_KV_LORA], ctx_cache[..., MLA_KV_LORA:], w_ukv)
    k = jnp.concatenate([k_lat, k_ctx], axis=1)
    v = jnp.concatenate([v_lat, v_ctx], axis=1)
    o = block_attention(q, k, v).reshape(b, t, MLA_HEADS * MLA_V)
    return o @ w_o

def retention_scan(q, k, v, log_g, s0):
    b, h, t, _ = q.shape
    nc = t // RET_CHUNK
    def chunks(a):
        return a.reshape(b, h, nc, RET_CHUNK, a.shape[-1]).transpose(2, 0, 1, 3, 4)
    idx = jnp.arange(RET_CHUNK, dtype=jnp.float32)
    rel = idx[:, None] - idx[None, :]
    lower = rel >= 0
    decay_in = jnp.where(lower, jnp.exp(jnp.where(lower, rel, 0.0)[None] * log_g[:, None, None]), 0.0)
    decay_q = jnp.exp((idx + 1)[None, :] * log_g[:, None])[..., None]
    decay_k = jnp.exp((RET_CHUNK - 1 - idx)[None, :] * log_g[:, None])[..., None]
    decay_chunk = jnp.exp(RET_CHUNK * log_g)[:, None, None]
    def step(s, qkv):
        qc, kc, vc = qkv
        scores = jnp.einsum('bhid,bhjd->bhij', qc, kc) * decay_in
        out = jnp.einsum('bhij,bhje->bhie', scores, vc) + jnp.einsum('bhid,bhde->bhie', qc * decay_q, s)
        s = decay_chunk * s + jnp.einsum('bhjd,bhje->bhde', kc * decay_k, vc)
        return s, out
    s_fin, out = lax.scan(step, s0.astype(jnp.float32), (chunks(q), chunks(k), chunks(v)))
    return out.transpose(1, 2, 0, 3, 4).reshape(b, h, t, -1), s_fin

def retention_mixer(h, s0_f, s0_b, w_in, logit_f, logit_b, w_o, positional):
    b, t, _ = h.shape
    qk = RET_HEADS * RET_DK
    vw = RET_HEADS * RET_DV
    z = h @ w_in
    q, k, v, g_f, g_b = jnp.split(z, [qk, 2 * qk, 2 * qk + vw, 2 * qk + 2 * vw], axis=-1)
    def heads(a, d):
        return a.reshape(b, t, RET_HEADS, d).transpose(0, 2, 1, 3).astype(jnp.float32)
    q = heads(q, RET_DK)
    k = heads(k, RET_DK) * (RET_DK ** -0.5)
    v = heads(v, RET_DV)
    if positional:
        inv = ROPE_BASE ** (-jnp.linspace(0.0, 1.0, RET_DK // 2))
        ang = jnp.arange(t, dtype=jnp.float32)[:, None] * inv[None, :]
        cos, sin = jnp.cos(ang), jnp.sin(ang)
        q = rotate(q, cos, sin)
        k = rotate(k, cos, sin)
    o_f, s_f = retention_scan(q, k, v, jax.nn.log_sigmoid(logit_f.astype(jnp.float32)), s0_f)
    o_b, s_b = retention_scan(q[:, :, ::-1], k[:, :, ::-1], v[:, :, ::-1],
                              jax.nn.log_sigmoid(logit_b.astype(jnp.float32)), s0_b)
    o_b = o_b[:, :, ::-1]
    def gated(o, g):
        o = rmsnorm(o).transpose(0, 2, 1, 3).reshape(b, t, vw)
        return jax.nn.silu(g.astype(jnp.float32)) * o
    y = (gated(o_f, g_f) + gated(o_b, g_b)).astype(h.dtype) @ w_o
    return y, s_f, s_b

def fourier_mixer(h, w):
    b, t, _ = h.shape
    hg = h.astype(jnp.float32).reshape(b, t, FNET_GROUPS, FNET_GROUP_DIM)
    f = jnp.fft.fft2(hg, axes=(1, 3), norm='ortho').real
    return f.reshape(b, t, D_MODEL).astype(h.dtype) @ w

def moe_ffn(h, router_w, router_b, w_gate, w_up, w_down):
    b, t, d = h.shape
    x = h.reshape(b * t, d)
    n = x.shape[0]
    scores = jax.nn.sigmoid(jnp.dot(x, router_w, preferred_element_type=jnp.float32))
    grouped = (scores + router_b.astype(jnp.float32)).reshape(n, N_EXPERT_GROUPS, EXPERTS_PER_GROUP)
    group_score = jnp.sum(lax.top_k(grouped, TOP_K)[0], axis=-1)
    best = jnp.argmax(group_score, axis=-1)
    keep = jnp.arange(N_EXPERT_GROUPS)[None, :] == best[:, None]
    masked = jnp.where(keep[:, :, None], grouped, -jnp.inf).reshape(n, N_EXPERTS)
    _, idx = lax.top_k(masked, TOP_K)
    wts = jnp.take_along_axis(scores, idx, axis=-1)
    wts = wts / jnp.sum(wts, axis=-1, keepdims=True)
    a = n * TOP_K
    flat_e = idx.reshape(a)
    order = jnp.argsort(flat_e)
    e_sorted = flat_e[order]
    tok_sorted = (jnp.arange(a, dtype=jnp.int32) // TOP_K)[order]
    w_sorted = wts.reshape(a)[order]
    counts = jnp.bincount(flat_e, length=N_EXPERTS)
    padded = (counts + MOE_BLOCK - 1) // MOE_BLOCK * MOE_BLOCK
    pad_end = jnp.cumsum(padded)
    pad_start = pad_end - padded
    start = jnp.cumsum(counts) - counts
    dest = pad_start[e_sorted] + jnp.arange(a, dtype=jnp.int32) - start[e_sorted]
    n_blocks = -(-a // MOE_BLOCK) + N_EXPERTS
    rows = n_blocks * MOE_BLOCK
    row_tok = jnp.zeros((rows,), jnp.int32).at[dest].set(tok_sorted)
    row_w = jnp.zeros((rows,), jnp.float32).at[dest].set(w_sorted)
    block_e = jnp.minimum(jnp.searchsorted(pad_end, jnp.arange(n_blocks, dtype=jnp.int32) * MOE_BLOCK,
                                           side='right'), N_EXPERTS - 1)
    def expert_block(args):
        e, tok, wt = args
        xb = x[tok]
        hid = jax.nn.silu(xb @ w_gate[e]) * (xb @ w_up[e])
        return (hid @ w_down[e]) * wt[:, None].astype(x.dtype)
    yb = lax.map(expert_block, (block_e, row_tok.reshape(n_blocks, MOE_BLOCK), row_w.reshape(n_blocks, MOE_BLOCK)))
    y = jnp.zeros_like(x).at[row_tok].add(yb.reshape(rows, d))
    return y.reshape(b, t, d)

def setup_inputs(seed: int = 0) -> dict:
    key = jax.random.key(seed)
    ks = iter(jax.random.split(key, 40))
    def nrm(shape, scale=1.0):
        return jax.random.normal(next(ks), shape, jnp.float32) * scale
    D = D_MODEL
    base = 1.0 - jnp.exp(jnp.linspace(math.log(1.0 / 32), math.log(1.0 / 512), RET_HEADS))
    base_logit = jnp.log(base) - jnp.log1p(-base)
    return {
        'x_prompt': nrm((BATCH, SEQ, D)),
        'x_sample': nrm((DEC_BATCH, DEC_SEQ, D)),
        'cache_mla': nrm((DEC_BATCH, N_MLA_LAYERS, PAST_LEN, MLA_KV_LORA + MLA_ROPE)),
        'state_ret': nrm((DEC_BATCH, N_RET_LAYERS, 2, RET_HEADS, RET_DK, RET_DV), 0.5),
        'c': nrm((DEC_BATCH, D)),
        'c_ctx': nrm((D,)),
        'norm1_g': 1.0 + nrm((DEPTH, D), 0.02),
        'norm2_g': 1.0 + nrm((DEPTH, D), 0.02),
        'ada_w': nrm((DEPTH, D, 6 * D), 0.5 * D ** -0.5),
        'ada_b': nrm((DEPTH, 6 * D), 0.01),
        'final_norm_g': 1.0 + nrm((D,), 0.02),
        'mla_w_in': nrm((N_MLA_LAYERS, D, MLA_Q_LORA + MLA_KV_LORA + MLA_ROPE), D ** -0.5),
        'mla_q_norm_g': 1.0 + nrm((N_MLA_LAYERS, MLA_Q_LORA), 0.02),
        'mla_kv_norm_g': 1.0 + nrm((N_MLA_LAYERS, MLA_KV_LORA), 0.02),
        'mla_w_uq': nrm((N_MLA_LAYERS, MLA_Q_LORA, MLA_HEADS * (MLA_NOPE + MLA_ROPE)), MLA_Q_LORA ** -0.5),
        'mla_w_ukv': nrm((N_MLA_LAYERS, MLA_KV_LORA, MLA_HEADS * (MLA_NOPE + MLA_V)), MLA_KV_LORA ** -0.5),
        'mla_w_o': nrm((N_MLA_LAYERS, MLA_HEADS * MLA_V, D), (MLA_HEADS * MLA_V) ** -0.5),
        'ret_w_in': nrm((N_RET_LAYERS, D, 2 * RET_HEADS * RET_DK + 3 * RET_HEADS * RET_DV), D ** -0.5),
        'ret_decay_f': base_logit[None, :] + nrm((N_RET_LAYERS, RET_HEADS), 0.1),
        'ret_decay_b': base_logit[None, :] + nrm((N_RET_LAYERS, RET_HEADS), 0.1),
        'ret_w_o': nrm((N_RET_LAYERS, RET_HEADS * RET_DV, D), (RET_HEADS * RET_DV) ** -0.5),
        'fnet_w': nrm((N_FNET_LAYERS, D, D), D ** -0.5),
        'router_w': nrm((D, N_EXPERTS), D ** -0.5),
        'router_b': nrm((N_EXPERTS,), 0.01),
        'moe_w_gate': nrm((DEPTH, N_EXPERTS, D, D_EXPERT), D ** -0.5),
        'moe_w_up': nrm((DEPTH, N_EXPERTS, D, D_EXPERT), D ** -0.5),
        'moe_w_down': nrm((DEPTH, N_EXPERTS, D_EXPERT, D), D_EXPERT ** -0.5),
    }

def reference(x_prompt, x_sample, cache_mla, state_ret, c, c_ctx, norm1_g, norm2_g, ada_w, ada_b,
              final_norm_g, mla_w_in, mla_q_norm_g, mla_kv_norm_g, mla_w_uq, mla_w_ukv, mla_w_o,
              ret_w_in, ret_decay_f, ret_decay_b, ret_w_o, fnet_w, router_w, router_b,
              moe_w_gate, moe_w_up, moe_w_down):
    xc, xl = x_prompt, x_sample
    cond_ctx = c_ctx[None, :]
    ctx_mla_states, ctx_ret_states = [], []
    counters = [0, 0, 0]
    for layer in range(DEPTH):
        kind = LAYER_MIXER[layer]
        j = counters[kind]
        counters[kind] += 1
        mod_c = modulation(cond_ctx, ada_w[layer], ada_b[layer])
        mod_l = modulation(c, ada_w[layer], ada_b[layer])
        hc = modulate(xc, norm1_g[layer], mod_c[0], mod_c[1])
        hl = modulate(xl, norm1_g[layer], mod_l[0], mod_l[1])
        if kind == 0:
            oc, ctx_kv = mla_context(hc, mla_w_in[j], mla_q_norm_g[j], mla_kv_norm_g[j],
                                     mla_w_uq[j], mla_w_ukv[j], mla_w_o[j])
            ol = mla_latent(hl, cache_mla[:, j], mla_w_in[j], mla_q_norm_g[j], mla_kv_norm_g[j],
                            mla_w_uq[j], mla_w_ukv[j], mla_w_o[j])
            ctx_mla_states.append(ctx_kv)
        elif kind == 1:
            zero = jnp.zeros((xc.shape[0], RET_HEADS, RET_DK, RET_DV), jnp.float32)
            oc, s_f, s_b = retention_mixer(hc, zero, zero, ret_w_in[j], ret_decay_f[j], ret_decay_b[j],
                                           ret_w_o[j], False)
            ol, _, _ = retention_mixer(hl, state_ret[:, j, 0], state_ret[:, j, 1], ret_w_in[j],
                                       ret_decay_f[j], ret_decay_b[j], ret_w_o[j], True)
            ctx_ret_states.append(jnp.stack([s_f, s_b], axis=1).astype(xc.dtype))
        else:
            oc = fourier_mixer(hc, fnet_w[j])
            ol = fourier_mixer(hl, fnet_w[j])
        xc = xc + mod_c[2][:, None, :] * oc
        xl = xl + mod_l[2][:, None, :] * ol
        hc = modulate(xc, norm2_g[layer], mod_c[3], mod_c[4])
        hl = modulate(xl, norm2_g[layer], mod_l[3], mod_l[4])
        xc = xc + mod_c[5][:, None, :] * moe_ffn(hc, router_w, router_b, moe_w_gate[layer],
                                                 moe_w_up[layer], moe_w_down[layer])
        xl = xl + mod_l[5][:, None, :] * moe_ffn(hl, router_w, router_b, moe_w_gate[layer],
                                                 moe_w_up[layer], moe_w_down[layer])
    y_prompt = rmsnorm(xc, final_norm_g)
    y_sample = rmsnorm(xl, final_norm_g)
    new_cache_mla = jnp.stack(ctx_mla_states, axis=1)
    new_state_ret = jnp.stack(ctx_ret_states, axis=1)
    return (y_prompt, y_sample, new_cache_mla, new_state_ret)


_drawn_inputs = setup_inputs


def setup_inputs(seed=0):
    import zlib

    import numpy as np

    out = dict(_drawn_inputs(seed))
    spreads = {}
    factors = {'cache_mla': 2.699, 'final_norm_g': 2.924, 'mla_q_norm_g': 8.0}
    for name, (base, spread) in spreads.items():
        noise = np.random.default_rng([zlib.crc32(name.encode()), seed]).standard_normal(out[name].shape)
        drawn = base * np.exp(spread * noise) if base else spread * noise
        out[name] = __import__('jax').numpy.asarray(drawn.astype(out[name].dtype))
    for name, factor in factors.items():
        out[name] = (out[name] * factor).astype(out[name].dtype)
    return out
```

```python
from contextlib import ExitStack

import numpy as np

import concourse.bass as bass
import concourse.mybir as mybir
from concourse.alu_op_type import AluOpType as ALU

F32 = mybir.dt.float32
I32 = mybir.dt.int32
U32 = mybir.dt.uint32
ACT = mybir.ActivationFunctionType
AX = mybir.AxisListType

P = 128
D = 1024
KD = D // P
SEQ, LAT, PAST = 128, 512, 128
T = SEQ + LAT
NT = T // P
RANGES = ((0, SEQ, 0), (SEQ, LAT, 1))
DEPTH = 2
EPS = 1e-6
GRID_W = 64
BASE = 10000.0

QL, KVL, ROPE, NOPE, VD, HEADS = 384, 256, 64, 128, 128, 8
KEYS = T + PAST
NKT = KEYS // P
LKEYS = LAT + PAST
PAIRS = HEADS // 2
UQ = NOPE + ROPE
MLA_SCALE = float(UQ) ** -0.5

RH, DK, DV = 4, 256, 512
KSCALE = float(DK) ** -0.5

NE, NG, EG, FE = 16, 4, 4, 512
TOPK = 2
ASSIGNED = T * TOPK
NBLK = (ASSIGNED - NE) // P + NE
BIG = 3.0e38

SLOT = 4096
NSLOT = 6


class Steps:

    def __init__(self, sem, names, ahead=0):
        self.sem, self.per, self.ahead = sem, len(names), ahead
        self.pos = {n: i + 1 for i, n in enumerate(names)}
        assert len(self.pos) == len(names)

    def value(self, name, i=0):
        return i * self.per + (self.pos[name] + self.ahead)

    def before(self, i):
        assert self.ahead
        return i * self.per + self.ahead


BASE_COLS = {"ident": P, "ones": P, "before": P, "iota16": NE, "iota4": NG, "iotab": NBLK}
MLA_COLS = {"swap": P, "rcos": LAT, "rsin": LAT}
RET_COLS = {"relf": LAT, "relb": LAT, "trif": P, "trib": P, "kf": 1, "kb": 1}
TRIG_COLS = {"cos": LAT, "sin": LAT, "idxf": LAT}


def _width(cols):
    return sum(cols.values())


def _views(tile, cols):
    at, out = 0, {}
    for n, w in cols.items():
        out[n] = tile[:, at:at + w]
        at += w
    return out


def shape_constants():
    f = np.float32
    p, m = np.arange(P)[:, None], np.arange(P)[None, :]
    n = np.arange(LAT)[None, :]
    one = np.ones((P, 1), f)
    base = [np.eye(P), np.ones((P, P)), p < m, one * np.arange(NE), one * np.arange(NG),
            one * np.arange(NBLK)]
    d = np.arange(P) % ROPE
    inv = (f(BASE) ** (-np.arange(0, ROPE // 2, 2, dtype=f) / f(ROPE // 2))).astype(f)[d % 16]
    where = np.where((d < 32)[:, None], n // GRID_W, n % GRID_W).astype(f)
    ang = (where * inv[:, None]).astype(f)
    sign = np.where(d % 32 < 16, -1.0, 1.0)[:, None]
    partner = (p // 32) * 32 + (p % 32 + 16) % 32
    mla = [partner == m, np.cos(ang), np.sin(ang) * sign]
    rel_f, rel_b = n - p, p + (LAT - P) - n
    ret = [np.maximum(rel_f, 0), np.maximum(rel_b, 0), m >= p, m <= p, P - 1 - p, p]
    inv = (f(BASE) ** (-np.linspace(0.0, 1.0, DK // 2, dtype=f))).astype(f)
    ang = (n.astype(f) * inv[:, None]).astype(f)
    trig = [np.cos(ang), np.sin(ang), one * (n + 1)]
    return [np.concatenate([np.asarray(a, f) for a in g], axis=1) for g in (base, mla, ret, trig)]


class Chip:

    def __init__(self, nc, stack, ops):
        self.nc, self.ops = nc, ops

        def sb(name, shape, dt=F32):
            return stack.enter_context(nc.sbuf_tensor(name, shape, dt))

        self.ps = stack.enter_context(nc.psum_tensor("ps", [P, 8, 512], F32))
        self.x = sb("x_resid", [P, KD, T])
        self.h = sb("h_normed", [P, KD, T])
        self.ring = sb("weight_ring", [P, NSLOT * SLOT])
        self.base_tile = sb("base_consts", [P, _width(BASE_COLS)])
        self.base = _views(self.base_tile, BASE_COLS)
        self.mod = sb("modulation", [P, DEPTH, 48, 2])
        self.amp = sb("norm_amplitude", [P, DEPTH, 2, KD, 2])
        self.cols_a = sb("norm_gain_and_ada_bias", [P, P])
        self.cols_b = sb("other_columns", [P, 32])
        self.zero2 = sb("no_shift", [P, KD, 2])
        self.fin2 = sb("final_gain", [P, KD, 2])
        self.cond = sb("silu_cond", [P, KD, 2])
        self.router = sb("router_w", [P, KD, NE])
        self.router_b = sb("router_b", [P, NE])
        self.eps = sb("eps", [P, 1])
        self.w12 = sb("route_weights", [P, TOPK, NT])
        self.dest = sb("route_rows", [P, TOPK, NT], I32)
        self.blk_e = sb("block_expert", [P, NBLK], I32)
        self.xs = ops["rows_in"]
        self.ys = ops["rows_out"]

    def slot(self, s, width=SLOT):
        return self.ring[:, s * SLOT:s * SLOT + width]

    def bank2(self, g):
        b = 2 * (g % 4)
        return self.ps[:, b:b + 2, :]


def sems(nc, stack, stage, names):
    return [stack.enter_context(nc.semaphore(f"{stage}_{n}")) for n in names]


def setup(c):
    nc, ops, ps = c.nc, c.ops, c.ps
    with ExitStack() as st:
        xt = st.enter_context(nc.sbuf_tensor("x_rows", [P, NT, D], F32))
        rows_a = st.enter_context(nc.sbuf_tensor("vector_rows_a", [P, P], F32))
        rows_b = st.enter_context(nc.sbuf_tensor("vector_rows_b", [P, P], F32))
        zeros = st.enter_context(nc.sbuf_tensor("zero_rows", [P, D], F32))
        consts_in, rows_in, x_in, small_in, zero_done, zeros_out, turned, taken_a, taken_v, memsets = sems(
            nc, st, "setup", ["consts", "rows", "x", "small", "zero", "zeros_out", "turned", "act", "dve", "memset"])
        NROWS_B = 2 * KD + KD + 3 + 2
        with nc.Block(no_gpsimd_drain=True) as block:
            @block.sync
            def _(sp):
                sp.dma_start(c.base_tile[:, :], ops["base_consts"]).then_inc(consts_in, 16)
                sp.dma_start(xt[:, 0, :], ops["x_prompt"][0]).then_inc(x_in, 16)
                sp.dma_start(xt[:, 1:NT, :], ops["x_sample"][0].rearrange("(t p) d -> p t d", p=P)).then_inc(x_in, 16)
                sp.dma_start(c.router[:, :, :], ops["router_w"].rearrange("(k p) e -> p k e", p=P)).then_inc(small_in, 16)
                sp.dma_start(c.router_b[:, :], ops["router_b"].rearrange("(a e) -> a e", a=1).broadcast_to([P, NE])).then_inc(small_in, 16)
                sp.wait_ge(small_in, 32)
                sp.wait_ge(zeros_out, 16 * NBLK)

            @block.gpsimd
            def _(pool):
                pool.memset(c.eps[:, :], EPS).then_inc(memsets, 1)
                pool.memset(c.zero2[:, :, :], 0.0).then_inc(memsets, 1)
                pool.memset(rows_b[:, :], 0.0).then_inc(memsets, 1)

            @block.scalar
            def _(act):
                act.dma_start(rows_a[0:16, :], ops["norm1_g"].rearrange("l (k p) -> (l k) p", p=P)).then_inc(rows_in, 16)
                act.dma_start(rows_a[16:32, :], ops["norm2_g"].rearrange("l (k p) -> (l k) p", p=P)).then_inc(rows_in, 16)
                act.dma_start(rows_a[32:128, :], ops["ada_b"].rearrange("l (k p) -> (l k) p", p=P)).then_inc(rows_in, 16)
                act.wait_ge(memsets, 3)
                for r, n in ((0, "c_ctx"), (8, "c"), (16, "final_norm_g"), (24, "mla_q_norm_g"), (27, "mla_kv_norm_g")):
                    v = ops[n] if len(ops[n].shape) == 1 else ops[n].rearrange("a n -> (a n)")
                    w = v.shape[0] // P
                    act.dma_start(rows_b[r:r + w, :], v.rearrange("(k p) -> k p", p=P)).then_inc(rows_in, 16)
                act.wait_ge(zero_done, 1)
                for b in range(NBLK):
                    act.dma_start(c.xs[b * P:(b + 1) * P, :], zeros[:, :]).then_inc(zeros_out, 16)
                for g in range(1, 2 * NT, 2):
                    act.wait_ge(turned, g + 3)
                    nc.scalar.copy(c.x[:, 4:8, (g // 2) * P:(g // 2 + 1) * P],
                                   ps[:, 2 + g % 6, :].rearrange("p (k n) -> p k n", k=4)).then_inc(taken_a, 1)
                act.wait_ge(taken_v, 3)
                for j in range(2):
                    nc.scalar.activation(c.cond[:, :, j], c.cols_b[:, 8 * j:8 * j + 8], ACT.Silu).then_inc(taken_a, 1)

            @block.tensor
            def _(pe):
                pe.wait_ge(consts_in, 16)
                pe.wait_ge(rows_in, 16 * 8)
                pe.wait_ge(memsets, 3)
                pe.transpose(ps[:, 0, 0:P], rows_a[:, :], c.base["ident"]).then_inc(turned, 1)
                pe.transpose(ps[:, 1, 0:P], rows_b[:, :], c.base["ident"]).then_inc(turned, 1)
                pe.wait_ge(x_in, 32)
                for g in range(2 * NT):
                    if g >= 6:
                        pe.wait_ge(taken_v, 3 + (g - 6) // 2 + 1)
                        pe.wait_ge(taken_a, (g - 6) // 2 + 1)
                    for k in range(4):
                        mm = pe.transpose(ps[:, 2 + g % 6, k * P:(k + 1) * P],
                                          xt[:, g // 2, (4 * (g % 2) + k) * P:(4 * (g % 2) + k + 1) * P], c.base["ident"])
                    mm.then_inc(turned, 1)

            @block.vector
            def _(dve):
                dve.memset(zeros[:, :], 0.0).then_inc(zero_done, 1)
                dve.wait_ge(turned, 1)
                dve.tensor_copy(c.cols_a[:, :], ps[:, 0, 0:P]).then_inc(taken_v, 1)
                dve.wait_ge(turned, 2)
                dve.tensor_copy(c.cols_b[:, :], ps[:, 1, 0:32]).then_inc(taken_v, 1)
                dve.wait_ge(taken_v, 2)
                dve.tensor_copy(c.fin2[:, :, 0], c.cols_b[:, 16:24]).then_inc(taken_v, 1)
                for g in range(0, 2 * NT, 2):
                    dve.wait_ge(turned, g + 3)
                    dve.tensor_copy(c.x[:, 0:4, (g // 2) * P:(g // 2 + 1) * P],
                                    ps[:, 2 + g % 6, :].rearrange("p (k n) -> p k n", k=4)).then_inc(taken_v, 1)
                dve.tensor_copy(c.fin2[:, :, 1], c.cols_b[:, 16:24]).then_inc(taken_v, 1)


def modulation(c):
    nc, ops, ps = c.nc, c.ops, c.ps
    CH = 6 * D // 512
    w = ops["ada_w"].rearrange("l (k p) (g n) -> l g p k n", p=P, n=512)
    with ExitStack() as st:
        full = sems(nc, st, "ada", [f"full{s}" for s in range(NSLOT)])
        used, biased, amp = sems(nc, st, "ada", ["used", "biased", "amp"])
        with nc.Block(no_gpsimd_drain=True) as block:
            @block.sync
            def _(sp):
                for n in range(DEPTH * CH):
                    if n >= NSLOT:
                        sp.wait_ge(used, n - NSLOT + 1)
                    sp.dma_start(c.slot(n % NSLOT).rearrange("p (k n) -> p k n", k=KD), w[n // CH, n % CH]).then_inc(full[n % NSLOT], 16)

            @block.tensor
            def _(pe):
                for layer in range(DEPTH):
                    for g in range(CH // NSLOT):
                        for s in range(NSLOT):
                            pe.wait_ge(full[s], 16 * (layer * (CH // NSLOT) + g + 1))
                            wt = c.slot(s).rearrange("p (k n) -> p k n", k=KD)
                            for b in range(4):
                                col = 2 * ((g * NSLOT + s) * 4 + b)
                                for k in range(KD):
                                    mm = pe.matmul(ps[:, layer, col:col + 2], wt[:, k, b * P:(b + 1) * P],
                                                   c.cond[:, k, :], start=(k == 0), stop=(k == KD - 1))
                            mm.then_inc(used, 1)

            @block.vector
            def _(dve):
                for layer in range(DEPTH):
                    dve.wait_ge(used, (layer + 1) * CH)
                    bias = c.cols_a[:, 32 + 48 * layer:32 + 48 * layer + 48]
                    for j in range(2):
                        dve.tensor_tensor(c.mod[:, layer, :, j],
                                          ps[:, layer, 0:96].rearrange("p (m j) -> p m j", j=2)[:, :, j],
                                          bias, ALU.add).then_inc(biased, 1)
                    dve.wait_ge(biased, 2 * layer + 2)
                    for n, m in ((0, 1), (1, 4)):
                        gain = c.cols_a[:, 16 * n + 8 * layer:16 * n + 8 * layer + 8]
                        for j in range(2):
                            dve.scalar_tensor_tensor(out=c.amp[:, layer, n, :, j],
                                                     in0=c.mod[:, layer, 8 * m:8 * m + 8, j], scalar=1.0,
                                                     in1=gain, op0=ALU.add, op1=ALU.mult).then_inc(amp, 1)


def norm(c, name, amp, shift):
    nc, ps = c.nc, c.ps
    with ExitStack() as st:
        rstd = st.enter_context(nc.sbuf_tensor(f"{name}_rstd", [P, T], F32))
        squared, summed, rooted, inverted, scaled, shifted = sems(
            nc, st, name, ["squared", "summed", "rooted", "inverted", "scaled", "shifted"])
        with nc.Block(no_gpsimd_drain=True) as block:
            @block.scalar
            def _(act):
                for k in range(KD):
                    nc.scalar.activation(c.h[:, k, :], c.x[:, k, :], ACT.Square).then_inc(squared, 1)
                for r, (a, n, j) in enumerate(RANGES):
                    act.wait_ge(summed, r + 1)
                    nc.scalar.activation(rstd[:, a:a + n], ps[:, r, 0:n], ACT.Sqrt, bias=c.eps[:, :],
                                         scale=1.0 / D).then_inc(rooted, 1)
                i = 0
                for k in range(KD):
                    for a, n, j in RANGES:
                        i += 1
                        act.wait_ge(scaled, i)
                        nc.scalar.activation(c.h[:, k, a:a + n], c.h[:, k, a:a + n], ACT.Identity,
                                             bias=shift[:, k, j:j + 1]).then_inc(shifted, 1)

            @block.tensor
            def _(pe):
                for r, (a, n, j) in enumerate(RANGES):
                    for k in range(KD):
                        pe.wait_ge(squared, k + 1)
                        mm = pe.matmul(ps[:, r, 0:n], c.base["ones"], c.h[:, k, a:a + n],
                                       start=(k == 0), stop=(k == KD - 1))
                    mm.then_inc(summed, 1)

            @block.vector
            def _(dve):
                for r, (a, n, j) in enumerate(RANGES):
                    dve.wait_ge(rooted, r + 1)
                    dve.reciprocal(rstd[:, a:a + n], rstd[:, a:a + n]).then_inc(inverted, 1)
                dve.wait_ge(inverted, 2)
                for k in range(KD):
                    for a, n, j in RANGES:
                        dve.scalar_tensor_tensor(out=c.h[:, k, a:a + n], in0=c.x[:, k, a:a + n],
                                                 scalar=amp[:, k, j:j + 1], in1=rstd[:, a:a + n],
                                                 op0=ALU.mult, op1=ALU.mult).then_inc(scaled, 1)


def mla(c, layer, j):
    nc = c.nc
    with ExitStack() as st:
        def sb(name, shape):
            return st.enter_context(nc.sbuf_tensor("mla_" + name, shape, F32))

        m = {"consts": sb("consts", [P, _width(MLA_COLS)]), "cq": sb("cq", [P, 3, T]),
             "ckv": sb("ckv", [P, 2, KEYS]), "kpe": sb("kpe", [P, KEYS]), "full": None}
        m.update(_views(m["consts"], MLA_COLS))
        mla_project(c, m, j)
        mla_pairs(c, m, layer, j)


def mla_project(c, m, j):
    nc, ops, ps = c.nc, c.ops, c.ps
    W = QL + KVL + ROPE
    w_in = c.ring[:, 3 * SLOT:3 * SLOT + KD * W].rearrange("p (k n) -> p k n", k=KD)
    cq, ckv, kpe = m["cq"], m["ckv"], m["kpe"]
    with ExitStack() as st:
        sq = st.enter_context(nc.sbuf_tensor("mla_squares", [P, 5, T], F32))
        rq = st.enter_context(nc.sbuf_tensor("mla_rstd", [P, 2, T], F32))
        cache = st.enter_context(nc.sbuf_tensor("mla_cache_rows", [P, 3 * P], F32))
        w_kpe2 = st.enter_context(nc.sbuf_tensor("mla_w_kpe_twice", [P, KD, P], F32))
        rows = st.enter_context(nc.sbuf_tensor("mla_new_cache", [P, 3 * P], F32))
        rope = st.enter_context(nc.sbuf_tensor("mla_rope_parts", [P, 2, LAT], F32))
        loaded, const_in, cache_in, done, act_s, dve_s, out_s, dup_s = sems(
            nc, st, "mlap", ["w_in", "consts", "cache_in", "products", "act", "dve", "out", "dup"])
        prod = Steps(done, [f"z{b}" for b in range(6)] + ["cache", "sq", "skv", "swap", "rows"])
        act_n = Steps(act_s, [f"z{b}{r}" for b in range(6) for r in range(2)] + [f"s{b}" for b in range(5)]
                      + ["cacheT"] + [f"root{g}{r}" for g in range(2) for r in range(2)])
        dve_n = Steps(dve_s, ["cachepe"] + [f"inv{g}" for g in range(2)] + [f"n{b}{r}" for b in range(5) for r in range(2)]
                      + ["rc", "rs", "rot", "rows"])
        with nc.Block(no_gpsimd_drain=True) as block:
            @block.sync
            def _(sp):
                sp.dma_start(w_in, ops["mla_w_in"][j].rearrange("(k p) n -> p k n", p=P)).then_inc(loaded, 16)
                sp.dma_start(cache[:, 0:KVL + ROPE], ops["cache_mla"][0, j]).then_inc(cache_in, 16)
                sp.dma_start(cache[:, KVL + ROPE:3 * P], ops["cache_mla"][0, j, :, KVL:KVL + ROPE]).then_inc(cache_in, 16)
                sp.dma_start(m["consts"][:, :], ops["mla_consts"]).then_inc(const_in, 16)
                sp.wait_ge(dve_n.sem, dve_n.value("rows"))
                sp.dma_start(ops["new_cache"][0, j], rows[:, 0:KVL + ROPE]).then_inc(out_s, 16)
                sp.wait_ge(out_s, 16)

            @block.tensor
            def _(pe):
                pe.wait_ge(loaded, 16)
                pe.wait_ge(dup_s, 2)
                for b in range(6):
                    if b >= 3:
                        pe.wait_ge(act_n.sem, act_n.value(f"z{b - 3}1"))
                    for r, (a, n, _) in enumerate(RANGES):
                        for k in range(KD):
                            lhs = w_in[:, k, b * P:(b + 1) * P] if b < 5 else w_kpe2[:, k, :]
                            mm = pe.matmul(ps[:, 2 * (b % 3) + r, 0:n], lhs, c.h[:, k, a:a + n],
                                           start=(k == 0), stop=(k == KD - 1))
                    mm.then_inc(done, 1)
                pe.wait_ge(cache_in, 32)
                for b in range(3):
                    mm = pe.transpose(ps[:, 6 + b // 2, (b % 2) * P:(b % 2 + 1) * P], cache[:, b * P:(b + 1) * P], c.base["ident"])
                mm.then_inc(done, 1)
                pe.wait_ge(act_n.sem, act_n.value("s4"))
                for g, blocks in ((0, (0, 1, 2)), (1, (3, 4))):
                    for r, (a, n, _) in enumerate(RANGES):
                        for b in blocks:
                            mm = pe.matmul(ps[:, 2 * g + r, 0:n], c.base["ones"], sq[:, b, a:a + n],
                                           start=(b == blocks[0]), stop=(b == blocks[-1]))
                    mm.then_inc(done, 1)
                pe.wait_ge(const_in, 16)
                pe.matmul(ps[:, 5, :], m["swap"], kpe[:, SEQ:T], start=True, stop=True).then_inc(done, 1)
                pe.wait_ge(dve_n.sem, dve_n.value("n41"))
                for b in range(2):
                    pe.transpose(ps[:, 7, b * P:(b + 1) * P], ckv[:, b, 0:P], c.base["ident"])
                pe.transpose(ps[:, 7, 2 * P:3 * P], kpe[:, 0:P], c.base["ident"]).then_inc(done, 1)

            @block.scalar
            def _(act):
                for b in range(6):
                    act.wait_ge(prod.sem, prod.value(f"z{b}"))
                    for r, (a, n, _) in enumerate(RANGES):
                        dst = cq[:, b] if b < 3 else ckv[:, b - 3] if b < 5 else kpe
                        nc.scalar.copy(dst[:, a:a + n], ps[:, 2 * (b % 3) + r, 0:n]).then_inc(act_s, 1)
                for b in range(5):
                    src = cq[:, b, :] if b < 3 else ckv[:, b - 3, 0:T]
                    act.wait_ge(act_n.sem, act_n.value("z51"))
                    nc.scalar.activation(sq[:, b, :], src, ACT.Square).then_inc(act_s, 1)
                act.wait_ge(prod.sem, prod.value("cache"))
                nc.scalar.copy(ckv[:, :, T:KEYS], ps[:, 6, 0:2 * P].rearrange("p (b n) -> p b n", b=2)).then_inc(act_s, 1)
                for g, width in ((0, QL), (1, KVL)):
                    act.wait_ge(prod.sem, prod.value("sq" if g == 0 else "skv"))
                    for r, (a, n, _) in enumerate(RANGES):
                        nc.scalar.activation(rq[:, g, a:a + n], ps[:, 2 * g + r, 0:n], ACT.Sqrt,
                                             bias=c.eps[:, :], scale=1.0 / width).then_inc(act_s, 1)

            @block.vector
            def _(dve):
                dve.wait_ge(loaded, 16)
                for i in range(2):
                    dve.tensor_copy(w_kpe2[:, :, i * ROPE:(i + 1) * ROPE], w_in[:, :, QL + KVL:W]).then_inc(dup_s, 1)
                dve.wait_ge(prod.sem, prod.value("cache"))
                dve.tensor_copy(kpe[:, T:KEYS], ps[:, 7, 0:P]).then_inc(dve_s, 1)
                for g in range(2):
                    dve.wait_ge(act_n.sem, act_n.value(f"root{g}1"))
                    dve.reciprocal(rq[:, g, :], rq[:, g, :]).then_inc(dve_s, 1)
                for b in range(5):
                    dve.wait_ge(dve_n.sem, dve_n.value(f"inv{b // 3}"))
                    for a, n, _ in RANGES:
                        t = cq[:, b, a:a + n] if b < 3 else ckv[:, b - 3, a:a + n]
                        dve.scalar_tensor_tensor(out=t, in0=t, scalar=c.cols_b[:, 24 + b:25 + b],
                                                 in1=rq[:, b // 3, a:a + n], op0=ALU.mult, op1=ALU.mult).then_inc(dve_s, 1)
                dve.wait_ge(const_in, 16)
                dve.wait_ge(act_n.sem, act_n.value("z51"))
                dve.tensor_tensor(rope[:, 0, :], kpe[:, SEQ:T], m["rcos"], ALU.mult).then_inc(dve_s, 1)
                dve.wait_ge(prod.sem, prod.value("swap"))
                dve.tensor_tensor(rope[:, 1, :], ps[:, 5, :], m["rsin"], ALU.mult).then_inc(dve_s, 1)
                dve.wait_ge(dve_n.sem, dve_n.value("rs"))
                dve.tensor_tensor(kpe[:, SEQ:T], rope[:, 0, :], rope[:, 1, :], ALU.add).then_inc(dve_s, 1)
                dve.wait_ge(prod.sem, prod.value("rows"))
                dve.tensor_copy(rows[:, :], ps[:, 7, 0:3 * P]).then_inc(dve_s, 1)


def mla_pairs(c, m, layer, j):
    nc, ops, ps = c.nc, c.ops, c.ps
    cq, ckv, kpe = m["cq"], m["ckv"], m["kpe"]
    UNITS = [(hd, t) for hd in range(2) for t in range(NT)]
    NU = len(UNITS)
    order = ["q0", "q1", "qp", "qs", "k0", "k1", "v0", "v1", "v2", "S0", "S1"]
    for u in range(NU):
        order += ([f"S{u + 2}"] if u + 2 < NU else []) + [f"T{u}"] + (["O0"] if u == NT else [])
    order += ["O1"] + [f"w{d}" for d in range(KD)]
    bank = {n: 2 * (i % 4) for i, n in enumerate(order)}
    wq = c.slot(0, 3 * 2 * UQ).rearrange("p (k n) -> p k n", k=3)
    wkv = c.slot(1, 2 * 512).rearrange("p (k h n) -> p k h n", k=2, h=2)
    wo = c.slot(2, 2 * D).rearrange("p (h n) -> p h n", h=2)
    act_names = ["q00", "q01", "q10", "q11", "qp0", "qp1", "k0", "k1", "v0", "v1", "v2"]
    for u, (hd, t) in enumerate(UNITS):
        act_names += [f"e{u}"] + ([f"T{u - 1}"] if u else [])
    act_names += [f"T{NU - 1}"]
    dve_names = ["rc", "rs", "rot"]
    for u, (hd, t) in enumerate(UNITS):
        dve_names += [f"m{u}", f"b{u}"] + ([f"i{u - 1}", f"p{u - 1}"] if u else [])
        dve_names += [f"t{u - 1}"] if u and UNITS[u - 1][1] else []
        dve_names += ["o00", "o01"] if u == NT + 1 else []
    dve_names += [f"i{NU - 1}", f"p{NU - 1}", f"t{NU - 1}", "o10", "o11"] + [f"x{d}{r}" for d in range(KD) for r in range(2)]
    last = {"q0": ("a", "q01"), "q1": ("a", "q11"), "qp": ("a", "qp1"), "qs": ("v", "rs"), "k0": ("a", "k0"), "k1": ("a", "k1"),
            "v0": ("a", "v0"), "v1": ("a", "v1"), "v2": ("a", "v2"), "O0": ("v", "o01"), "O1": ("v", "o11")}
    last |= {f"S{u}": ("a", f"e{u}") for u in range(NU)}
    last |= {f"w{d}": ("v", f"x{d}1") for d in range(KD)}
    with ExitStack() as st:
        def sb(name, shape):
            return st.enter_context(nc.sbuf_tensor("mla_" + name, shape, F32))

        q, qpe, qraw = sb("q", [P, 2, T]), sb("qpe", [P, T]), sb("qraw", [P, LAT])
        rope = sb("qrope", [P, 2, LAT])
        k, v = sb("k", [P, 2, KEYS]), sb("v", [P, NKT, 2 * VD])
        prob = sb("prob", [P, 3, LKEYS])
        pt = c.h[:, :, :].rearrange("p k n -> p (k n)").rearrange("p (h x n) -> p h x n", h=2, x=5)
        ptc = sb("prob_t_ctx", [P, 2, P])
        o = sb("o", [P, 2, T])
        mx, bias, den, inv = (sb(n, [P, NU]) for n in ("max", "bias", "den", "inv"))
        fq, fkv, fo, done, act_s, dve_s = sems(nc, st, "mla", ["wq_full", "wkv_full", "wo_full", "products", "act", "dve"])
        prod = Steps(done, order)
        act_n, dve_n = Steps(act_s, act_names, 1), Steps(dve_s, dve_names, 1)
        by = {"a": act_n, "v": dve_n}
        gate = c.mod[:, layer, 16:24, :]
        with nc.Block(no_gpsimd_drain=True) as block:
            @block.sync
            def _(sp):
                def load_q(i):
                    src = ops["mla_w_uq"][j].rearrange("(k p) (g h n) -> g p k h n", p=P, h=2, n=UQ)
                    for first, width, at in ((0, NOPE, 0), (NOPE, ROPE, 2 * NOPE)):
                        for hd in range(2):
                            sp.dma_start(wq[:, :, at + hd * width:at + (hd + 1) * width],
                                         src[bass.ds(i, 1), :, :, hd, first:first + width].rearrange("a p k n -> (a p) k n"))\
                              .then_inc(fq, 16)

                def load_kv(i):
                    sp.dma_start(c.slot(1, 2 * 512).rearrange("p (k n) -> p k n", k=2),
                                 ops["mla_w_ukv"][j].rearrange("(k p) (g n) -> g p k n", p=P, n=512)[bass.ds(i, 1)]
                                 .rearrange("a p k n -> (a p) k n")).then_inc(fkv, 16)

                def load_o(i):
                    sp.dma_start(wo, ops["mla_w_o"][j].rearrange("(g h p) n -> g p h n", p=P, h=2)[bass.ds(i, 1)]
                                 .rearrange("a p h n -> (a p) h n")).then_inc(fo, 16)

                load_q(0)
                load_kv(0)
                load_o(0)
                with sp.Fori(0, PAIRS - 1) as i:
                    sp.wait_ge(prod.sem, prod.value("qp", i))
                    load_q(i + 1)
                    sp.wait_ge(prod.sem, prod.value("v2", i))
                    load_kv(i + 1)
                    sp.wait_ge(prod.sem, prod.value(f"w{KD - 1}", i))
                    load_o(i + 1)

            @block.tensor
            def _(pe):
                def two_ranges(name, mms, i):
                    for r, (a, n, _) in enumerate(RANGES):
                        for x, (lhs, rhs) in enumerate(mms):
                            mm = pe.matmul(ps[:, bank[name] + r, 0:n], lhs, rhs[:, a:a + n],
                                           start=(x == 0), stop=(x == len(mms) - 1))
                    mm.then_inc(done, 1)

                def free(name, i):
                    g = order.index(name) - 4
                    if g >= 0:
                        old = order[g]
                        if old[0] == "T":
                            u = int(old[1:])
                            pe.wait_ge(act_n.sem, act_n.value(f"T{u}", i))
                            if UNITS[u][1]:
                                pe.wait_ge(dve_n.sem, dve_n.value(f"t{u}", i))
                        else:
                            e, s = last[old]
                            pe.wait_ge(by[e].sem, by[e].value(s, i))

                def scores(u, i):
                    hd, t = UNITS[u]
                    free(f"S{u}", i)
                    b = bank[f"S{u}"]
                    half = slice(hd * ROPE, (hd + 1) * ROPE)
                    cols = slice(t * P, (t + 1) * P)
                    spans = [(0, SEQ)] if t == 0 else [(SEQ, LKEYS // 2), (SEQ + LKEYS // 2, LKEYS // 2)]
                    for r, (a, n) in enumerate(spans):
                        pe.matmul(ps[:, b + r, 0:n], q[:, hd, cols], k[:, hd, a:a + n], start=True, stop=False)
                        mm = pe.matmul(ps[:, b + r, 0:n], qpe[half, cols], kpe[half, a:a + n], start=False, stop=True)
                    mm.then_inc(done, 1)

                def turn(u, i):
                    hd, t = UNITS[u]
                    free(f"T{u}", i)
                    b = bank[f"T{u}"]
                    pe.wait_ge(dve_n.sem, dve_n.value(f"p{u}", i))
                    for x in range(1 if t == 0 else 5):
                        mm = pe.transpose(ps[:, b + x // 4, (x % 4) * P:(x % 4 + 1) * P],
                                          prob[:, u % 3, x * P:(x + 1) * P], c.base["ident"])
                    mm.then_inc(done, 1)

                def attend(hd, i):
                    free(f"O{hd}", i)
                    b, u = bank[f"O{hd}"], hd * NT + NT - 1
                    pe.wait_ge(act_n.sem, act_n.value(f"T{u}", i))
                    pe.wait_ge(dve_n.sem, dve_n.value(f"t{u}", i))
                    vh = slice(hd * VD, (hd + 1) * VD)
                    pe.matmul(ps[:, b, 0:P], v[:, 0, vh], ptc[:, hd, :], start=True, stop=True)
                    for x in range(5):
                        mm = pe.matmul(ps[:, b + 1, :], v[:, 1 + x, vh], pt[:, hd, x, :], start=(x == 0), stop=(x == 4))
                    mm.then_inc(done, 1)

                with pe.Fori(0, PAIRS) as i:
                    pe.wait_ge(fq, (i + 1) * 64)
                    pe.wait_ge(act_n.sem, act_n.before(i))
                    pe.wait_ge(dve_n.sem, dve_n.before(i))
                    for hd in range(2):
                        two_ranges(f"q{hd}", [(wq[:, b, hd * NOPE:(hd + 1) * NOPE], cq[:, b, :]) for b in range(3)], i)
                    two_ranges("qp", [(wq[:, b, 2 * NOPE:2 * UQ], cq[:, b, :]) for b in range(3)], i)
                    pe.wait_ge(act_n.sem, act_n.value("qp1", i))
                    pe.matmul(ps[:, bank["qs"], :], m["swap"], qraw[:, :], start=True, stop=True).then_inc(done, 1)
                    pe.wait_ge(fkv, (i + 1) * 16)
                    for hd in range(2):
                        free(f"k{hd}", i)
                        for r in range(2):
                            for b in range(2):
                                mm = pe.matmul(ps[:, bank[f"k{hd}"] + r, 0:KEYS // 2], wkv[:, b, hd, 0:NOPE],
                                               ckv[:, b, r * KEYS // 2:(r + 1) * KEYS // 2], start=(b == 0), stop=(b == 1))
                        mm.then_inc(done, 1)
                    for g in range(3):
                        free(f"v{g}", i)
                        for r in range(2):
                            t = 2 * g + r
                            for b in range(2):
                                mm = pe.matmul(ps[:, bank[f"v{g}"] + r, 0:2 * VD], ckv[:, b, t * P:(t + 1) * P],
                                               wkv[:, b, :, NOPE:2 * NOPE], start=(b == 0), stop=(b == 1))
                        mm.then_inc(done, 1)
                    pe.wait_ge(act_n.sem, act_n.value("k1", i))
                    pe.wait_ge(dve_n.sem, dve_n.value("rot", i))
                    scores(0, i)
                    scores(1, i)
                    for u in range(NU):
                        if u + 2 < NU:
                            scores(u + 2, i)
                        turn(u, i)
                        if u == NT:
                            attend(0, i)
                    attend(1, i)
                    pe.wait_ge(fo, (i + 1) * 16)
                    pe.wait_ge(dve_n.sem, dve_n.value("o11", i))
                    for d in range(KD):
                        free(f"w{d}", i)
                        two_ranges(f"w{d}", [(wo[:, hd, d * P:(d + 1) * P], o[:, hd, :]) for hd in range(2)], i)

            @block.scalar
            def _(act):
                def take_turned(u, i):
                    hd, t = UNITS[u]
                    act.wait_ge(prod.sem, prod.value(f"T{u}", i))
                    b = bank[f"T{u}"]
                    if t == 0:
                        nc.scalar.copy(ptc[:, hd, :], ps[:, b, 0:P]).then_inc(act_s, 1)
                    else:
                        nc.scalar.copy(pt[:, hd, 0:4, (t - 1) * P:t * P],
                                       ps[:, b, :].rearrange("p (x n) -> p x n", x=4)).then_inc(act_s, 1)

                act.sem_inc(act_s, 1)
                with act.Fori(0, PAIRS) as i:
                    for hd in range(2):
                        act.wait_ge(prod.sem, prod.value(f"q{hd}", i))
                        for r, (a, n, _) in enumerate(RANGES):
                            nc.scalar.copy(q[:, hd, a:a + n], ps[:, bank[f"q{hd}"] + r, 0:n]).then_inc(act_s, 1)
                    act.wait_ge(prod.sem, prod.value("qp", i))
                    nc.scalar.copy(qpe[:, 0:SEQ], ps[:, bank["qp"], 0:SEQ]).then_inc(act_s, 1)
                    nc.scalar.copy(qraw[:, :], ps[:, bank["qp"] + 1, :]).then_inc(act_s, 1)
                    for hd in range(2):
                        act.wait_ge(prod.sem, prod.value(f"k{hd}", i))
                        nc.scalar.copy(k[:, hd, :].rearrange("p (r n) -> p r n", r=2),
                                       ps[:, bank[f"k{hd}"]:bank[f"k{hd}"] + 2, 0:KEYS // 2]).then_inc(act_s, 1)
                    for g in range(3):
                        act.wait_ge(prod.sem, prod.value(f"v{g}", i))
                        nc.scalar.copy(v[:, 2 * g:2 * g + 2, :],
                                       ps[:, bank[f"v{g}"]:bank[f"v{g}"] + 2, 0:2 * VD]).then_inc(act_s, 1)
                    for u, (hd, t) in enumerate(UNITS):
                        b = bank[f"S{u}"]
                        act.wait_ge(dve_n.sem, dve_n.value(f"b{u}", i))
                        if u >= 3:
                            act.wait_ge(prod.sem, prod.value(f"T{u - 3}", i))
                        src = ps[:, b, 0:SEQ] if t == 0 else ps[:, b:b + 2, 0:LKEYS // 2]
                        dst = prob[:, u % 3, 0:SEQ] if t == 0 else prob[:, u % 3, :].rearrange("p (r n) -> p r n", r=2)
                        nc.scalar.activation(dst, src, ACT.Exp, bias=bias[:, u:u + 1], scale=MLA_SCALE,
                                             accum_out=den[:, u:u + 1]).then_inc(act_s, 1)
                        if u:
                            take_turned(u - 1, i)
                    take_turned(NU - 1, i)

            @block.vector
            def _(dve):
                def normalise(u, i):
                    hd, t = UNITS[u]
                    n = SEQ if t == 0 else LKEYS
                    dve.wait_ge(act_n.sem, act_n.value(f"e{u}", i))
                    dve.reciprocal(inv[:, u:u + 1], den[:, u:u + 1]).then_inc(dve_s, 1)
                    dve.wait_ge(dve_n.sem, dve_n.value(f"i{u}", i))
                    dve.tensor_scalar(prob[:, u % 3, 0:n], prob[:, u % 3, 0:n], inv[:, u:u + 1], None,
                                      ALU.mult).then_inc(dve_s, 1)

                def take_last(u, i):
                    hd, t = UNITS[u]
                    dve.wait_ge(prod.sem, prod.value(f"T{u}", i))
                    dve.tensor_copy(pt[:, hd, 4, (t - 1) * P:t * P], ps[:, bank[f"T{u}"] + 1, 0:P]).then_inc(dve_s, 1)

                def take_o(hd, i):
                    dve.wait_ge(prod.sem, prod.value(f"O{hd}", i))
                    for r, (a, n, _) in enumerate(RANGES):
                        dve.tensor_copy(o[:, hd, a:a + n], ps[:, bank[f"O{hd}"] + r, 0:n]).then_inc(dve_s, 1)

                dve.sem_inc(dve_s, 1)
                with dve.Fori(0, PAIRS) as i:
                    dve.wait_ge(act_n.sem, act_n.value("qp1", i))
                    dve.tensor_tensor(rope[:, 0, :], qraw[:, :], m["rcos"], ALU.mult).then_inc(dve_s, 1)
                    dve.wait_ge(prod.sem, prod.value("qs", i))
                    dve.tensor_tensor(rope[:, 1, :], ps[:, bank["qs"], :], m["rsin"], ALU.mult).then_inc(dve_s, 1)
                    dve.wait_ge(dve_n.sem, dve_n.value("rs", i))
                    dve.tensor_tensor(qpe[:, SEQ:T], rope[:, 0, :], rope[:, 1, :], ALU.add).then_inc(dve_s, 1)
                    for u, (hd, t) in enumerate(UNITS):
                        b = bank[f"S{u}"]
                        dve.wait_ge(prod.sem, prod.value(f"S{u}", i))
                        if t == 0:
                            dve.tensor_reduce(mx[:, u:u + 1], ps[:, b, 0:SEQ], AX.X, ALU.max).then_inc(dve_s, 1)
                        else:
                            dve.tensor_reduce(mx[:, u:u + 1], ps[:, b:b + 2, 0:LKEYS // 2], AX.XY, ALU.max).then_inc(dve_s, 1)
                        dve.wait_ge(dve_n.sem, dve_n.value(f"m{u}", i))
                        dve.tensor_scalar(bias[:, u:u + 1], mx[:, u:u + 1], -MLA_SCALE, None, ALU.mult).then_inc(dve_s, 1)
                        if u:
                            normalise(u - 1, i)
                            if UNITS[u - 1][1]:
                                take_last(u - 1, i)
                        if u == NT + 1:
                            take_o(0, i)
                    normalise(NU - 1, i)
                    take_last(NU - 1, i)
                    take_o(1, i)
                    for d in range(KD):
                        dve.wait_ge(prod.sem, prod.value(f"w{d}", i))
                        for r, (a, n, jc) in enumerate(RANGES):
                            dve.scalar_tensor_tensor(out=c.x[:, d, a:a + n], in0=ps[:, bank[f"w{d}"] + r, 0:n],
                                                     scalar=gate[:, d, jc:jc + 1], in1=c.x[:, d, a:a + n],
                                                     op0=ALU.mult, op1=ALU.add).then_inc(dve_s, 1)


def retention(c, layer, j):
    nc, ops, ps = c.nc, c.ops, c.ps
    order = ["q0", "q1", "k0", "k1", "v0", "v1", "v2", "kc", "fs", "bs"]
    order += ["f0", "f1", "f2", "b0", "b1", "b2", "sc", "s0", "s1", "s2", "s3"]
    order += [f"o{t}" for t in range(NT)] + [f"y{t}" for t in range(NT)] + [f"w{d}" for d in range(KD)]
    bank = {n: 2 * (i % 4) for i, n in enumerate(order)}
    last = {"q0": ("a", "q01"), "q1": ("a", "q11"), "k0": ("a", "k01"), "k1": ("a", "k11"),
            "kc": ("v", "kb"), "fs": ("v", "fs"), "bs": ("v", "bs"),
            "f0": ("a", "f0"), "f1": ("a", "f1"), "f2": ("a", "f2"), "b0": ("a", "b0"), "b1": ("a", "b1"), "b2": ("a", "b2"),
            "v0": ("v", "v0"), "v1": ("v", "v1"), "v2": ("v", "v2"), "sc": ("v", "scb")}
    last |= {f"s{x}": ("v", f"s{x}b") for x in range(4)}
    last |= {f"o{t}": ("v", f"o{t}b") for t in range(NT)}
    last |= {f"y{t}": ("a", f"y{t}") for t in range(NT)}
    last |= {f"w{d}": ("v", f"x{d}1") for d in range(KD)}
    act_names = ["df", "db", "kdf", "kdb", "ef", "q00", "q01", "q10", "q11", "k00", "k01", "k10", "k11",
                 "f0", "f1", "f2", "b0", "b1", "b2", "eb"]
    act_names += [f"o{t}{r}" for t in range(NT) for r in "fb"] + [f"y{t}" for t in range(NT)]
    dve_names = ["lg", "tf", "tb", "v0", "v1", "v2", "kf", "kb", "fs", "bs"]
    dve_names += [f"q{x}" for x in range(6)] + ["idxb", "qf0", "qf1", "scf", "scb"]
    dve_names += [f"s{x}{r}" for x in range(4) for r in "fb"] + ["qb0", "qb1"]
    for t in range(NT + 1):
        if t < NT:
            dve_names += [f"m{t}"]
        if t:
            dve_names += [f"o{t - 1}f", f"o{t - 1}b", f"y{t - 1}"]
    dve_names += [f"x{d}{r}" for d in range(KD) for r in range(2)]
    pool_names = [f"k{x}" for x in range(6)] + [f"r{t}" for t in range(NT)]
    with ExitStack() as st:
        def sb(name, shape):
            return st.enter_context(nc.sbuf_tensor("ret_" + name, shape, F32))

        consts = sb("consts", [P, _width(RET_COLS)])
        m = _views(consts, RET_COLS)
        s0 = c.ring[:, 5 * SLOT:5 * SLOT + 2048].rearrange("p (f b n) -> p f b n", f=2, b=2)
        trig = c.ring[:, 5 * SLOT + 2048:5 * SLOT + 2048 + 3 * LAT]
        m.update(_views(trig, TRIG_COLS))
        expo = c.ring[:, 5 * SLOT + 2048 + 3 * LAT:6 * SLOT]
        q, k = sb("q", [P, 2, T]), sb("k", [P, 2, T])
        v, gf, gb = (sb(n, [P, NT, DV]) for n in ("v", "gate_f", "gate_b"))
        yt = v[:, :, :].rearrange("p t n -> p (t n)").rearrange("p (b n) -> p b n", b=4)
        dec = sb("decay", [P, 2, LAT])
        kc = sb("k_ctx_rows", [P, 2, DK])
        ss = sb("scores", [P, 4, T])
        sctx = kc[:, :, 0:P]
        stage = sb("new_state", [P, 2, DV])
        qd = stage
        idxb = sb("index_b", [P, LAT])
        junk = idxb
        kd, lgs, lg = sb("k_decay", [P, 2]), sb("log_decays", [P, RH, 2]), sb("log_decay", [P, 2])
        raw, lt1, lt2 = (sb(n, [P, 2, RH]) for n in ("logits", "log_tmp1", "log_tmp2"))
        sumsq, mean, rs, half = sb("sumsq", [P, NT, 2]), sb("meansq", [P, NT, 2]), sb("rstd", [P, NT, 2]), sb("minus_half", [P, 2])
        tmp = ss[:, :, :].rearrange("p t n -> p (t n)")[:, 0:4 * LAT].rearrange("p (x n) -> p x n", x=4)
        full = sems(nc, st, "ret", [f"full{s}" for s in range(6)])
        const_in, logit_in, prep, dprep, done, act_s, dve_s, pool_s, store_s = sems(
            nc, st, "ret", ["consts", "logits", "prep", "dve_prep", "products", "act", "dve", "pool", "stored"])
        prod, act_n, dve_n, pool_n = Steps(done, order), Steps(act_s, act_names, 1), Steps(dve_s, dve_names, 1), Steps(pool_s, pool_names)
        by = {"a": act_n, "v": dve_n}
        gate = c.mod[:, layer, 16:24, :]
        W0 = {"q": 0, "k": RH * DK, "v": 2 * RH * DK, "f": 2 * RH * DK + RH * DV, "b": 2 * RH * DK + 2 * RH * DV}
        w3 = ops["ret_w_in"][j].rearrange("(k p) n -> p k n", p=P)
        wqk, wv, wf, wb = (c.slot(s).rearrange("p (k n) -> p k n", k=KD) for s in range(4))
        wo = c.slot(4).rearrange("p (b n) -> p b n", b=4)
        with nc.Block(no_gpsimd_drain=True) as block:
            @block.sync
            def _(sp):
                sp.dma_start(raw[:, 0, :], ops["ret_decay_f"].broadcast_to([P, RH])).then_inc(logit_in, 16)
                sp.dma_start(raw[:, 1, :], ops["ret_decay_b"].broadcast_to([P, RH])).then_inc(logit_in, 16)
                sp.dma_start(consts[:, :], ops["ret_consts"]).then_inc(const_in, 16)
                sp.dma_start(trig, ops["trig_consts"]).then_inc(const_in, 16)

                def columns(first, width, i):
                    return w3[:, :, bass.ds(i * width + first, width)]

                def load_in(s, i):
                    if s == 0:
                        sp.dma_start(wqk[:, :, 0:DK], columns(W0["q"], DK, i)).then_inc(full[0], 16)
                        sp.dma_start(wqk[:, :, DK:2 * DK], columns(W0["k"], DK, i)).then_inc(full[0], 16)
                    else:
                        sp.dma_start((wqk, wv, wf, wb)[s], columns(W0["qvfb"[s]], DV, i)).then_inc(full[s], 16)

                def load_state(i):
                    src = ops["state_ret"][0, j].rearrange("f h (b p) n -> h f b p n", p=P)
                    for f in range(2):
                        for b in range(2):
                            sp.dma_start(s0[:, f, b, :], src[bass.ds(i, 1), f, b].rearrange("a p n -> (a p) n")).then_inc(full[5], 16)

                def load_out(i):
                    sp.dma_start(wo, ops["ret_w_o"][j].rearrange("(h b p) n -> h p b n", p=P, b=4)[bass.ds(i, 1)]
                                 .rearrange("a p b n -> (a p) b n")).then_inc(full[4], 16)

                def store_state(f, i):
                    sp.wait_ge(dve_n.sem, dve_n.value(("fs", "bs")[f], i))
                    dst = ops["new_state"][0, j, f].rearrange("h (b p) n -> h p b n", p=P)
                    sp.dma_start(dst[bass.ds(i, 1)].rearrange("a p b n -> (a p) b n"), stage[:, :, :]).then_inc(store_s, 16)

                sp.sem_inc(store_s, 16)
                for s in range(4):
                    load_in(s, 0)
                load_state(0)
                load_out(0)
                with sp.Fori(0, RH - 1) as i:
                    for s, n in enumerate(("k1", "v2")):
                        sp.wait_ge(prod.sem, prod.value(n, i))
                        load_in(s, i + 1)
                    store_state(0, i)
                    store_state(1, i)
                    for s, n in enumerate(("f2", "b2")):
                        sp.wait_ge(prod.sem, prod.value(n, i))
                        load_in(s + 2, i + 1)
                    sp.wait_ge(prod.sem, prod.value(f"o{NT - 1}", i))
                    load_state(i + 1)
                    sp.wait_ge(prod.sem, prod.value(f"w{KD - 1}", i))
                    load_out(i + 1)
                store_state(0, RH - 1)
                store_state(1, RH - 1)
                sp.wait_ge(store_s, RH * 32 + 16)

            @block.gpsimd
            def _(pool):
                pool.memset(half[:, :], -0.5).then_inc(prep, 1)
                with pool.Fori(0, RH) as i:
                    pool.wait_ge(const_in, 32)
                    pool.wait_ge(act_n.sem, act_n.value("k11", i))
                    k1, k2 = k[:, 0, SEQ:T], k[:, 1, SEQ:T]
                    pool.tensor_tensor(tmp[:, 0, :], k1, m["sin"], ALU.mult).then_inc(pool_s, 1)
                    pool.tensor_tensor(tmp[:, 1, :], k2, m["sin"], ALU.mult).then_inc(pool_s, 1)
                    pool.wait_ge(pool_n.sem, pool_n.value("k1", i))
                    pool.tensor_tensor(k1, k1, m["cos"], ALU.mult).then_inc(pool_s, 1)
                    pool.tensor_tensor(k2, k2, m["cos"], ALU.mult).then_inc(pool_s, 1)
                    pool.wait_ge(pool_n.sem, pool_n.value("k3", i))
                    pool.tensor_tensor(k1, k1, tmp[:, 1, :], ALU.subtract).then_inc(pool_s, 1)
                    pool.tensor_tensor(k2, k2, tmp[:, 0, :], ALU.add).then_inc(pool_s, 1)
                    for t in range(NT):
                        pool.wait_ge(prep, 1)
                        pool.wait_ge(dve_n.sem, dve_n.value(f"m{t}", i))
                        pool.tensor_tensor(rs[:, t, :], mean[:, t, :], half[:, :], ALU.pow).then_inc(pool_s, 1)

            @block.tensor
            def _(pe):
                def free(name, i):
                    g = order.index(name) - 4
                    if g >= 0:
                        e, s = last[order[g]]
                        pe.wait_ge(by[e].sem, by[e].value(s, i))

                def two_ranges(name, mms, i):
                    free(name, i)
                    for r, (a, n, _) in enumerate(RANGES):
                        for x, (lhs, rhs) in enumerate(mms):
                            mm = pe.matmul(ps[:, bank[name] + r, 0:n], lhs, rhs[:, a:a + n],
                                           start=(x == 0), stop=(x == len(mms) - 1))
                    mm.then_inc(done, 1)

                def rows_of(name, w, i):
                    for g in range(3):
                        free(f"{name}{g}", i)
                        for r in range(2):
                            t = 2 * g + r
                            if t < NT:
                                for b in range(KD):
                                    mm = pe.matmul(ps[:, bank[f"{name}{g}"] + r, :], c.h[:, b, t * P:(t + 1) * P],
                                                   w[:, b, :], start=(b == 0), stop=(b == KD - 1))
                        mm.then_inc(done, 1)

                with pe.Fori(0, RH) as i:
                    pe.wait_ge(full[0], (i + 1) * 32)
                    pe.wait_ge(act_n.sem, act_n.before(i))
                    pe.wait_ge(dve_n.sem, dve_n.before(i))
                    for x, n in enumerate(("q0", "q1", "k0", "k1")):
                        two_ranges(n, [(wqk[:, b, x * P:(x + 1) * P], c.h[:, b, :]) for b in range(KD)], i)
                    pe.wait_ge(full[1], (i + 1) * 16)
                    rows_of("v", wv, i)
                    free("kc", i)
                    pe.wait_ge(act_n.sem, act_n.value("k11", i))
                    for b in range(2):
                        mm = pe.transpose(ps[:, bank["kc"], b * P:(b + 1) * P], k[:, b, 0:P], c.base["ident"])
                    mm.then_inc(done, 1)
                    pe.wait_ge(dve_n.sem, dve_n.value("kb", i))
                    for f, n in enumerate(("fs", "bs")):
                        free(n, i)
                        for b in range(2):
                            mm = pe.matmul(ps[:, bank[n] + b, :], kc[:, f, b * P:(b + 1) * P], v[:, 0, :], start=True, stop=True)
                        mm.then_inc(done, 1)
                    pe.wait_ge(full[2], (i + 1) * 16)
                    rows_of("f", wf, i)
                    pe.wait_ge(full[3], (i + 1) * 16)
                    rows_of("b", wb, i)
                    free("sc", i)
                    for b in range(2):
                        mm = pe.matmul(ps[:, bank["sc"], 0:P], k[:, b, 0:P], q[:, b, 0:P], start=(b == 0), stop=(b == 1))
                    mm.then_inc(done, 1)
                    pe.wait_ge(pool_n.sem, pool_n.value("k5", i))
                    pe.wait_ge(dve_n.sem, dve_n.value("q5", i))
                    for x in range(4):
                        free(f"s{x}", i)
                        for b in range(2):
                            mm = pe.matmul(ps[:, bank[f"s{x}"], :], k[:, b, SEQ + x * P:SEQ + (x + 1) * P], q[:, b, SEQ:T],
                                           start=(b == 0), stop=(b == 1))
                        mm.then_inc(done, 1)
                    pe.wait_ge(full[5], (i + 1) * 64)
                    pe.wait_ge(dve_n.sem, dve_n.value("qb1", i))
                    for t in range(NT):
                        free(f"o{t}", i)
                        for f in range(2):
                            out = ps[:, bank[f"o{t}"] + f, :]
                            if t == 0:
                                mm = pe.matmul(out, sctx[:, f, :], v[:, 0, :], start=True, stop=True)
                                continue
                            n = t - 1
                            mms = [(ss[:, x, (n + 1 - f) * P:(n + 2 - f) * P], v[:, 1 + x, :])
                                   for x in (range(n + 1) if f == 0 else range(n, 4))]
                            qq = qd if f == 0 else q[:, :, SEQ:T]
                            mms += [(qq[:, b, n * P:(n + 1) * P], s0[:, f, b, :]) for b in range(2)]
                            for x, (lhs, rhs) in enumerate(mms):
                                mm = pe.matmul(out, lhs, rhs, start=(x == 0), stop=(x == len(mms) - 1))
                        mm.then_inc(done, 1)
                    for t in range(NT):
                        free(f"y{t}", i)
                        pe.wait_ge(dve_n.sem, dve_n.value(f"y{t}", i))
                        for b in range(4):
                            mm = pe.transpose(ps[:, bank[f"y{t}"], b * P:(b + 1) * P], gf[:, t, b * P:(b + 1) * P], c.base["ident"])
                        mm.then_inc(done, 1)
                    pe.wait_ge(full[4], (i + 1) * 16)
                    pe.wait_ge(act_n.sem, act_n.value(f"y{NT - 1}", i))
                    for d in range(KD):
                        two_ranges(f"w{d}", [(wo[:, b, d * P:(d + 1) * P], yt[:, b, :]) for b in range(4)], i)

            @block.scalar
            def _(act):
                act.wait_ge(prep, 2)
                nc.scalar.activation(lt1[:, :, :], lt1[:, :, :], ACT.Exp, scale=-1.0).then_inc(prep, 1)
                act.wait_ge(prep, 3)
                nc.scalar.activation(lt1[:, :, :], lt1[:, :, :], ACT.Ln, bias=1.0).then_inc(prep, 1)
                act.wait_ge(const_in, 32)
                act.sem_inc(act_s, 1)
                with act.Fori(0, RH) as i:
                    act.wait_ge(dve_n.sem, dve_n.value("lg", i))
                    nc.scalar.activation(dec[:, 0, :], m["relf"], ACT.Exp, scale=lg[:, 0:1]).then_inc(act_s, 1)
                    nc.scalar.activation(dec[:, 1, :], m["relb"], ACT.Exp, scale=lg[:, 1:2]).then_inc(act_s, 1)
                    nc.scalar.activation(kd[:, 0:1], m["kf"], ACT.Exp, scale=lg[:, 0:1]).then_inc(act_s, 1)
                    nc.scalar.activation(kd[:, 1:2], m["kb"], ACT.Exp, scale=lg[:, 1:2]).then_inc(act_s, 1)
                    nc.scalar.activation(expo, m["idxf"], ACT.Exp, scale=lg[:, 0:1]).then_inc(act_s, 1)
                    for x, n in enumerate(("q0", "q1", "k0", "k1")):
                        act.wait_ge(prod.sem, prod.value(n, i))
                        for r, (a, w, _) in enumerate(RANGES):
                            nc.scalar.activation((q, k)[x // 2][:, x % 2, a:a + w], ps[:, bank[n] + r, 0:w], ACT.Identity,
                                                 scale=1.0 if x < 2 else KSCALE).then_inc(act_s, 1)
                    for f, g in (("f", gf), ("b", gb)):
                        for x in range(3):
                            act.wait_ge(prod.sem, prod.value(f"{f}{x}", i))
                            w = 2 if x < 2 else 1
                            nc.scalar.activation(g[:, 2 * x:2 * x + w, :], ps[:, bank[f"{f}{x}"]:bank[f"{f}{x}"] + w, :],
                                                 ACT.Silu).then_inc(act_s, 1)
                    act.wait_ge(dve_n.sem, dve_n.value("qf1", i))
                    nc.scalar.activation(expo, idxb[:, :], ACT.Exp, scale=lg[:, 1:2]).then_inc(act_s, 1)
                    for t in range(NT):
                        act.wait_ge(prod.sem, prod.value(f"o{t}", i))
                        for f in range(2):
                            act.wait_ge(act_n.sem, act_n.value(f"o{t}f", i) - 1 + f)
                            nc.scalar.activation(junk[:, :], ps[:, bank[f"o{t}"] + f, :], ACT.Square,
                                                 accum_out=sumsq[:, t, f:f + 1]).then_inc(act_s, 1)
                    for t in range(NT):
                        act.wait_ge(prod.sem, prod.value(f"y{t}", i))
                        nc.scalar.copy(yt[:, :, t * P:(t + 1) * P],
                                       ps[:, bank[f"y{t}"], :].rearrange("p (b n) -> p b n", b=4)).then_inc(act_s, 1)

            @block.vector
            def _(dve):
                dve.wait_ge(logit_in, 32)
                dve.wait_ge(prep, 1)
                dve.tensor_scalar(lt2[:, :, :], raw[:, :, :], -1.0, None, ALU.mult).then_inc(dprep, 1)
                dve.wait_ge(dprep, 1)
                dve.tensor_tensor(lt1[:, :, :], raw[:, :, :], lt2[:, :, :], ALU.max).then_inc(prep, 1)
                dve.wait_ge(prep, 2)
                dve.tensor_scalar(lt2[:, :, :], raw[:, :, :], 0.0, None, ALU.min).then_inc(dprep, 1)
                dve.wait_ge(dprep, 2)
                dve.wait_ge(prep, 4)
                dve.tensor_tensor(lgs[:, :, :].rearrange("p h f -> p f h"), lt2[:, :, :], lt1[:, :, :], ALU.subtract).then_inc(dprep, 1)
                dve.wait_ge(dprep, 3)
                dve.wait_ge(const_in, 32)
                dve.sem_inc(dve_s, 1)
                with dve.Fori(0, RH) as i:
                    dve.wait_ge(act_n.sem, act_n.before(i))
                    dve.tensor_copy(lg[:, :], lgs[:, bass.ds(i, 1), :].rearrange("p a f -> p (a f)")).then_inc(dve_s, 1)
                    dve.wait_ge(act_n.sem, act_n.value("db", i))
                    dve.tensor_tensor(dec[:, 0, 0:P], dec[:, 0, 0:P], m["trif"], ALU.mult).then_inc(dve_s, 1)
                    dve.tensor_tensor(dec[:, 1, LAT - P:LAT], dec[:, 1, LAT - P:LAT], m["trib"], ALU.mult).then_inc(dve_s, 1)
                    for x in range(3):
                        dve.wait_ge(prod.sem, prod.value(f"v{x}", i))
                        w = 2 if x < 2 else 1
                        dve.tensor_copy(v[:, 2 * x:2 * x + w, :], ps[:, bank[f"v{x}"]:bank[f"v{x}"] + w, :]).then_inc(dve_s, 1)
                    dve.wait_ge(prod.sem, prod.value("kc", i))
                    dve.wait_ge(act_n.sem, act_n.value("kdb", i))
                    for f in range(2):
                        dve.tensor_scalar(kc[:, f, :], ps[:, bank["kc"], 0:DK], kd[:, f:f + 1], None, ALU.mult).then_inc(dve_s, 1)
                    for f, n in enumerate(("fs", "bs")):
                        dve.wait_ge(prod.sem, prod.value(n, i))
                        dve.wait_ge(store_s, i * 32 + 16 * (f + 1))
                        dve.tensor_copy(stage[:, :, :], ps[:, bank[n]:bank[n] + 2, :]).then_inc(dve_s, 1)
                    q1, q2 = q[:, 0, SEQ:T], q[:, 1, SEQ:T]
                    dve.wait_ge(act_n.sem, act_n.value("q11", i))
                    dve.tensor_tensor(tmp[:, 2, :], q1, m["sin"], ALU.mult).then_inc(dve_s, 1)
                    dve.tensor_tensor(tmp[:, 3, :], q2, m["sin"], ALU.mult).then_inc(dve_s, 1)
                    dve.wait_ge(dve_n.sem, dve_n.value("q1", i))
                    dve.tensor_tensor(q1, q1, m["cos"], ALU.mult).then_inc(dve_s, 1)
                    dve.tensor_tensor(q2, q2, m["cos"], ALU.mult).then_inc(dve_s, 1)
                    dve.wait_ge(dve_n.sem, dve_n.value("q3", i))
                    dve.tensor_tensor(q1, q1, tmp[:, 3, :], ALU.subtract).then_inc(dve_s, 1)
                    dve.tensor_tensor(q2, q2, tmp[:, 2, :], ALU.add).then_inc(dve_s, 1)
                    dve.tensor_scalar(idxb[:, :], m["idxf"], -1.0, float(LAT + 1), ALU.mult, ALU.add).then_inc(dve_s, 1)
                    dve.wait_ge(dve_n.sem, dve_n.value("q5", i))
                    dve.wait_ge(store_s, i * 32 + 48)
                    for b in range(2):
                        dve.tensor_tensor(qd[:, b, :], q[:, b, SEQ:T], expo, ALU.mult).then_inc(dve_s, 1)
                    dve.wait_ge(prod.sem, prod.value("sc", i))
                    dve.wait_ge(dve_n.sem, dve_n.value("tb", i))
                    dve.tensor_tensor(sctx[:, 0, :], ps[:, bank["sc"], 0:P], dec[:, 0, 0:P], ALU.mult).then_inc(dve_s, 1)
                    dve.tensor_tensor(sctx[:, 1, :], ps[:, bank["sc"], 0:P], dec[:, 1, LAT - P:LAT], ALU.mult).then_inc(dve_s, 1)
                    for x in range(4):
                        dve.wait_ge(prod.sem, prod.value(f"s{x}", i))
                        s = ps[:, bank[f"s{x}"], :]
                        dve.tensor_tensor(ss[:, x, (x + 1) * P:T], s[:, x * P:LAT], dec[:, 0, 0:LAT - x * P], ALU.mult).then_inc(dve_s, 1)
                        dve.tensor_tensor(ss[:, x, 0:(x + 1) * P], s[:, 0:(x + 1) * P], dec[:, 1, LAT - (x + 1) * P:LAT],
                                          ALU.mult).then_inc(dve_s, 1)
                    dve.wait_ge(act_n.sem, act_n.value("eb", i))
                    for b in range(2):
                        dve.tensor_tensor(q[:, b, SEQ:T], q[:, b, SEQ:T], expo, ALU.mult).then_inc(dve_s, 1)
                    for t in range(NT + 1):
                        if t < NT:
                            dve.wait_ge(act_n.sem, act_n.value(f"o{t}b", i))
                            dve.tensor_scalar(mean[:, t, :], sumsq[:, t, :], 1.0 / DV, EPS, ALU.mult, ALU.add).then_inc(dve_s, 1)
                        if t:
                            n = t - 1
                            dve.wait_ge(pool_n.sem, pool_n.value(f"r{n}", i))
                            for f, g in enumerate((gf, gb)):
                                dve.scalar_tensor_tensor(out=g[:, n, :], in0=ps[:, bank[f"o{n}"] + f, :], scalar=rs[:, n, f:f + 1],
                                                         in1=g[:, n, :], op0=ALU.mult, op1=ALU.mult).then_inc(dve_s, 1)
                            dve.wait_ge(dve_n.sem, dve_n.value(f"o{n}b", i))
                            dve.tensor_tensor(gf[:, n, :], gf[:, n, :], gb[:, n, :], ALU.add).then_inc(dve_s, 1)
                    for d in range(KD):
                        dve.wait_ge(prod.sem, prod.value(f"w{d}", i))
                        for r, (a, n, jc) in enumerate(RANGES):
                            dve.scalar_tensor_tensor(out=c.x[:, d, a:a + n], in0=ps[:, bank[f"w{d}"] + r, 0:n],
                                                     scalar=gate[:, d, jc:jc + 1], in1=c.x[:, d, a:a + n],
                                                     op0=ALU.mult, op1=ALU.add).then_inc(dve_s, 1)


def route(c, layer):
    nc, ps = c.nc, c.ps
    G = NT * NG
    with ExitStack() as st:
        def sb(name, shape, dt=F32):
            return st.enter_context(nc.sbuf_tensor(f"route{layer}_" + name, shape, dt))

        rows = sb("rows", [P, NT, D])
        s, gr, msk, o1, o2, on, tmp = (sb(n, [P, NT, NE]) for n in ("scores", "biased", "masked", "one1", "one2", "both", "tmp"))
        pair, keep, off = sb("pair", [P, 2, G]), sb("keep", [P, NT, NG]), sb("off", [P, NT, NG])
        g8, m8, e8 = sb("g8", [P, NT, 8]), sb("m8", [P, NT, 8]), sb("e8", [P, NT, 8])
        i8, x8 = sb("i8", [P, NT, 8], U32), sb("x8", [P, NT, 8], U32)
        best, ex = sb("best", [P, NT]), sb("experts", [P, 2, NT])
        wsum, dst = sb("wsum", [P, NT]), sb("dst", [P, 2, NT])
        nb, cs, start = sb("blocks", [P, NE]), sb("cumulated", [P, 2, NE]), sb("start", [P, NE])
        cmp, eb = sb("compare", [P, NBLK, NE]), sb("block_e", [P, NBLK])
        logits, ranks, turned, taken, expd, chain, scattered = sems(
            nc, st, f"route{layer}", ["logits", "ranks", "turned", "taken", "exp", "chain", "scattered"])
        with nc.Block(no_gpsimd_drain=True) as block:
            mark = {}

            @block.vector
            def _(dve):
                n = 0

                def link(ins):
                    nonlocal n
                    n += 1
                    ins.then_inc(chain, 1)
                    dve.wait_ge(chain, n)

                link(dve.memset(g8[:, :, :], -BIG))
                dve.wait_ge(expd, 1)
                link(dve.tensor_scalar(s[:, :, :], s[:, :, :], 1.0, None, ALU.add))
                link(dve.reciprocal(s[:, :, :], s[:, :, :]))
                link(dve.tensor_tensor(gr[:, :, :], s[:, :, :], c.router_b[:, :].unsqueeze(1).to_broadcast([P, NT, NE]), ALU.add))
                m = gr[:, :, :].rearrange("p t (g e) -> p (t g) e", e=EG)
                link(dve.tensor_tensor(pair[:, 0, :], m[:, :, 0], m[:, :, 1], ALU.add))
                for a in range(EG):
                    for b in range(max(a + 1, 2), EG):
                        link(dve.tensor_tensor(pair[:, 1, :], m[:, :, a], m[:, :, b], ALU.add))
                        link(dve.tensor_tensor(pair[:, 0, :], pair[:, 0, :], pair[:, 1, :], ALU.max))
                link(dve.tensor_copy(g8[:, :, 0:NG], pair[:, 0, :].rearrange("p (t g) -> p t g", t=NT)))
                for t in range(NT):
                    link(dve.max(m8[:, t, :], g8[:, t, :]))
                    link(dve.max_index(i8[:, t, :], m8[:, t, :], g8[:, t, :]))
                link(dve.tensor_copy(best[:, :], i8[:, :, 0]))
                for t in range(NT):
                    link(dve.tensor_scalar(keep[:, t, :], c.base["iota4"], best[:, t:t + 1], None, ALU.is_equal))
                link(dve.tensor_scalar(off[:, :, :], keep[:, :, :], -1.0, BIG, ALU.add, ALU.mult))
                mm_, kp = msk[:, :, :].rearrange("p t (g e) -> p (t g) e", e=EG), keep[:, :, :].rearrange("p t g -> p (t g)")
                of = off[:, :, :].rearrange("p t g -> p (t g)")
                for e in range(EG):
                    link(dve.tensor_tensor(mm_[:, :, e], m[:, :, e], kp, ALU.mult))
                    link(dve.tensor_tensor(mm_[:, :, e], mm_[:, :, e], of, ALU.add))
                for t in range(NT):
                    link(dve.max(e8[:, t, :], msk[:, t, :]))
                    link(dve.max_index(x8[:, t, :], e8[:, t, :], msk[:, t, :]))
                for k, o in enumerate((o1, o2)):
                    link(dve.tensor_copy(ex[:, k, :], x8[:, :, k]))
                    for t in range(NT):
                        link(dve.tensor_scalar(o[:, t, :], c.base["iota16"], ex[:, k, t:t + 1], None, ALU.is_equal))
                link(dve.tensor_tensor(on[:, :, :], o1[:, :, :], o2[:, :, :], ALU.add))
                mark["onehot"] = n
                for k, o in enumerate((o1, o2)):
                    link(dve.tensor_tensor(tmp[:, :, :], o[:, :, :], s[:, :, :], ALU.mult))
                    link(dve.tensor_reduce(c.w12[:, k, :], tmp[:, :, :], AX.X, ALU.add))
                link(dve.tensor_tensor(wsum[:, :], c.w12[:, 0, :], c.w12[:, 1, :], ALU.add))
                link(dve.reciprocal(wsum[:, :], wsum[:, :]))
                for k in range(2):
                    link(dve.tensor_tensor(c.w12[:, k, :], c.w12[:, k, :], wsum[:, :], ALU.mult))
                dve.wait_ge(ranks, 1)
                count = ps[:, 1, NT * NE:(NT + 1) * NE]
                link(dve.tensor_scalar(nb[:, :], count, 0.0, None, ALU.is_gt))
                for b in range(1, NT):
                    link(dve.scalar_tensor_tensor(out=nb[:, :], in0=count, scalar=float(b * P), in1=nb[:, :],
                                                  op0=ALU.is_gt, op1=ALU.add))
                link(dve.tensor_copy(cs[:, 0, :], nb[:, :]))
                a = 0
                for sh in (1, 2, 4, 8):
                    link(dve.tensor_copy(cs[:, 1 - a, 0:sh], cs[:, a, 0:sh]))
                    link(dve.tensor_tensor(cs[:, 1 - a, sh:NE], cs[:, a, sh:NE], cs[:, a, 0:NE - sh], ALU.add))
                    a = 1 - a
                link(dve.tensor_tensor(start[:, :], cs[:, a, :], nb[:, :], ALU.subtract))
                for t in range(NT):
                    link(dve.scalar_tensor_tensor(out=tmp[:, t, :], in0=start[:, :], scalar=float(P),
                                                  in1=ps[:, 1, t * NE:(t + 1) * NE], op0=ALU.mult, op1=ALU.add))
                for k, o in enumerate((o1, o2)):
                    link(dve.tensor_tensor(o[:, :, :], o[:, :, :], tmp[:, :, :], ALU.mult))
                    link(dve.tensor_reduce(dst[:, k, :], o[:, :, :], AX.X, ALU.add))
                link(dve.tensor_copy(c.dest[:, :, :], dst[:, :, :]))
                mark["dest"] = n
                link(dve.tensor_tensor(cmp[:, :, :], cs[:, a, :].unsqueeze(1).to_broadcast([P, NBLK, NE]),
                                       c.base["iotab"].unsqueeze(2).to_broadcast([P, NBLK, NE]), ALU.is_le))
                link(dve.tensor_reduce(eb[:, :], cmp[:, :, :], AX.X, ALU.add))
                link(dve.tensor_scalar(c.blk_e[:, :], eb[:, :], float(NE - 1), None, ALU.min))

            @block.tensor
            def _(pe):
                for t in range(NT):
                    for k in range(KD):
                        mm = pe.matmul(ps[:, 0, t * NE:(t + 1) * NE], c.h[:, k, t * P:(t + 1) * P], c.router[:, k, :],
                                       start=(k == 0), stop=(k == KD - 1))
                mm.then_inc(logits, 1)
                for g in range(2 * NT):
                    if g >= 4:
                        pe.wait_ge(taken, g - 3)
                    for k in range(4):
                        mm = pe.transpose(ps[:, 2 + g % 4, k * P:(k + 1) * P],
                                          c.h[:, 4 * (g % 2) + k, (g // 2) * P:(g // 2 + 1) * P], c.base["ident"])
                    mm.then_inc(turned, 1)
                pe.wait_ge(chain, mark["onehot"])
                for t in range(NT + 1):
                    for u in range(min(t + 1, NT)):
                        mm = pe.matmul(ps[:, 1, t * NE:(t + 1) * NE], c.base["before"] if u == t else c.base["ones"],
                                       on[:, u, :], start=(u == 0), stop=(u == min(t, NT - 1)))
                mm.then_inc(ranks, 1)

            @block.scalar
            def _(act):
                act.wait_ge(logits, 1)
                nc.scalar.activation(s[:, :, :], ps[:, 0, 0:NT * NE].rearrange("p (t e) -> p t e", t=NT), ACT.Exp,
                                     scale=-1.0).then_inc(expd, 1)
                for g in range(2 * NT):
                    act.wait_ge(turned, g + 1)
                    nc.scalar.copy(rows[:, g // 2, 512 * (g % 2):512 * (g % 2 + 1)], ps[:, 2 + g % 4, :]).then_inc(taken, 1)

            @block.gpsimd
            def _(pool):
                pool.wait_ge(chain, mark["dest"])
                for t in range(NT):
                    pool.wait_ge(taken, 2 * t + 2)
                    for k in range(TOPK):
                        pool.indirect_dma_start(c.xs, bass.IndirectOffsetOnAxis(c.dest[:, k, t:t + 1], 0),
                                                rows[:, t, :], None).then_inc(scattered, 16)
                pool.wait_ge(scattered, 16 * NT * TOPK)


def experts(c, layer):
    nc, ops, ps = c.nc, c.ops, c.ps
    PAIRS_B = (NBLK - 1) // 2
    order = ["x", "g", "u", "h", "d"]
    with ExitStack() as st:
        def sb(name, shape):
            return st.enter_context(nc.sbuf_tensor(f"moe{layer}_" + name, shape, F32))

        xr, xt = sb("rows", [P, 2, D]), sb("rows_t", [P, 2, KD, P])
        sil, hid, ht = sb("silu", [P, FE]), sb("hidden", [P, FE]), sb("hidden_t", [P, 4, P])
        y = sb("out_rows", [P, 2, D])
        xfull = sems(nc, st, f"moe{layer}", ["x_full0", "x_full1"])
        wfull = sems(nc, st, f"moe{layer}", [f"{n}_full{u}" for u in range(2) for n in "gud"])
        stored = sems(nc, st, f"moe{layer}", ["stored0", "stored1"])
        turned, gated, upped, hturned, downed, xa, xv, silued, hidden, htaken, ya, yv = sems(
            nc, st, f"moe{layer}", ["x_turned", "gate", "up", "h_turned", "down", "xt_act", "xt_dve", "silu", "hidden",
                                    "ht", "y_act", "y_dve"])
        wslot = [[c.slot(3 * u).rearrange("p (k n) -> p k n", k=KD), c.slot(3 * u + 1).rearrange("p (k n) -> p k n", k=KD),
                  c.slot(3 * u + 2).rearrange("p (k n) -> p k n", k=4)] for u in range(2)]
        wsrc = [ops[n][layer].rearrange("e (k p) n -> e p k n", p=P) for n in ("moe_w_gate", "moe_w_up", "moe_w_down")]
        with nc.Block(no_gpsimd_drain=True) as block:
            @block.sync
            def _(sp):
                def load_rows(b, u):
                    sp.dma_start(xr[:, u, :], c.xs.rearrange("(b p) d -> b p d", p=P)[bass.ds(b, 1)].rearrange("a p d -> (a p) d"))\
                      .then_inc(xfull[u], 16)

                def load_weight(e, u, w):
                    sp.dma_start(wslot[u][w], wsrc[w][bass.ds(e, 1)].rearrange("a p k n -> (a p) k n")).then_inc(wfull[3 * u + w], 16)

                def expert_of(b):
                    return sp.value_load(c.blk_e[0:1, bass.ds(b, 1)], min_val=0, max_val=NE - 1)

                for u in range(2):
                    load_rows(u, u)
                    e = expert_of(u)
                    for w in range(3):
                        load_weight(e, u, w)

                def refill(i, u):
                    b = i * 2 + u
                    e = expert_of(b + 2)
                    sp.wait_ge(turned, b + 1)
                    load_rows(b + 2, u)
                    for w, (used, n) in enumerate(((gated, 1), (upped, 1), (downed, 2))):
                        sp.wait_ge(used, b + n)
                        load_weight(e, u, w)

                with sp.Fori(0, PAIRS_B - 1) as i:
                    for u in range(2):
                        refill(i, u)
                refill(PAIRS_B - 1, 0)

            @block.tensor
            def _(pe):
                def turn_rows(b, u, i):
                    pe.wait_ge(xfull[u], 16 * (i + 1))
                    pe.wait_ge(xa, b + 1)
                    pe.wait_ge(xv, b + 1)
                    for k in range(KD):
                        mm = pe.transpose(ps[:, k // 4, (k % 4) * P:(k % 4 + 1) * P], xr[:, u, k * P:(k + 1) * P], c.base["ident"])
                    mm.then_inc(turned, 1)

                def products(b, u, i, following):
                    pe.wait_ge(xa, b + 2)
                    pe.wait_ge(xv, b + 2)
                    for w, bank, freed, done in ((0, 2, silued, gated), (1, 3, hidden, upped)):
                        pe.wait_ge(wfull[3 * u + w], 16 * (i + 1))
                        pe.wait_ge(freed, b + 1)
                        for k in range(KD):
                            mm = pe.matmul(ps[:, bank, :], xt[:, u, k, :], wslot[u][w][:, k, :], start=(k == 0), stop=(k == KD - 1))
                        mm.then_inc(done, 1)
                    following()
                    pe.wait_ge(hidden, b + 2)
                    pe.wait_ge(htaken, b + 1)
                    for k in range(4):
                        mm = pe.transpose(ps[:, 4, k * P:(k + 1) * P], hid[:, k * P:(k + 1) * P], c.base["ident"])
                    mm.then_inc(hturned, 1)
                    pe.wait_ge(htaken, b + 2)
                    pe.wait_ge(wfull[3 * u + 2], 16 * (i + 1))
                    pe.wait_ge(ya, b + 1)
                    pe.wait_ge(yv, b + 1)
                    for n in range(2):
                        for k in range(4):
                            mm = pe.matmul(ps[:, 5 + n, :], ht[:, k, :], wslot[u][2][:, k, n * 512:(n + 1) * 512],
                                           start=(k == 0), stop=(k == 3))
                    mm.then_inc(downed, 1)

                for ahead in (hturned, downed):
                    pe.sem_inc(ahead, 1)
                turn_rows(0, 0, 0)
                with pe.Fori(0, PAIRS_B) as i:
                    products(i * 2, 0, i, lambda: turn_rows(i * 2 + 1, 1, i))
                    products(i * 2 + 1, 1, i, lambda: turn_rows(i * 2 + 2, 0, i + 1))
                products(NBLK - 1, 0, PAIRS_B, lambda: None)

            @block.scalar
            def _(act):
                def body(b, u, i):
                    act.wait_ge(turned, b + 1)
                    nc.scalar.copy(xt[:, u, 0:4, :], ps[:, 0, :].rearrange("p (k n) -> p k n", k=4)).then_inc(xa, 1)
                    act.wait_ge(gated, b + 1)
                    act.wait_ge(hidden, b + 1)
                    nc.scalar.activation(sil[:, :], ps[:, 2, :], ACT.Silu).then_inc(silued, 1)
                    act.wait_ge(downed, b + 2)
                    act.wait_ge(stored[u], i * 16 + 16)
                    nc.scalar.copy(y[:, u, 0:512], ps[:, 5, :]).then_inc(ya, 1)
                    act.wait_ge(ya, b + 2)
                    act.wait_ge(yv, b + 2)
                    act.dma_start(c.ys.rearrange("(b p) d -> b p d", p=P)[bass.ds(b, 1)].rearrange("a p d -> (a p) d"), y[:, u, :])\
                       .then_inc(stored[u], 16)

                for ahead in (xa, silued, ya):
                    act.sem_inc(ahead, 1)
                for ahead in stored:
                    act.sem_inc(ahead, 16)
                with act.Fori(0, PAIRS_B) as i:
                    body(i * 2, 0, i)
                    body(i * 2 + 1, 1, i)
                body(NBLK - 1, 0, PAIRS_B)
                act.wait_ge(stored[0], 16 * (PAIRS_B + 2))
                act.wait_ge(stored[1], 16 * (PAIRS_B + 1))

            @block.vector
            def _(dve):
                def body(b, u, i):
                    dve.wait_ge(turned, b + 1)
                    dve.tensor_copy(xt[:, u, 4:8, :], ps[:, 1, :].rearrange("p (k n) -> p k n", k=4)).then_inc(xv, 1)
                    dve.wait_ge(silued, b + 2)
                    dve.wait_ge(upped, b + 1)
                    dve.wait_ge(hturned, b + 1)
                    dve.tensor_tensor(hid[:, :], sil[:, :], ps[:, 3, :], ALU.mult).then_inc(hidden, 1)
                    dve.wait_ge(hturned, b + 2)
                    dve.wait_ge(downed, b + 1)
                    dve.tensor_copy(ht[:, :, :], ps[:, 4, :].rearrange("p (k n) -> p k n", k=4)).then_inc(htaken, 1)
                    dve.wait_ge(downed, b + 2)
                    dve.wait_ge(stored[u], i * 16 + 16)
                    dve.tensor_copy(y[:, u, 512:1024], ps[:, 6, :]).then_inc(yv, 1)

                for ahead in (xv, hidden, htaken, yv):
                    dve.sem_inc(ahead, 1)
                with dve.Fori(0, PAIRS_B) as i:
                    body(i * 2, 0, i)
                    body(i * 2 + 1, 1, i)
                body(NBLK - 1, 0, PAIRS_B)


def combine(c, layer):
    nc, ps = c.nc, c.ps
    gate = c.mod[:, layer, 40:48, :]
    with ExitStack() as st:
        y = st.enter_context(nc.sbuf_tensor(f"comb{layer}_rows", [P, 2, TOPK, D], F32))
        got = sems(nc, st, f"comb{layer}", [f"got{u}{k}" for u in range(2) for k in range(2)])
        weighed, summed, turned, added = sems(nc, st, f"comb{layer}", ["weighed", "summed", "turned", "added"])
        with nc.Block(no_gpsimd_drain=True) as block:
            @block.gpsimd
            def _(pool):
                for t in range(NT):
                    if t >= 2:
                        pool.wait_ge(turned, t - 1)
                    for k in range(TOPK):
                        pool.indirect_dma_start(y[:, t % 2, k, :], None, c.ys,
                                                bass.IndirectOffsetOnAxis(c.dest[:, k, t:t + 1], 0)).then_inc(got[2 * (t % 2) + k], 16)

            @block.tensor
            def _(pe):
                for t in range(NT):
                    pe.wait_ge(summed, t + 1)
                    if t >= 4:
                        pe.wait_ge(added, (t - 3) * KD)
                    for k in range(KD):
                        mm = pe.transpose(ps[:, 2 * (t % 4) + k // 4, (k % 4) * P:(k % 4 + 1) * P],
                                          y[:, t % 2, 0, k * P:(k + 1) * P], c.base["ident"])
                    mm.then_inc(turned, 1)

            @block.vector
            def _(dve):
                for t in range(NT):
                    dve.wait_ge(got[2 * (t % 2)], 16 * (t // 2 + 1))
                    dve.wait_ge(got[2 * (t % 2) + 1], 16 * (t // 2 + 1))
                    dve.tensor_scalar(y[:, t % 2, 0, :], y[:, t % 2, 0, :], c.w12[:, 0, t:t + 1], None, ALU.mult).then_inc(weighed, 1)
                    dve.wait_ge(weighed, t + 1)
                    dve.scalar_tensor_tensor(out=y[:, t % 2, 0, :], in0=y[:, t % 2, 1, :], scalar=c.w12[:, 1, t:t + 1],
                                             in1=y[:, t % 2, 0, :], op0=ALU.mult, op1=ALU.add).then_inc(summed, 1)
                    dve.wait_ge(turned, t + 1)
                    jc = 0 if t == 0 else 1
                    for k in range(KD):
                        cols = slice(t * P, (t + 1) * P)
                        dve.scalar_tensor_tensor(out=c.x[:, k, cols], in0=ps[:, 2 * (t % 4) + k // 4, (k % 4) * P:(k % 4 + 1) * P],
                                                 scalar=gate[:, k, jc:jc + 1], in1=c.x[:, k, cols],
                                                 op0=ALU.mult, op1=ALU.add).then_inc(added, 1)


def write_out(c):
    nc, ops, ps = c.nc, c.ops, c.ps
    with ExitStack() as st:
        rows = st.enter_context(nc.sbuf_tensor("out_rows", [P, NT, D], F32))
        turned, taken, taken_v, out_s = sems(nc, st, "out", ["turned", "act", "dve", "stored"])
        with nc.Block(no_gpsimd_drain=True) as block:
            @block.tensor
            def _(pe):
                for g in range(2 * NT):
                    if g >= 8:
                        pe.wait_ge(taken, (g - 8) // 2 + 1)
                        pe.wait_ge(taken_v, (g - 8) // 2 + 1)
                    for k in range(4):
                        mm = pe.transpose(ps[:, g % 8, k * P:(k + 1) * P],
                                          c.h[:, 4 * (g % 2) + k, (g // 2) * P:(g // 2 + 1) * P], c.base["ident"])
                    mm.then_inc(turned, 1)

            @block.scalar
            def _(act):
                for g in range(0, 2 * NT, 2):
                    act.wait_ge(turned, g + 1)
                    nc.scalar.copy(rows[:, g // 2, 0:512], ps[:, g % 8, :]).then_inc(taken, 1)

            @block.vector
            def _(dve):
                for g in range(1, 2 * NT, 2):
                    dve.wait_ge(turned, g + 1)
                    dve.tensor_copy(rows[:, g // 2, 512:1024], ps[:, g % 8, :]).then_inc(taken_v, 1)

            @block.sync
            def _(sp):
                for t in range(NT):
                    sp.wait_ge(taken, t + 1)
                    sp.wait_ge(taken_v, t + 1)
                    dst = ops["y_prompt"][0] if t == 0 else ops["y_sample"][0, (t - 1) * P:t * P]
                    sp.dma_start(dst, rows[:, t, :]).then_inc(out_s, 16)
                sp.wait_ge(out_s, 16 * NT)


def trunk_step(nc, ops):
    with ExitStack() as stack:
        c = Chip(nc, stack, ops)
        setup(c)
        modulation(c)
        counters = [0, 0]
        for layer in range(DEPTH):
            kind = layer % 3
            norm(c, f"norm1_{layer}", c.amp[:, layer, 0], c.mod[:, layer, 0:8, :])
            (mla, retention)[kind](c, layer, counters[kind])
            counters[kind] += 1
            norm(c, f"norm2_{layer}", c.amp[:, layer, 1], c.mod[:, layer, 24:32, :])
            route(c, layer)
            experts(c, layer)
            combine(c, layer)
        norm(c, "norm_final", c.fin2, c.zero2)
        write_out(c)


_INS = ["x_prompt", "x_sample", "cache_mla", "state_ret", "c", "c_ctx", "norm1_g", "norm2_g", "ada_w", "ada_b",
        "final_norm_g", "mla_w_in", "mla_q_norm_g", "mla_kv_norm_g", "mla_w_uq", "mla_w_ukv", "mla_w_o",
        "ret_w_in", "ret_decay_f", "ret_decay_b", "ret_w_o", "router_w", "router_b",
        "moe_w_gate", "moe_w_up", "moe_w_down"]
_CONSTS = ["base_consts", "mla_consts", "ret_consts", "trig_consts"]
_OUTS = {"y_prompt": (1, SEQ, D), "y_sample": (1, LAT, D), "new_cache": (1, 1, SEQ, KVL + ROPE),
         "new_state": (1, 1, 2, RH, DK, DV)}


def kernel(**inputs):
    import concourse.bacc as bacc
    from concourse.bass_utils import run_bass_kernel_spmd

    nc = bacc.Bacc("TRN2", target_bir_lowering=False, num_devices=1)
    arrays, ops = {}, {}
    for name, a in [(n, inputs[n]) for n in _INS] + list(zip(_CONSTS, shape_constants())):
        a = np.ascontiguousarray(a)
        arrays["in_" + name] = a
        ops[name] = nc.dram_tensor("in_" + name, a.shape, F32, kind="ExternalInput").ap()
    for name, shape in _OUTS.items():
        ops[name] = nc.dram_tensor("out_" + name, shape, F32, kind="ExternalOutput").ap()
    for name in ("rows_in", "rows_out"):
        ops[name] = nc.dram_tensor(name, (NBLK * P, D), F32, kind="Internal").ap()
    trunk_step(nc, ops)
    r = run_bass_kernel_spmd(nc, [arrays], core_ids=[0])
    return tuple(r.results[0]["out_" + name] for name in _OUTS)
```

```python
from contextlib import ExitStack

import numpy as np

import concourse.bass as bass
import concourse.mybir as mybir
from concourse.alu_op_type import AluOpType as ALU

F32 = mybir.dt.float32
F32R = mybir.dt.float32r
I32 = mybir.dt.int32
U32 = mybir.dt.uint32
ACT = mybir.ActivationFunctionType
AX = mybir.AxisListType

P = 128
D = 1024
KD = D // P
SEQ, LAT, PAST = 128, 512, 128
T = SEQ + LAT
NT = T // P
RANGES = ((0, SEQ, 0), (SEQ, LAT, 1))
DEPTH = 2
EPS = 1e-6
GRID_W = 64
BASE = 10000.0

QL, KVL, ROPE, NOPE, VD, HEADS = 384, 256, 64, 128, 128, 8
KEYS = T + PAST
NKT = KEYS // P
LKEYS = LAT + PAST
PAIRS = HEADS // 2
UQ = NOPE + ROPE
MLA_SCALE = float(UQ) ** -0.5

RH, DK, DV = 4, 256, 512
KSCALE = float(DK) ** -0.5

NE, NG, EG, FE = 16, 4, 4, 512
TOPK = 2
ASSIGNED = T * TOPK
NOVER = (ASSIGNED - NE) // P
NBLK = (NE + NOVER + 1) // 2 * 2
BIG = 3.0e38

SLOT = 4096
NSLOT = 6


class Steps:

    def __init__(self, sem, names, ahead=0):
        self.sem, self.per, self.ahead = sem, len(names), ahead
        self.pos = {n: i + 1 for i, n in enumerate(names)}
        assert len(self.pos) == len(names)

    def value(self, name, i=0):
        return i * self.per + (self.pos[name] + self.ahead)

    def before(self, i):
        assert self.ahead
        return i * self.per + self.ahead


BASE_COLS = {"ident": P, "ones": P, "before": P, "iota16": NE, "iota4": NG, "iotab": NBLK, "pick": 2}
MLA_COLS = {"swap": P, "rcos": LAT, "rsin": LAT}
RET_COLS = {"relf": LAT, "relb": LAT, "trif": P, "trib": P, "kf": 1, "kb": 1}
TRIG_COLS = {"cos": LAT, "sin": LAT, "idxf": LAT}


def _width(cols):
    return sum(cols.values())


def _views(tile, cols):
    at, out = 0, {}
    for n, w in cols.items():
        out[n] = tile[:, at:at + w]
        at += w
    return out


def shape_constants():
    f = np.float32
    p, m = np.arange(P)[:, None], np.arange(P)[None, :]
    n = np.arange(LAT)[None, :]
    one = np.ones((P, 1), f)
    base = [np.eye(P), np.ones((P, P)), p < m, one * np.arange(NE), one * np.arange(NG),
            one * np.arange(NBLK), p % 2 == np.arange(2)]
    d = np.arange(P) % ROPE
    inv = (f(BASE) ** (-np.arange(0, ROPE // 2, 2, dtype=f) / f(ROPE // 2))).astype(f)[d % 16]
    where = np.where((d < 32)[:, None], n // GRID_W, n % GRID_W).astype(f)
    ang = (where * inv[:, None]).astype(f)
    sign = np.where(d % 32 < 16, -1.0, 1.0)[:, None]
    partner = (p // 32) * 32 + (p % 32 + 16) % 32
    mla = [partner == m, np.cos(ang), np.sin(ang) * sign]
    rel_f, rel_b = n - p, p + (LAT - P) - n
    ret = [np.maximum(rel_f, 0), np.maximum(rel_b, 0), m >= p, m <= p, P - 1 - p, p]
    inv = (f(BASE) ** (-np.linspace(0.0, 1.0, DK // 2, dtype=f))).astype(f)
    ang = (n.astype(f) * inv[:, None]).astype(f)
    trig = [np.cos(ang), np.sin(ang), one * (n + 1)]
    return [np.concatenate([np.asarray(a, f) for a in g], axis=1) for g in (base, mla, ret, trig)]


class Chip:

    def __init__(self, nc, stack, ops):
        self.nc, self.ops = nc, ops

        def sb(name, shape, dt=F32):
            return stack.enter_context(nc.sbuf_tensor(name, shape, dt))

        self.ps = stack.enter_context(nc.psum_tensor("ps", [P, 8, 512], F32))
        self.x = sb("x_resid", [P, KD, T])
        self.h = sb("h_normed", [P, KD, T])
        self.ring = sb("weight_ring", [P, NSLOT * SLOT])
        self.base_tile = sb("base_consts", [P, _width(BASE_COLS)])
        self.base = _views(self.base_tile, BASE_COLS)
        self.mod = sb("modulation", [P, DEPTH, 48, 2])
        self.amp = sb("norm_amplitude", [P, DEPTH, 2, KD, 2])
        self.cols_a = sb("norm_gain_and_ada_bias", [P, P])
        self.cols_b = sb("other_columns", [P, 32])
        self.zero2 = sb("no_shift", [P, KD, 2])
        self.fin2 = sb("final_gain", [P, KD, 2])
        self.router = sb("router_w", [P, KD, NE])
        self.router_b = sb("router_b", [P, NE])
        self.eps = sb("eps", [P, 1])
        self.w12 = sb("route_weights", [P, TOPK, NT])
        self.dest = sb("route_rows", [P, TOPK, NT], I32)
        self.blk_e = sb("block_expert", [P, NBLK], I32)
        self.turns = sb("block_pairs", [P, 3], I32)
        self.norm_sems = sems(nc, stack, "norm", ["squared", "summed", "rooted", "inverted", "scaled", "shifted"])
        self.ada_full = sems(nc, stack, "ada", [f"full{i}" for i in range(NSLOT)])
        self.moe_full = [sems(nc, stack, f"moe{l}", [f"{n}_full{u}" for u in range(2) for n in "gud"]) for l in range(DEPTH)]
        self.w_in_full, self.wq_full, self.wkv_full, self.wo_full = sems(nc, stack, "mla", ["w_in", "wq_full", "wkv_full", "wo_full"])
        self.xs = ops["rows_in"]
        self.ys = ops["rows_out"]

    def slot(self, s, width=SLOT):
        return self.ring[:, s * SLOT:s * SLOT + width]

    def bank2(self, g):
        b = 2 * (g % 4)
        return self.ps[:, b:b + 2, :]


def sems(nc, stack, stage, names):
    return [stack.enter_context(nc.semaphore(f"{stage}_{n}")) for n in names]


def setup(c, cond4):
    nc, ops, ps = c.nc, c.ops, c.ps
    with ExitStack() as st:
        xt = st.enter_context(nc.sbuf_tensor("x_rows", [P, NT, D], F32))
        rows_a = st.enter_context(nc.sbuf_tensor("vector_rows_a", [P, P], F32))
        rows_b = st.enter_context(nc.sbuf_tensor("vector_rows_b", [P, P], F32))
        cond = st.enter_context(nc.sbuf_tensor("silu_cond", [P, KD, 2], F32))
        (silued,) = sems(nc, st, "setup", ["silu"])
        consts_in, rows_in, x_in, small_in, turned, taken_a, taken_v, memsets = sems(
            nc, st, "setup", ["consts", "rows", "x", "small", "turned", "act", "dve", "memset"])
        with nc.Block(no_gpsimd_drain=True) as block:
            @block.sync
            def _(sp):
                sp.dma_start(c.base_tile[:, :], ops["base_consts"]).then_inc(consts_in, 16)
                sp.dma_start(xt[:, 0, :], ops["x_prompt"][0]).then_inc(x_in, 16)
                sp.dma_start(xt[:, 1:NT, :], ops["x_sample"][0].rearrange("(t p) d -> p t d", p=P)).then_inc(x_in, 16)
                sp.dma_start(c.router[:, :, :], ops["router_w"].rearrange("(k p) e -> p k e", p=P)).then_inc(small_in, 16)
                sp.dma_start(c.router_b[:, :], ops["router_b"].rearrange("(a e) -> a e", a=1).broadcast_to([P, NE])).then_inc(small_in, 16)
                for n in range(NSLOT):
                    load_ada(c, sp, n)
                sp.wait_ge(small_in, 32)

            @block.gpsimd
            def _(pool):
                pool.memset(c.eps[:, :], EPS).then_inc(memsets, 1)
                pool.memset(c.zero2[:, :, :], 0.0).then_inc(memsets, 1)
                pool.memset(rows_b[:, :], 0.0).then_inc(memsets, 1)

            @block.scalar
            def _(act):
                act.dma_start(rows_a[0:16, :], ops["norm1_g"].rearrange("l (k p) -> (l k) p", p=P)).then_inc(rows_in, 16)
                act.dma_start(rows_a[16:32, :], ops["norm2_g"].rearrange("l (k p) -> (l k) p", p=P)).then_inc(rows_in, 16)
                act.dma_start(rows_a[32:128, :], ops["ada_b"].rearrange("l (k p) -> (l k) p", p=P)).then_inc(rows_in, 16)
                act.wait_ge(memsets, 3)
                for r, n in ((0, "c_ctx"), (8, "c"), (16, "final_norm_g"), (24, "mla_q_norm_g"), (27, "mla_kv_norm_g")):
                    v = ops[n] if len(ops[n].shape) == 1 else ops[n].rearrange("a n -> (a n)")
                    w = v.shape[0] // P
                    act.dma_start(rows_b[r:r + w, :], v.rearrange("(k p) -> k p", p=P)).then_inc(rows_in, 16)
                for g in range(1, 2 * NT, 2):
                    act.wait_ge(turned, g + 3)
                    nc.scalar.copy(c.x[:, 4:8, (g // 2) * P:(g // 2 + 1) * P],
                                   ps[:, 2 + g % 6, :].rearrange("p (k n) -> p k n", k=4)).then_inc(taken_a, 1)
                act.wait_ge(taken_v, 3)
                for j in range(2):
                    nc.scalar.activation(cond[:, :, j], c.cols_b[:, 8 * j:8 * j + 8], ACT.Silu).then_inc(silued, 1)
                act.wait_ge(silued, 2)
                nc.scalar.activation(cond4[:, :, 0:2], cond[:, :, :], ACT.Identity).then_inc(silued, 1)

            @block.tensor
            def _(pe):
                pe.wait_ge(consts_in, 16)
                pe.wait_ge(rows_in, 16 * 8)
                pe.wait_ge(memsets, 3)
                pe.transpose(ps[:, 0, 0:P], rows_a[:, :], c.base["ident"]).then_inc(turned, 1)
                pe.transpose(ps[:, 1, 0:P], rows_b[:, :], c.base["ident"]).then_inc(turned, 1)
                pe.wait_ge(x_in, 32)
                for g in range(2 * NT):
                    if g >= 6:
                        pe.wait_ge(taken_v, 3 + (g - 6) // 2 + 1)
                        pe.wait_ge(taken_a, (g - 6) // 2 + 1)
                    for k in range(4):
                        mm = pe.transpose(ps[:, 2 + g % 6, k * P:(k + 1) * P],
                                          xt[:, g // 2, (4 * (g % 2) + k) * P:(4 * (g % 2) + k + 1) * P], c.base["ident"])
                    mm.then_inc(turned, 1)

            @block.vector
            def _(dve):
                dve.wait_ge(turned, 1)
                dve.tensor_copy(c.cols_a[:, :], ps[:, 0, 0:P]).then_inc(taken_v, 1)
                dve.wait_ge(turned, 2)
                dve.tensor_copy(c.cols_b[:, :], ps[:, 1, 0:32]).then_inc(taken_v, 1)
                dve.wait_ge(taken_v, 2)
                dve.tensor_copy(c.fin2[:, :, 0], c.cols_b[:, 16:24]).then_inc(taken_v, 1)
                for g in range(0, 2 * NT, 2):
                    dve.wait_ge(turned, g + 3)
                    dve.tensor_copy(c.x[:, 0:4, (g // 2) * P:(g // 2 + 1) * P],
                                    ps[:, 2 + g % 6, :].rearrange("p (k n) -> p k n", k=4)).then_inc(taken_v, 1)
                dve.tensor_copy(c.fin2[:, :, 1], c.cols_b[:, 16:24]).then_inc(taken_v, 1)
                dve.wait_ge(silued, 3)
                dve.tensor_tensor(cond4[:, :, 2:4], cond[:, :, :], cond4[:, :, 0:2].bitcast(F32), ALU.subtract).then_inc(taken_v, 1)


ADA_CH = 6 * D // 512


def load_ada(c, sp, n):
    src = c.ops["ada_w"].rearrange("l (k p) (g n) -> l g p k n", p=P, n=512)[n // ADA_CH, n % ADA_CH]
    sp.dma_start(c.slot(n % NSLOT).rearrange("p (k n) -> p k n", k=KD), src).then_inc(c.ada_full[n % NSLOT], 16)


def modulation(c, cond4, prefetch):
    nc, ops, ps = c.nc, c.ops, c.ps
    N = DEPTH * ADA_CH
    UN = 4
    with ExitStack() as st:
        whi = st.enter_context(nc.sbuf_tensor("ada_w_hi", [P, 4, 2, 512], F32R))
        wlo = st.enter_context(nc.sbuf_tensor("ada_w_lo", [P, 4, 2, 512], F32R))
        rows = st.enter_context(nc.sbuf_tensor("ada_rows", [4, 2, 512], F32))
        hi_s, lo_s, used, rowed, turned, biased, amp = sems(nc, st, "ada", ["w_hi", "w_lo", "used", "rows", "turned", "biased", "amp"])

        def part(n, x):
            return c.slot(n % NSLOT).rearrange("p (k n) -> p k n", k=KD)[:, 2 * x:2 * x + 2, :]

        with nc.Block(no_gpsimd_drain=True) as block:
            @block.sync
            def _(sp):
                for n in range(NSLOT, N):
                    sp.wait_ge(lo_s, UN * (n - NSLOT + 1))
                    load_ada(c, sp, n)
                prefetch(sp, lo_s, UN, N)

            @block.scalar
            def _(act):
                for n in range(N):
                    act.wait_ge(c.ada_full[n % NSLOT], 16 * (n // NSLOT + 1))
                    for x in range(UN):
                        if UN * n + x >= 4:
                            act.wait_ge(used, UN * n + x - 3)
                        nc.scalar.activation(whi[:, x], part(n, x), ACT.Identity).then_inc(hi_s, 1)

            @block.tensor
            def _(pe):
                def turn(n):
                    pe.wait_ge(rowed, n + 1)
                    for b in range(4):
                        col = 2 * ((n % ADA_CH) * 4 + b)
                        mm = pe.matmul(ps[:, 4 + n // ADA_CH, col:col + 2], rows[:, n % 2, b * P:(b + 1) * P],
                                       c.base["pick"][0:4, :], start=True, stop=True)
                    mm.then_inc(turned, 1)

                for n in range(N):
                    if n >= 4:
                        pe.wait_ge(rowed, n - 3)
                    for x in range(UN):
                        pe.wait_ge(lo_s, UN * n + x + 1)
                        for k in range(2):
                            for w in (whi, wlo):
                                mm = pe.matmul(ps[0:4, n % 4, :], cond4[:, 2 * x + k, :], w[:, x, k, :],
                                               start=(x == 0 and k == 0 and w is whi), stop=(x == UN - 1 and k == 1 and w is wlo))
                        mm.then_inc(used, 1)
                    if n:
                        turn(n - 1)
                turn(N - 1)

            @block.vector
            def _(dve):
                def take_rows(n):
                    dve.wait_ge(used, UN * (n + 1))
                    if n >= 2:
                        dve.wait_ge(turned, n - 1)
                    dve.tensor_copy(rows[:, n % 2, :], ps[0:4, n % 4, :]).then_inc(rowed, 1)

                for n in range(N):
                    for x in range(UN):
                        dve.wait_ge(hi_s, UN * n + x + 1)
                        dve.tensor_tensor(wlo[:, x], part(n, x), whi[:, x].bitcast(F32), ALU.subtract).then_inc(lo_s, 1)
                    if n:
                        take_rows(n - 1)
                take_rows(N - 1)
                for layer in range(DEPTH):
                    dve.wait_ge(turned, (layer + 1) * ADA_CH)
                    bias = c.cols_a[:, 32 + 48 * layer:32 + 48 * layer + 48]
                    for j in range(2):
                        dve.tensor_tensor(c.mod[:, layer, :, j],
                                          ps[:, 4 + layer, 0:96].rearrange("p (m j) -> p m j", j=2)[:, :, j],
                                          bias, ALU.add).then_inc(biased, 1)
                    dve.wait_ge(biased, 2 * layer + 2)
                    for n, m in ((0, 1), (1, 4)):
                        gain = c.cols_a[:, 16 * n + 8 * layer:16 * n + 8 * layer + 8]
                        for j in range(2):
                            dve.scalar_tensor_tensor(out=c.amp[:, layer, n, :, j],
                                                     in0=c.mod[:, layer, 8 * m:8 * m + 8, j], scalar=1.0,
                                                     in1=gain, op0=ALU.add, op1=ALU.mult).then_inc(amp, 1)


def norm(c, call, amp, shift, prefetch=None):
    nc, ps = c.nc, c.ps
    with ExitStack() as st:
        rstd = st.enter_context(nc.sbuf_tensor(f"norm{call}_rstd", [P, T], F32))
        squared, summed, rooted, inverted, scaled, shifted = c.norm_sems
        before2, before8, before16 = 2 * call, KD * call, 2 * KD * call
        with nc.Block(no_gpsimd_drain=True) as block:
            if prefetch:
                @block.sync
                def _(sp):
                    prefetch(sp)

            @block.scalar
            def _(act):
                for k in range(KD):
                    nc.scalar.activation(c.h[:, k, :], c.x[:, k, :], ACT.Square).then_inc(squared, 1)
                for r, (a, n, j) in enumerate(RANGES):
                    act.wait_ge(summed, before2 + r + 1)
                    nc.scalar.activation(rstd[:, a:a + n], ps[:, r, 0:n], ACT.Sqrt, bias=c.eps[:, :],
                                         scale=1.0 / D).then_inc(rooted, 1)
                i = 0
                for k in range(KD):
                    for a, n, j in RANGES:
                        i += 1
                        act.wait_ge(scaled, before16 + i)
                        nc.scalar.activation(c.h[:, k, a:a + n], c.h[:, k, a:a + n], ACT.Identity,
                                             bias=shift[:, k, j:j + 1]).then_inc(shifted, 1)

            @block.tensor
            def _(pe):
                for r, (a, n, j) in enumerate(RANGES):
                    for k in range(KD):
                        pe.wait_ge(squared, before8 + k + 1)
                        mm = pe.matmul(ps[:, r, 0:n], c.base["ones"], c.h[:, k, a:a + n],
                                       start=(k == 0), stop=(k == KD - 1))
                    mm.then_inc(summed, 1)

            @block.vector
            def _(dve):
                for r, (a, n, j) in enumerate(RANGES):
                    dve.wait_ge(rooted, before2 + r + 1)
                    dve.reciprocal(rstd[:, a:a + n], rstd[:, a:a + n]).then_inc(inverted, 1)
                dve.wait_ge(inverted, before2 + 2)
                for k in range(KD):
                    for a, n, j in RANGES:
                        dve.scalar_tensor_tensor(out=c.h[:, k, a:a + n], in0=c.x[:, k, a:a + n],
                                                 scalar=amp[:, k, j:j + 1], in1=rstd[:, a:a + n],
                                                 op0=ALU.mult, op1=ALU.mult).then_inc(scaled, 1)


def mla(c, layer, j):
    nc = c.nc
    with ExitStack() as st:
        def sb(name, shape):
            return st.enter_context(nc.sbuf_tensor("mla_" + name, shape, F32))

        m = {"consts": sb("consts", [P, _width(MLA_COLS)]), "cq": sb("cq", [P, 3, T]),
             "ckv": sb("ckv", [P, 2, KEYS]), "kpe": sb("kpe", [P, KEYS]), "full": None}
        m.update(_views(m["consts"], MLA_COLS))
        mla_project(c, m, j)
        mla_pairs(c, m, layer, j)


def mla_project(c, m, j):
    nc, ops, ps = c.nc, c.ops, c.ps
    W = QL + KVL + ROPE
    w_in = c.ring[:, 3 * SLOT:3 * SLOT + KD * W].rearrange("p (k n) -> p k n", k=KD)
    cq, ckv, kpe = m["cq"], m["ckv"], m["kpe"]
    with ExitStack() as st:
        sq = st.enter_context(nc.sbuf_tensor("mla_squares", [P, 5, T], F32))
        rq = st.enter_context(nc.sbuf_tensor("mla_rstd", [P, 2, T], F32))
        cache = st.enter_context(nc.sbuf_tensor("mla_cache_rows", [P, 3 * P], F32))
        w_kpe2 = st.enter_context(nc.sbuf_tensor("mla_w_kpe_twice", [P, KD, P], F32))
        rows = st.enter_context(nc.sbuf_tensor("mla_new_cache", [P, 3 * P], F32))
        rope = st.enter_context(nc.sbuf_tensor("mla_rope_parts", [P, 2, LAT], F32))
        loaded = c.w_in_full
        zero_s, zeros_out = sems(nc, st, "mlap", ["zero", "zeros_out"])
        zeros = st.enter_context(nc.sbuf_tensor("zero_rows", [P, D], F32))
        const_in, cache_in, done, act_s, dve_s, out_s, dup_s = sems(
            nc, st, "mlap", ["consts", "cache_in", "products", "act", "dve", "out", "dup"])
        prod = Steps(done, [f"z{b}" for b in range(6)] + ["cache", "sq", "skv", "swap", "rows"])
        act_n = Steps(act_s, [f"z{b}{r}" for b in range(6) for r in range(2)] + [f"s{b}" for b in range(5)]
                      + ["cacheT"] + [f"root{g}{r}" for g in range(2) for r in range(2)])
        dve_n = Steps(dve_s, ["cachepe"] + [f"inv{g}" for g in range(2)] + [f"n{b}{r}" for b in range(5) for r in range(2)]
                      + ["rc", "rs", "rot", "rows"])
        with nc.Block(no_gpsimd_drain=True) as block:
            @block.sync
            def _(sp):
                sp.dma_start(cache[:, 0:KVL + ROPE], ops["cache_mla"][0, j]).then_inc(cache_in, 16)
                sp.dma_start(cache[:, KVL + ROPE:3 * P], ops["cache_mla"][0, j, :, KVL:KVL + ROPE]).then_inc(cache_in, 16)
                sp.dma_start(m["consts"][:, :], ops["mla_consts"]).then_inc(const_in, 16)
                sp.wait_ge(zero_s, 1)
                for b in range(NBLK):
                    sp.dma_start(c.xs[b * P:(b + 1) * P, :], zeros[:, :]).then_inc(zeros_out, 16)
                for b in range(NE, NBLK):
                    sp.dma_start(c.ys[b * P:(b + 1) * P, :], zeros[:, :]).then_inc(zeros_out, 16)
                sp.wait_ge(zeros_out, 16 * (NBLK + NBLK - NE))
                sp.wait_ge(dve_n.sem, dve_n.value("rows"))
                sp.dma_start(ops["new_cache"][0, j], rows[:, 0:KVL + ROPE]).then_inc(out_s, 16)
                sp.wait_ge(out_s, 16)

            @block.tensor
            def _(pe):
                pe.wait_ge(loaded, 16)
                pe.wait_ge(dup_s, 2)
                for b in range(6):
                    if b >= 3:
                        pe.wait_ge(act_n.sem, act_n.value(f"z{b - 3}1"))
                    for r, (a, n, _) in enumerate(RANGES):
                        for k in range(KD):
                            lhs = w_in[:, k, b * P:(b + 1) * P] if b < 5 else w_kpe2[:, k, :]
                            mm = pe.matmul(ps[:, 2 * (b % 3) + r, 0:n], lhs, c.h[:, k, a:a + n],
                                           start=(k == 0), stop=(k == KD - 1))
                    mm.then_inc(done, 1)
                pe.wait_ge(cache_in, 32)
                for b in range(3):
                    mm = pe.transpose(ps[:, 6 + b // 2, (b % 2) * P:(b % 2 + 1) * P], cache[:, b * P:(b + 1) * P], c.base["ident"])
                mm.then_inc(done, 1)
                pe.wait_ge(act_n.sem, act_n.value("s4"))
                for g, blocks in ((0, (0, 1, 2)), (1, (3, 4))):
                    for r, (a, n, _) in enumerate(RANGES):
                        for b in blocks:
                            mm = pe.matmul(ps[:, 2 * g + r, 0:n], c.base["ones"], sq[:, b, a:a + n],
                                           start=(b == blocks[0]), stop=(b == blocks[-1]))
                    mm.then_inc(done, 1)
                pe.wait_ge(const_in, 16)
                pe.matmul(ps[:, 5, :], m["swap"], kpe[:, SEQ:T], start=True, stop=True).then_inc(done, 1)
                pe.wait_ge(dve_n.sem, dve_n.value("n41"))
                for b in range(2):
                    pe.transpose(ps[:, 7, b * P:(b + 1) * P], ckv[:, b, 0:P], c.base["ident"])
                pe.transpose(ps[:, 7, 2 * P:3 * P], kpe[:, 0:P], c.base["ident"]).then_inc(done, 1)

            @block.scalar
            def _(act):
                for b in range(6):
                    act.wait_ge(prod.sem, prod.value(f"z{b}"))
                    for r, (a, n, _) in enumerate(RANGES):
                        dst = cq[:, b] if b < 3 else ckv[:, b - 3] if b < 5 else kpe
                        nc.scalar.copy(dst[:, a:a + n], ps[:, 2 * (b % 3) + r, 0:n]).then_inc(act_s, 1)
                for b in range(5):
                    src = cq[:, b, :] if b < 3 else ckv[:, b - 3, 0:T]
                    act.wait_ge(act_n.sem, act_n.value("z51"))
                    nc.scalar.activation(sq[:, b, :], src, ACT.Square).then_inc(act_s, 1)
                act.wait_ge(prod.sem, prod.value("cache"))
                nc.scalar.copy(ckv[:, :, T:KEYS], ps[:, 6, 0:2 * P].rearrange("p (b n) -> p b n", b=2)).then_inc(act_s, 1)
                for g, width in ((0, QL), (1, KVL)):
                    act.wait_ge(prod.sem, prod.value("sq" if g == 0 else "skv"))
                    for r, (a, n, _) in enumerate(RANGES):
                        nc.scalar.activation(rq[:, g, a:a + n], ps[:, 2 * g + r, 0:n], ACT.Sqrt,
                                             bias=c.eps[:, :], scale=1.0 / width).then_inc(act_s, 1)

            @block.gpsimd
            def _(pool):
                pool.memset(zeros[:, :], 0.0).then_inc(zero_s, 1)

            @block.vector
            def _(dve):
                dve.wait_ge(loaded, 16)
                for i in range(2):
                    dve.tensor_copy(w_kpe2[:, :, i * ROPE:(i + 1) * ROPE], w_in[:, :, QL + KVL:W]).then_inc(dup_s, 1)
                dve.wait_ge(prod.sem, prod.value("cache"))
                dve.tensor_copy(kpe[:, T:KEYS], ps[:, 7, 0:P]).then_inc(dve_s, 1)
                for g in range(2):
                    dve.wait_ge(act_n.sem, act_n.value(f"root{g}1"))
                    dve.reciprocal(rq[:, g, :], rq[:, g, :]).then_inc(dve_s, 1)
                for b in range(5):
                    dve.wait_ge(dve_n.sem, dve_n.value(f"inv{b // 3}"))
                    for a, n, _ in RANGES:
                        t = cq[:, b, a:a + n] if b < 3 else ckv[:, b - 3, a:a + n]
                        dve.scalar_tensor_tensor(out=t, in0=t, scalar=c.cols_b[:, 24 + b:25 + b],
                                                 in1=rq[:, b // 3, a:a + n], op0=ALU.mult, op1=ALU.mult).then_inc(dve_s, 1)
                dve.wait_ge(const_in, 16)
                dve.wait_ge(act_n.sem, act_n.value("z51"))
                dve.tensor_tensor(rope[:, 0, :], kpe[:, SEQ:T], m["rcos"], ALU.mult).then_inc(dve_s, 1)
                dve.wait_ge(prod.sem, prod.value("swap"))
                dve.tensor_tensor(rope[:, 1, :], ps[:, 5, :], m["rsin"], ALU.mult).then_inc(dve_s, 1)
                dve.wait_ge(dve_n.sem, dve_n.value("rs"))
                dve.tensor_tensor(kpe[:, SEQ:T], rope[:, 0, :], rope[:, 1, :], ALU.add).then_inc(dve_s, 1)
                dve.wait_ge(prod.sem, prod.value("rows"))
                dve.tensor_copy(rows[:, :], ps[:, 7, 0:3 * P]).then_inc(dve_s, 1)


def mla_slots(c):
    wq = c.slot(0, 3 * 2 * UQ).rearrange("p (k n) -> p k n", k=3)
    wkv = c.slot(1, 2 * 512).rearrange("p (k h n) -> p k h n", k=2, h=2)
    wo = c.slot(2, 2 * D).rearrange("p (h n) -> p h n", h=2)
    return wq, wkv, wo


def load_mla_in(c, sp, j):
    W = QL + KVL + ROPE
    sp.dma_start(c.ring[:, 3 * SLOT:3 * SLOT + KD * W].rearrange("p (k n) -> p k n", k=KD),
                 c.ops["mla_w_in"][j].rearrange("(k p) n -> p k n", p=P)).then_inc(c.w_in_full, 16)


def load_mla_q(c, sp, j, i):
    wq = mla_slots(c)[0]
    src = c.ops["mla_w_uq"][j].rearrange("(k p) (g h n) -> g p k h n", p=P, h=2, n=UQ)
    for first, width, at in ((0, NOPE, 0), (NOPE, ROPE, 2 * NOPE)):
        for hd in range(2):
            sp.dma_start(wq[:, :, at + hd * width:at + (hd + 1) * width],
                         src[bass.ds(i, 1), :, :, hd, first:first + width].rearrange("a p k n -> (a p) k n"))\
              .then_inc(c.wq_full, 16)


def load_mla_kv(c, sp, j, i):
    sp.dma_start(c.slot(1, 2 * 512).rearrange("p (k n) -> p k n", k=2),
                 c.ops["mla_w_ukv"][j].rearrange("(k p) (g n) -> g p k n", p=P, n=512)[bass.ds(i, 1)]
                 .rearrange("a p k n -> (a p) k n")).then_inc(c.wkv_full, 16)


def load_mla_o(c, sp, j, i):
    sp.dma_start(mla_slots(c)[2], c.ops["mla_w_o"][j].rearrange("(g h p) n -> g p h n", p=P, h=2)[bass.ds(i, 1)]
                 .rearrange("a p h n -> (a p) h n")).then_inc(c.wo_full, 16)


def mla_pairs(c, m, layer, j):
    nc, ops, ps = c.nc, c.ops, c.ps
    cq, ckv, kpe = m["cq"], m["ckv"], m["kpe"]
    UNITS = [(hd, t) for hd in range(2) for t in range(NT)]
    NU = len(UNITS)
    order = ["q0", "q1", "qp", "qs", "k0", "k1", "v0", "v1", "v2", "S0", "S1"]
    for u in range(NU):
        order += ([f"S{u + 2}"] if u + 2 < NU else []) + [f"T{u}"] + (["O0"] if u == NT else [])
    order += ["O1"] + [f"w{d}" for d in range(KD)]
    bank = {n: 2 * (i % 4) for i, n in enumerate(order)}
    wq, wkv, wo = mla_slots(c)
    act_names = ["q00", "q01", "q10", "q11", "qp0", "qp1", "k0", "k1", "v0", "v1", "v2"]
    for u, (hd, t) in enumerate(UNITS):
        act_names += [f"e{u}"] + ([f"T{u - 1}"] if u else [])
    act_names += [f"T{NU - 1}"]
    dve_names = ["rc", "rs", "rot"]
    for u, (hd, t) in enumerate(UNITS):
        dve_names += [f"m{u}", f"b{u}"] + ([f"i{u - 1}", f"p{u - 1}"] if u else [])
        dve_names += [f"t{u - 1}"] if u and UNITS[u - 1][1] else []
        dve_names += ["o00", "o01"] if u == NT + 1 else []
    dve_names += [f"i{NU - 1}", f"p{NU - 1}", f"t{NU - 1}", "o10", "o11"] + [f"x{d}{r}" for d in range(KD) for r in range(2)]
    last = {"q0": ("a", "q01"), "q1": ("a", "q11"), "qp": ("a", "qp1"), "qs": ("v", "rs"), "k0": ("a", "k0"), "k1": ("a", "k1"),
            "v0": ("a", "v0"), "v1": ("a", "v1"), "v2": ("a", "v2"), "O0": ("v", "o01"), "O1": ("v", "o11")}
    last |= {f"S{u}": ("a", f"e{u}") for u in range(NU)}
    last |= {f"w{d}": ("v", f"x{d}1") for d in range(KD)}
    with ExitStack() as st:
        def sb(name, shape):
            return st.enter_context(nc.sbuf_tensor("mla_" + name, shape, F32))

        q, qpe, qraw = sb("q", [P, 2, T]), sb("qpe", [P, T]), sb("qraw", [P, LAT])
        rope = sb("qrope", [P, 2, LAT])
        k, v = sb("k", [P, 2, KEYS]), sb("v", [P, NKT, 2 * VD])
        prob = sb("prob", [P, 3, LKEYS])
        pt = c.h[:, :, :].rearrange("p k n -> p (k n)").rearrange("p (h x n) -> p h x n", h=2, x=5)
        ptc = sb("prob_t_ctx", [P, 2, P])
        o = sb("o", [P, 2, T])
        mx, bias, den, inv = (sb(n, [P, NU]) for n in ("max", "bias", "den", "inv"))
        fq, fkv, fo = c.wq_full, c.wkv_full, c.wo_full
        done, act_s, dve_s = sems(nc, st, "mla", ["products", "act", "dve"])
        prod = Steps(done, order)
        act_n, dve_n = Steps(act_s, act_names, 1), Steps(dve_s, dve_names, 1)
        by = {"a": act_n, "v": dve_n}
        gate = c.mod[:, layer, 16:24, :]
        with nc.Block(no_gpsimd_drain=True) as block:
            @block.sync
            def _(sp):
                with sp.Fori(0, PAIRS - 1) as i:
                    sp.wait_ge(prod.sem, prod.value("qp", i))
                    load_mla_q(c, sp, j, i + 1)
                    sp.wait_ge(prod.sem, prod.value("v2", i))
                    load_mla_kv(c, sp, j, i + 1)
                    sp.wait_ge(prod.sem, prod.value(f"w{KD - 1}", i))
                    load_mla_o(c, sp, j, i + 1)

            @block.tensor
            def _(pe):
                def two_ranges(name, mms, i):
                    for r, (a, n, _) in enumerate(RANGES):
                        for x, (lhs, rhs) in enumerate(mms):
                            mm = pe.matmul(ps[:, bank[name] + r, 0:n], lhs, rhs[:, a:a + n],
                                           start=(x == 0), stop=(x == len(mms) - 1))
                    mm.then_inc(done, 1)

                def free(name, i):
                    g = order.index(name) - 4
                    if g >= 0:
                        old = order[g]
                        if old[0] == "T":
                            u = int(old[1:])
                            pe.wait_ge(act_n.sem, act_n.value(f"T{u}", i))
                            if UNITS[u][1]:
                                pe.wait_ge(dve_n.sem, dve_n.value(f"t{u}", i))
                        else:
                            e, s = last[old]
                            pe.wait_ge(by[e].sem, by[e].value(s, i))

                def scores(u, i):
                    hd, t = UNITS[u]
                    free(f"S{u}", i)
                    b = bank[f"S{u}"]
                    half = slice(hd * ROPE, (hd + 1) * ROPE)
                    cols = slice(t * P, (t + 1) * P)
                    spans = [(0, SEQ)] if t == 0 else [(SEQ, LKEYS // 2), (SEQ + LKEYS // 2, LKEYS // 2)]
                    for r, (a, n) in enumerate(spans):
                        pe.matmul(ps[:, b + r, 0:n], q[:, hd, cols], k[:, hd, a:a + n], start=True, stop=False)
                        mm = pe.matmul(ps[:, b + r, 0:n], qpe[half, cols], kpe[half, a:a + n], start=False, stop=True)
                    mm.then_inc(done, 1)

                def turn(u, i):
                    hd, t = UNITS[u]
                    free(f"T{u}", i)
                    b = bank[f"T{u}"]
                    pe.wait_ge(dve_n.sem, dve_n.value(f"p{u}", i))
                    for x in range(1 if t == 0 else 5):
                        mm = pe.transpose(ps[:, b + x // 4, (x % 4) * P:(x % 4 + 1) * P],
                                          prob[:, u % 3, x * P:(x + 1) * P], c.base["ident"])
                    mm.then_inc(done, 1)

                def attend(hd, i):
                    free(f"O{hd}", i)
                    b, u = bank[f"O{hd}"], hd * NT + NT - 1
                    pe.wait_ge(act_n.sem, act_n.value(f"T{u}", i))
                    pe.wait_ge(dve_n.sem, dve_n.value(f"t{u}", i))
                    vh = slice(hd * VD, (hd + 1) * VD)
                    pe.matmul(ps[:, b, 0:P], v[:, 0, vh], ptc[:, hd, :], start=True, stop=True)
                    for x in range(5):
                        mm = pe.matmul(ps[:, b + 1, :], v[:, 1 + x, vh], pt[:, hd, x, :], start=(x == 0), stop=(x == 4))
                    mm.then_inc(done, 1)

                with pe.Fori(0, PAIRS) as i:
                    pe.wait_ge(fq, (i + 1) * 64)
                    pe.wait_ge(act_n.sem, act_n.before(i))
                    pe.wait_ge(dve_n.sem, dve_n.before(i))
                    for hd in range(2):
                        two_ranges(f"q{hd}", [(wq[:, b, hd * NOPE:(hd + 1) * NOPE], cq[:, b, :]) for b in range(3)], i)
                    two_ranges("qp", [(wq[:, b, 2 * NOPE:2 * UQ], cq[:, b, :]) for b in range(3)], i)
                    pe.wait_ge(act_n.sem, act_n.value("qp1", i))
                    pe.matmul(ps[:, bank["qs"], :], m["swap"], qraw[:, :], start=True, stop=True).then_inc(done, 1)
                    pe.wait_ge(fkv, (i + 1) * 16)
                    for hd in range(2):
                        free(f"k{hd}", i)
                        for r in range(2):
                            for b in range(2):
                                mm = pe.matmul(ps[:, bank[f"k{hd}"] + r, 0:KEYS // 2], wkv[:, b, hd, 0:NOPE],
                                               ckv[:, b, r * KEYS // 2:(r + 1) * KEYS // 2], start=(b == 0), stop=(b == 1))
                        mm.then_inc(done, 1)
                    for g in range(3):
                        free(f"v{g}", i)
                        for r in range(2):
                            t = 2 * g + r
                            for b in range(2):
                                mm = pe.matmul(ps[:, bank[f"v{g}"] + r, 0:2 * VD], ckv[:, b, t * P:(t + 1) * P],
                                               wkv[:, b, :, NOPE:2 * NOPE], start=(b == 0), stop=(b == 1))
                        mm.then_inc(done, 1)
                    pe.wait_ge(act_n.sem, act_n.value("k1", i))
                    pe.wait_ge(dve_n.sem, dve_n.value("rot", i))
                    scores(0, i)
                    scores(1, i)
                    for u in range(NU):
                        if u + 2 < NU:
                            scores(u + 2, i)
                        turn(u, i)
                        if u == NT:
                            attend(0, i)
                    attend(1, i)
                    pe.wait_ge(fo, (i + 1) * 16)
                    pe.wait_ge(dve_n.sem, dve_n.value("o11", i))
                    for d in range(KD):
                        free(f"w{d}", i)
                        two_ranges(f"w{d}", [(wo[:, hd, d * P:(d + 1) * P], o[:, hd, :]) for hd in range(2)], i)

            @block.scalar
            def _(act):
                def take_turned(u, i):
                    hd, t = UNITS[u]
                    act.wait_ge(prod.sem, prod.value(f"T{u}", i))
                    b = bank[f"T{u}"]
                    if t == 0:
                        nc.scalar.copy(ptc[:, hd, :], ps[:, b, 0:P]).then_inc(act_s, 1)
                    else:
                        nc.scalar.copy(pt[:, hd, 0:4, (t - 1) * P:t * P],
                                       ps[:, b, :].rearrange("p (x n) -> p x n", x=4)).then_inc(act_s, 1)

                act.sem_inc(act_s, 1)
                with act.Fori(0, PAIRS) as i:
                    for hd in range(2):
                        act.wait_ge(prod.sem, prod.value(f"q{hd}", i))
                        for r, (a, n, _) in enumerate(RANGES):
                            nc.scalar.copy(q[:, hd, a:a + n], ps[:, bank[f"q{hd}"] + r, 0:n]).then_inc(act_s, 1)
                    act.wait_ge(prod.sem, prod.value("qp", i))
                    nc.scalar.copy(qpe[:, 0:SEQ], ps[:, bank["qp"], 0:SEQ]).then_inc(act_s, 1)
                    nc.scalar.copy(qraw[:, :], ps[:, bank["qp"] + 1, :]).then_inc(act_s, 1)
                    for hd in range(2):
                        act.wait_ge(prod.sem, prod.value(f"k{hd}", i))
                        nc.scalar.copy(k[:, hd, :].rearrange("p (r n) -> p r n", r=2),
                                       ps[:, bank[f"k{hd}"]:bank[f"k{hd}"] + 2, 0:KEYS // 2]).then_inc(act_s, 1)
                    for g in range(3):
                        act.wait_ge(prod.sem, prod.value(f"v{g}", i))
                        nc.scalar.copy(v[:, 2 * g:2 * g + 2, :],
                                       ps[:, bank[f"v{g}"]:bank[f"v{g}"] + 2, 0:2 * VD]).then_inc(act_s, 1)
                    for u, (hd, t) in enumerate(UNITS):
                        b = bank[f"S{u}"]
                        act.wait_ge(dve_n.sem, dve_n.value(f"b{u}", i))
                        if u >= 3:
                            act.wait_ge(prod.sem, prod.value(f"T{u - 3}", i))
                        src = ps[:, b, 0:SEQ] if t == 0 else ps[:, b:b + 2, 0:LKEYS // 2]
                        dst = prob[:, u % 3, 0:SEQ] if t == 0 else prob[:, u % 3, :].rearrange("p (r n) -> p r n", r=2)
                        nc.scalar.activation(dst, src, ACT.Exp, bias=bias[:, u:u + 1], scale=MLA_SCALE,
                                             accum_out=den[:, u:u + 1]).then_inc(act_s, 1)
                        if u:
                            take_turned(u - 1, i)
                    take_turned(NU - 1, i)

            @block.vector
            def _(dve):
                def normalise(u, i):
                    hd, t = UNITS[u]
                    n = SEQ if t == 0 else LKEYS
                    dve.wait_ge(act_n.sem, act_n.value(f"e{u}", i))
                    dve.reciprocal(inv[:, u:u + 1], den[:, u:u + 1]).then_inc(dve_s, 1)
                    dve.wait_ge(dve_n.sem, dve_n.value(f"i{u}", i))
                    dve.tensor_scalar(prob[:, u % 3, 0:n], prob[:, u % 3, 0:n], inv[:, u:u + 1], None,
                                      ALU.mult).then_inc(dve_s, 1)

                def take_last(u, i):
                    hd, t = UNITS[u]
                    dve.wait_ge(prod.sem, prod.value(f"T{u}", i))
                    dve.tensor_copy(pt[:, hd, 4, (t - 1) * P:t * P], ps[:, bank[f"T{u}"] + 1, 0:P]).then_inc(dve_s, 1)

                def take_o(hd, i):
                    dve.wait_ge(prod.sem, prod.value(f"O{hd}", i))
                    for r, (a, n, _) in enumerate(RANGES):
                        dve.tensor_copy(o[:, hd, a:a + n], ps[:, bank[f"O{hd}"] + r, 0:n]).then_inc(dve_s, 1)

                dve.sem_inc(dve_s, 1)
                with dve.Fori(0, PAIRS) as i:
                    dve.wait_ge(act_n.sem, act_n.value("qp1", i))
                    dve.tensor_tensor(rope[:, 0, :], qraw[:, :], m["rcos"], ALU.mult).then_inc(dve_s, 1)
                    dve.wait_ge(prod.sem, prod.value("qs", i))
                    dve.tensor_tensor(rope[:, 1, :], ps[:, bank["qs"], :], m["rsin"], ALU.mult).then_inc(dve_s, 1)
                    dve.wait_ge(dve_n.sem, dve_n.value("rs", i))
                    dve.tensor_tensor(qpe[:, SEQ:T], rope[:, 0, :], rope[:, 1, :], ALU.add).then_inc(dve_s, 1)
                    for u, (hd, t) in enumerate(UNITS):
                        b = bank[f"S{u}"]
                        dve.wait_ge(prod.sem, prod.value(f"S{u}", i))
                        if t == 0:
                            dve.tensor_reduce(mx[:, u:u + 1], ps[:, b, 0:SEQ], AX.X, ALU.max).then_inc(dve_s, 1)
                        else:
                            dve.tensor_reduce(mx[:, u:u + 1], ps[:, b:b + 2, 0:LKEYS // 2], AX.XY, ALU.max).then_inc(dve_s, 1)
                        dve.wait_ge(dve_n.sem, dve_n.value(f"m{u}", i))
                        dve.tensor_scalar(bias[:, u:u + 1], mx[:, u:u + 1], -MLA_SCALE, None, ALU.mult).then_inc(dve_s, 1)
                        if u:
                            normalise(u - 1, i)
                            if UNITS[u - 1][1]:
                                take_last(u - 1, i)
                        if u == NT + 1:
                            take_o(0, i)
                    normalise(NU - 1, i)
                    take_last(NU - 1, i)
                    take_o(1, i)
                    for d in range(KD):
                        dve.wait_ge(prod.sem, prod.value(f"w{d}", i))
                        for r, (a, n, jc) in enumerate(RANGES):
                            dve.scalar_tensor_tensor(out=c.x[:, d, a:a + n], in0=ps[:, bank[f"w{d}"] + r, 0:n],
                                                     scalar=gate[:, d, jc:jc + 1], in1=c.x[:, d, a:a + n],
                                                     op0=ALU.mult, op1=ALU.add).then_inc(dve_s, 1)


def retention(c, layer, j):
    nc, ops, ps = c.nc, c.ops, c.ps
    order = ["q0", "q1", "k0", "k1", "v0", "v1", "v2", "kc", "fs", "bs"]
    order += ["f0", "f1", "f2", "b0", "b1", "b2", "sc", "s0", "s1", "s2", "s3"]
    order += [f"o{t}" for t in range(NT)] + [f"y{t}" for t in range(NT)] + [f"w{d}" for d in range(KD)]
    bank = {n: 2 * (i % 4) for i, n in enumerate(order)}
    last = {"q0": ("a", "q01"), "q1": ("a", "q11"), "k0": ("a", "k01"), "k1": ("a", "k11"),
            "kc": ("v", "kb"), "fs": ("v", "fs"), "bs": ("v", "bs"),
            "f0": ("a", "f0"), "f1": ("a", "f1"), "f2": ("a", "f2"), "b0": ("a", "b0"), "b1": ("a", "b1"), "b2": ("a", "b2"),
            "v0": ("v", "v0"), "v1": ("v", "v1"), "v2": ("v", "v2"), "sc": ("v", "scb")}
    last |= {f"s{x}": ("v", f"s{x}b") for x in range(4)}
    last |= {f"o{t}": ("v", f"o{t}b") for t in range(NT)}
    last |= {f"y{t}": ("a", f"y{t}") for t in range(NT)}
    last |= {f"w{d}": ("v", f"x{d}1") for d in range(KD)}
    act_names = ["df", "db", "kdf", "kdb", "ef", "q00", "q01", "q10", "q11", "k00", "k01", "k10", "k11",
                 "f0", "f1", "f2", "b0", "b1", "b2", "eb"]
    act_names += [f"o{t}{r}" for t in range(NT) for r in "fb"] + [f"y{t}" for t in range(NT)]
    dve_names = ["lg", "tf", "tb", "v0", "v1", "v2", "kf", "kb", "fs", "bs"]
    dve_names += [f"q{x}" for x in range(6)] + ["idxb", "qf0", "qf1", "scf", "scb"]
    dve_names += [f"s{x}{r}" for x in range(4) for r in "fb"] + ["qb0", "qb1"]
    for t in range(NT + 1):
        if t < NT:
            dve_names += [f"m{t}"]
        if t:
            dve_names += [f"o{t - 1}f", f"o{t - 1}b", f"y{t - 1}"]
    dve_names += [f"x{d}{r}" for d in range(KD) for r in range(2)]
    pool_names = [f"k{x}" for x in range(6)] + [f"r{t}" for t in range(NT)]
    with ExitStack() as st:
        def sb(name, shape):
            return st.enter_context(nc.sbuf_tensor("ret_" + name, shape, F32))

        consts = sb("consts", [P, _width(RET_COLS)])
        m = _views(consts, RET_COLS)
        s0 = c.ring[:, 5 * SLOT:5 * SLOT + 2048].rearrange("p (f b n) -> p f b n", f=2, b=2)
        trig = c.ring[:, 5 * SLOT + 2048:5 * SLOT + 2048 + 3 * LAT]
        m.update(_views(trig, TRIG_COLS))
        expo = c.ring[:, 5 * SLOT + 2048 + 3 * LAT:6 * SLOT]
        q, k = sb("q", [P, 2, T]), sb("k", [P, 2, T])
        v, gf, gb = (sb(n, [P, NT, DV]) for n in ("v", "gate_f", "gate_b"))
        yt = v[:, :, :].rearrange("p t n -> p (t n)").rearrange("p (b n) -> p b n", b=4)
        dec = sb("decay", [P, 2, LAT])
        kc = sb("k_ctx_rows", [P, 2, DK])
        ss = sb("scores", [P, 4, T])
        sctx = kc[:, :, 0:P]
        stage = sb("new_state", [P, 2, DV])
        qd = stage
        idxb = sb("index_b", [P, LAT])
        junk = idxb
        kd, lgs, lg = sb("k_decay", [P, 2]), sb("log_decays", [P, RH, 2]), sb("log_decay", [P, 2])
        raw, lt1, lt2 = (sb(n, [P, 2, RH]) for n in ("logits", "log_tmp1", "log_tmp2"))
        sumsq, mean, rs, half = sb("sumsq", [P, NT, 2]), sb("meansq", [P, NT, 2]), sb("rstd", [P, NT, 2]), sb("minus_half", [P, 2])
        tmp = ss[:, :, :].rearrange("p t n -> p (t n)")[:, 0:4 * LAT].rearrange("p (x n) -> p x n", x=4)
        full = sems(nc, st, "ret", [f"full{s}" for s in range(6)])
        const_in, logit_in, prep, dprep, done, act_s, dve_s, pool_s, store_s = sems(
            nc, st, "ret", ["consts", "logits", "prep", "dve_prep", "products", "act", "dve", "pool", "stored"])
        prod, act_n, dve_n, pool_n = Steps(done, order), Steps(act_s, act_names, 1), Steps(dve_s, dve_names, 1), Steps(pool_s, pool_names)
        by = {"a": act_n, "v": dve_n}
        gate = c.mod[:, layer, 16:24, :]
        W0 = {"q": 0, "k": RH * DK, "v": 2 * RH * DK, "f": 2 * RH * DK + RH * DV, "b": 2 * RH * DK + 2 * RH * DV}
        w3 = ops["ret_w_in"][j].rearrange("(k p) n -> p k n", p=P)
        wqk, wv, wf, wb = (c.slot(s).rearrange("p (k n) -> p k n", k=KD) for s in range(4))
        wo = c.slot(4).rearrange("p (b n) -> p b n", b=4)
        with nc.Block(no_gpsimd_drain=True) as block:
            @block.sync
            def _(sp):
                sp.dma_start(raw[:, 0, :], ops["ret_decay_f"].broadcast_to([P, RH])).then_inc(logit_in, 16)
                sp.dma_start(raw[:, 1, :], ops["ret_decay_b"].broadcast_to([P, RH])).then_inc(logit_in, 16)
                sp.dma_start(consts[:, :], ops["ret_consts"]).then_inc(const_in, 16)
                sp.dma_start(trig, ops["trig_consts"]).then_inc(const_in, 16)

                def columns(first, width, i):
                    return w3[:, :, bass.ds(i * width + first, width)]

                def load_in(s, i):
                    if s == 0:
                        sp.dma_start(wqk[:, :, 0:DK], columns(W0["q"], DK, i)).then_inc(full[0], 16)
                        sp.dma_start(wqk[:, :, DK:2 * DK], columns(W0["k"], DK, i)).then_inc(full[0], 16)
                    else:
                        sp.dma_start((wqk, wv, wf, wb)[s], columns(W0["qvfb"[s]], DV, i)).then_inc(full[s], 16)

                def load_state(i):
                    src = ops["state_ret"][0, j].rearrange("f h (b p) n -> h f b p n", p=P)
                    for f in range(2):
                        for b in range(2):
                            sp.dma_start(s0[:, f, b, :], src[bass.ds(i, 1), f, b].rearrange("a p n -> (a p) n")).then_inc(full[5], 16)

                def load_out(i):
                    sp.dma_start(wo, ops["ret_w_o"][j].rearrange("(h b p) n -> h p b n", p=P, b=4)[bass.ds(i, 1)]
                                 .rearrange("a p b n -> (a p) b n")).then_inc(full[4], 16)

                def store_state(f, i):
                    sp.wait_ge(dve_n.sem, dve_n.value(("fs", "bs")[f], i))
                    dst = ops["new_state"][0, j, f].rearrange("h (b p) n -> h p b n", p=P)
                    sp.dma_start(dst[bass.ds(i, 1)].rearrange("a p b n -> (a p) b n"), stage[:, :, :]).then_inc(store_s, 16)

                sp.sem_inc(store_s, 16)
                for s in range(4):
                    load_in(s, 0)
                load_state(0)
                load_out(0)
                with sp.Fori(0, RH - 1) as i:
                    for s, n in enumerate(("k1", "v2")):
                        sp.wait_ge(prod.sem, prod.value(n, i))
                        load_in(s, i + 1)
                    store_state(0, i)
                    store_state(1, i)
                    for s, n in enumerate(("f2", "b2")):
                        sp.wait_ge(prod.sem, prod.value(n, i))
                        load_in(s + 2, i + 1)
                    sp.wait_ge(prod.sem, prod.value(f"o{NT - 1}", i))
                    load_state(i + 1)
                    sp.wait_ge(prod.sem, prod.value(f"w{KD - 1}", i))
                    load_out(i + 1)
                store_state(0, RH - 1)
                store_state(1, RH - 1)
                sp.wait_ge(store_s, RH * 32 + 16)

            @block.gpsimd
            def _(pool):
                pool.memset(half[:, :], -0.5).then_inc(prep, 1)
                with pool.Fori(0, RH) as i:
                    pool.wait_ge(const_in, 32)
                    pool.wait_ge(act_n.sem, act_n.value("k11", i))
                    k1, k2 = k[:, 0, SEQ:T], k[:, 1, SEQ:T]
                    pool.tensor_tensor(tmp[:, 0, :], k1, m["sin"], ALU.mult).then_inc(pool_s, 1)
                    pool.tensor_tensor(tmp[:, 1, :], k2, m["sin"], ALU.mult).then_inc(pool_s, 1)
                    pool.wait_ge(pool_n.sem, pool_n.value("k1", i))
                    pool.tensor_tensor(k1, k1, m["cos"], ALU.mult).then_inc(pool_s, 1)
                    pool.tensor_tensor(k2, k2, m["cos"], ALU.mult).then_inc(pool_s, 1)
                    pool.wait_ge(pool_n.sem, pool_n.value("k3", i))
                    pool.tensor_tensor(k1, k1, tmp[:, 1, :], ALU.subtract).then_inc(pool_s, 1)
                    pool.tensor_tensor(k2, k2, tmp[:, 0, :], ALU.add).then_inc(pool_s, 1)
                    for t in range(NT):
                        pool.wait_ge(prep, 1)
                        pool.wait_ge(dve_n.sem, dve_n.value(f"m{t}", i))
                        pool.tensor_tensor(rs[:, t, :], mean[:, t, :], half[:, :], ALU.pow).then_inc(pool_s, 1)

            @block.tensor
            def _(pe):
                def free(name, i):
                    g = order.index(name) - 4
                    if g >= 0:
                        e, s = last[order[g]]
                        pe.wait_ge(by[e].sem, by[e].value(s, i))

                def two_ranges(name, mms, i):
                    free(name, i)
                    for r, (a, n, _) in enumerate(RANGES):
                        for x, (lhs, rhs) in enumerate(mms):
                            mm = pe.matmul(ps[:, bank[name] + r, 0:n], lhs, rhs[:, a:a + n],
                                           start=(x == 0), stop=(x == len(mms) - 1))
                    mm.then_inc(done, 1)

                def rows_of(name, w, i):
                    for g in range(3):
                        free(f"{name}{g}", i)
                        for r in range(2):
                            t = 2 * g + r
                            if t < NT:
                                for b in range(KD):
                                    mm = pe.matmul(ps[:, bank[f"{name}{g}"] + r, :], c.h[:, b, t * P:(t + 1) * P],
                                                   w[:, b, :], start=(b == 0), stop=(b == KD - 1))
                        mm.then_inc(done, 1)

                with pe.Fori(0, RH) as i:
                    pe.wait_ge(full[0], (i + 1) * 32)
                    pe.wait_ge(act_n.sem, act_n.before(i))
                    pe.wait_ge(dve_n.sem, dve_n.before(i))
                    for x, n in enumerate(("q0", "q1", "k0", "k1")):
                        two_ranges(n, [(wqk[:, b, x * P:(x + 1) * P], c.h[:, b, :]) for b in range(KD)], i)
                    pe.wait_ge(full[1], (i + 1) * 16)
                    rows_of("v", wv, i)
                    free("kc", i)
                    pe.wait_ge(act_n.sem, act_n.value("k11", i))
                    for b in range(2):
                        mm = pe.transpose(ps[:, bank["kc"], b * P:(b + 1) * P], k[:, b, 0:P], c.base["ident"])
                    mm.then_inc(done, 1)
                    pe.wait_ge(dve_n.sem, dve_n.value("kb", i))
                    for f, n in enumerate(("fs", "bs")):
                        free(n, i)
                        for b in range(2):
                            mm = pe.matmul(ps[:, bank[n] + b, :], kc[:, f, b * P:(b + 1) * P], v[:, 0, :], start=True, stop=True)
                        mm.then_inc(done, 1)
                    pe.wait_ge(full[2], (i + 1) * 16)
                    rows_of("f", wf, i)
                    pe.wait_ge(full[3], (i + 1) * 16)
                    rows_of("b", wb, i)
                    free("sc", i)
                    for b in range(2):
                        mm = pe.matmul(ps[:, bank["sc"], 0:P], k[:, b, 0:P], q[:, b, 0:P], start=(b == 0), stop=(b == 1))
                    mm.then_inc(done, 1)
                    pe.wait_ge(pool_n.sem, pool_n.value("k5", i))
                    pe.wait_ge(dve_n.sem, dve_n.value("q5", i))
                    for x in range(4):
                        free(f"s{x}", i)
                        for b in range(2):
                            mm = pe.matmul(ps[:, bank[f"s{x}"], :], k[:, b, SEQ + x * P:SEQ + (x + 1) * P], q[:, b, SEQ:T],
                                           start=(b == 0), stop=(b == 1))
                        mm.then_inc(done, 1)
                    pe.wait_ge(full[5], (i + 1) * 64)
                    pe.wait_ge(dve_n.sem, dve_n.value("qb1", i))
                    for t in range(NT):
                        free(f"o{t}", i)
                        for f in range(2):
                            out = ps[:, bank[f"o{t}"] + f, :]
                            if t == 0:
                                mm = pe.matmul(out, sctx[:, f, :], v[:, 0, :], start=True, stop=True)
                                continue
                            n = t - 1
                            mms = [(ss[:, x, (n + 1 - f) * P:(n + 2 - f) * P], v[:, 1 + x, :])
                                   for x in (range(n + 1) if f == 0 else range(n, 4))]
                            qq = qd if f == 0 else q[:, :, SEQ:T]
                            mms += [(qq[:, b, n * P:(n + 1) * P], s0[:, f, b, :]) for b in range(2)]
                            for x, (lhs, rhs) in enumerate(mms):
                                mm = pe.matmul(out, lhs, rhs, start=(x == 0), stop=(x == len(mms) - 1))
                        mm.then_inc(done, 1)
                    for t in range(NT):
                        free(f"y{t}", i)
                        pe.wait_ge(dve_n.sem, dve_n.value(f"y{t}", i))
                        for b in range(4):
                            mm = pe.transpose(ps[:, bank[f"y{t}"], b * P:(b + 1) * P], gf[:, t, b * P:(b + 1) * P], c.base["ident"])
                        mm.then_inc(done, 1)
                    pe.wait_ge(full[4], (i + 1) * 16)
                    pe.wait_ge(act_n.sem, act_n.value(f"y{NT - 1}", i))
                    for d in range(KD):
                        two_ranges(f"w{d}", [(wo[:, b, d * P:(d + 1) * P], yt[:, b, :]) for b in range(4)], i)

            @block.scalar
            def _(act):
                act.wait_ge(prep, 2)
                nc.scalar.activation(lt1[:, :, :], lt1[:, :, :], ACT.Exp, scale=-1.0).then_inc(prep, 1)
                act.wait_ge(prep, 3)
                nc.scalar.activation(lt1[:, :, :], lt1[:, :, :], ACT.Ln, bias=1.0).then_inc(prep, 1)
                act.wait_ge(const_in, 32)
                act.sem_inc(act_s, 1)
                with act.Fori(0, RH) as i:
                    act.wait_ge(dve_n.sem, dve_n.value("lg", i))
                    nc.scalar.activation(dec[:, 0, :], m["relf"], ACT.Exp, scale=lg[:, 0:1]).then_inc(act_s, 1)
                    nc.scalar.activation(dec[:, 1, :], m["relb"], ACT.Exp, scale=lg[:, 1:2]).then_inc(act_s, 1)
                    nc.scalar.activation(kd[:, 0:1], m["kf"], ACT.Exp, scale=lg[:, 0:1]).then_inc(act_s, 1)
                    nc.scalar.activation(kd[:, 1:2], m["kb"], ACT.Exp, scale=lg[:, 1:2]).then_inc(act_s, 1)
                    nc.scalar.activation(expo, m["idxf"], ACT.Exp, scale=lg[:, 0:1]).then_inc(act_s, 1)
                    for x, n in enumerate(("q0", "q1", "k0", "k1")):
                        act.wait_ge(prod.sem, prod.value(n, i))
                        for r, (a, w, _) in enumerate(RANGES):
                            nc.scalar.activation((q, k)[x // 2][:, x % 2, a:a + w], ps[:, bank[n] + r, 0:w], ACT.Identity,
                                                 scale=1.0 if x < 2 else KSCALE).then_inc(act_s, 1)
                    for f, g in (("f", gf), ("b", gb)):
                        for x in range(3):
                            act.wait_ge(prod.sem, prod.value(f"{f}{x}", i))
                            w = 2 if x < 2 else 1
                            nc.scalar.activation(g[:, 2 * x:2 * x + w, :], ps[:, bank[f"{f}{x}"]:bank[f"{f}{x}"] + w, :],
                                                 ACT.Silu).then_inc(act_s, 1)
                    act.wait_ge(dve_n.sem, dve_n.value("qf1", i))
                    nc.scalar.activation(expo, idxb[:, :], ACT.Exp, scale=lg[:, 1:2]).then_inc(act_s, 1)
                    for t in range(NT):
                        act.wait_ge(prod.sem, prod.value(f"o{t}", i))
                        for f in range(2):
                            act.wait_ge(act_n.sem, act_n.value(f"o{t}f", i) - 1 + f)
                            nc.scalar.activation(junk[:, :], ps[:, bank[f"o{t}"] + f, :], ACT.Square,
                                                 accum_out=sumsq[:, t, f:f + 1]).then_inc(act_s, 1)
                    for t in range(NT):
                        act.wait_ge(prod.sem, prod.value(f"y{t}", i))
                        nc.scalar.copy(yt[:, :, t * P:(t + 1) * P],
                                       ps[:, bank[f"y{t}"], :].rearrange("p (b n) -> p b n", b=4)).then_inc(act_s, 1)

            @block.vector
            def _(dve):
                dve.wait_ge(logit_in, 32)
                dve.wait_ge(prep, 1)
                dve.tensor_scalar(lt2[:, :, :], raw[:, :, :], -1.0, None, ALU.mult).then_inc(dprep, 1)
                dve.wait_ge(dprep, 1)
                dve.tensor_tensor(lt1[:, :, :], raw[:, :, :], lt2[:, :, :], ALU.max).then_inc(prep, 1)
                dve.wait_ge(prep, 2)
                dve.tensor_scalar(lt2[:, :, :], raw[:, :, :], 0.0, None, ALU.min).then_inc(dprep, 1)
                dve.wait_ge(dprep, 2)
                dve.wait_ge(prep, 4)
                dve.tensor_tensor(lgs[:, :, :].rearrange("p h f -> p f h"), lt2[:, :, :], lt1[:, :, :], ALU.subtract).then_inc(dprep, 1)
                dve.wait_ge(dprep, 3)
                dve.wait_ge(const_in, 32)
                dve.sem_inc(dve_s, 1)
                with dve.Fori(0, RH) as i:
                    dve.wait_ge(act_n.sem, act_n.before(i))
                    dve.tensor_copy(lg[:, :], lgs[:, bass.ds(i, 1), :].rearrange("p a f -> p (a f)")).then_inc(dve_s, 1)
                    dve.wait_ge(act_n.sem, act_n.value("db", i))
                    dve.tensor_tensor(dec[:, 0, 0:P], dec[:, 0, 0:P], m["trif"], ALU.mult).then_inc(dve_s, 1)
                    dve.tensor_tensor(dec[:, 1, LAT - P:LAT], dec[:, 1, LAT - P:LAT], m["trib"], ALU.mult).then_inc(dve_s, 1)
                    for x in range(3):
                        dve.wait_ge(prod.sem, prod.value(f"v{x}", i))
                        w = 2 if x < 2 else 1
                        dve.tensor_copy(v[:, 2 * x:2 * x + w, :], ps[:, bank[f"v{x}"]:bank[f"v{x}"] + w, :]).then_inc(dve_s, 1)
                    dve.wait_ge(prod.sem, prod.value("kc", i))
                    dve.wait_ge(act_n.sem, act_n.value("kdb", i))
                    for f in range(2):
                        dve.tensor_scalar(kc[:, f, :], ps[:, bank["kc"], 0:DK], kd[:, f:f + 1], None, ALU.mult).then_inc(dve_s, 1)
                    for f, n in enumerate(("fs", "bs")):
                        dve.wait_ge(prod.sem, prod.value(n, i))
                        dve.wait_ge(store_s, i * 32 + 16 * (f + 1))
                        dve.tensor_copy(stage[:, :, :], ps[:, bank[n]:bank[n] + 2, :]).then_inc(dve_s, 1)
                    q1, q2 = q[:, 0, SEQ:T], q[:, 1, SEQ:T]
                    dve.wait_ge(act_n.sem, act_n.value("q11", i))
                    dve.tensor_tensor(tmp[:, 2, :], q1, m["sin"], ALU.mult).then_inc(dve_s, 1)
                    dve.tensor_tensor(tmp[:, 3, :], q2, m["sin"], ALU.mult).then_inc(dve_s, 1)
                    dve.wait_ge(dve_n.sem, dve_n.value("q1", i))
                    dve.tensor_tensor(q1, q1, m["cos"], ALU.mult).then_inc(dve_s, 1)
                    dve.tensor_tensor(q2, q2, m["cos"], ALU.mult).then_inc(dve_s, 1)
                    dve.wait_ge(dve_n.sem, dve_n.value("q3", i))
                    dve.tensor_tensor(q1, q1, tmp[:, 3, :], ALU.subtract).then_inc(dve_s, 1)
                    dve.tensor_tensor(q2, q2, tmp[:, 2, :], ALU.add).then_inc(dve_s, 1)
                    dve.tensor_scalar(idxb[:, :], m["idxf"], -1.0, float(LAT + 1), ALU.mult, ALU.add).then_inc(dve_s, 1)
                    dve.wait_ge(dve_n.sem, dve_n.value("q5", i))
                    dve.wait_ge(store_s, i * 32 + 48)
                    for b in range(2):
                        dve.tensor_tensor(qd[:, b, :], q[:, b, SEQ:T], expo, ALU.mult).then_inc(dve_s, 1)
                    dve.wait_ge(prod.sem, prod.value("sc", i))
                    dve.wait_ge(dve_n.sem, dve_n.value("tb", i))
                    dve.tensor_tensor(sctx[:, 0, :], ps[:, bank["sc"], 0:P], dec[:, 0, 0:P], ALU.mult).then_inc(dve_s, 1)
                    dve.tensor_tensor(sctx[:, 1, :], ps[:, bank["sc"], 0:P], dec[:, 1, LAT - P:LAT], ALU.mult).then_inc(dve_s, 1)
                    for x in range(4):
                        dve.wait_ge(prod.sem, prod.value(f"s{x}", i))
                        s = ps[:, bank[f"s{x}"], :]
                        dve.tensor_tensor(ss[:, x, (x + 1) * P:T], s[:, x * P:LAT], dec[:, 0, 0:LAT - x * P], ALU.mult).then_inc(dve_s, 1)
                        dve.tensor_tensor(ss[:, x, 0:(x + 1) * P], s[:, 0:(x + 1) * P], dec[:, 1, LAT - (x + 1) * P:LAT],
                                          ALU.mult).then_inc(dve_s, 1)
                    dve.wait_ge(act_n.sem, act_n.value("eb", i))
                    for b in range(2):
                        dve.tensor_tensor(q[:, b, SEQ:T], q[:, b, SEQ:T], expo, ALU.mult).then_inc(dve_s, 1)
                    for t in range(NT + 1):
                        if t < NT:
                            dve.wait_ge(act_n.sem, act_n.value(f"o{t}b", i))
                            dve.tensor_scalar(mean[:, t, :], sumsq[:, t, :], 1.0 / DV, EPS, ALU.mult, ALU.add).then_inc(dve_s, 1)
                        if t:
                            n = t - 1
                            dve.wait_ge(pool_n.sem, pool_n.value(f"r{n}", i))
                            for f, g in enumerate((gf, gb)):
                                dve.scalar_tensor_tensor(out=g[:, n, :], in0=ps[:, bank[f"o{n}"] + f, :], scalar=rs[:, n, f:f + 1],
                                                         in1=g[:, n, :], op0=ALU.mult, op1=ALU.mult).then_inc(dve_s, 1)
                            dve.wait_ge(dve_n.sem, dve_n.value(f"o{n}b", i))
                            dve.tensor_tensor(gf[:, n, :], gf[:, n, :], gb[:, n, :], ALU.add).then_inc(dve_s, 1)
                    for d in range(KD):
                        dve.wait_ge(prod.sem, prod.value(f"w{d}", i))
                        for r, (a, n, jc) in enumerate(RANGES):
                            dve.scalar_tensor_tensor(out=c.x[:, d, a:a + n], in0=ps[:, bank[f"w{d}"] + r, 0:n],
                                                     scalar=gate[:, d, jc:jc + 1], in1=c.x[:, d, a:a + n],
                                                     op0=ALU.mult, op1=ALU.add).then_inc(dve_s, 1)


def route(c, layer):
    nc, ps = c.nc, c.ps
    G = NT * NG
    with ExitStack() as st:
        def sb(name, shape, dt=F32):
            return st.enter_context(nc.sbuf_tensor(f"route{layer}_" + name, shape, dt))

        rows = sb("rows", [P, NT, D])
        s, gr, msk, o1, o2, on, tmp, past = (sb(n, [P, NT, NE]) for n in
                                             ("scores", "biased", "masked", "one1", "one2", "both", "tmp", "past"))
        pair, keep, off = sb("pair", [P, 2, G]), sb("keep", [P, NT, NG]), sb("off", [P, NT, NG])
        top = sb("top", [P, NT])
        wsum, dst = sb("wsum", [P, NT]), sb("dst", [P, 2, NT])
        nb, cs, start, down = sb("more_blocks", [P, NE]), sb("cumulated", [P, 2, NE]), sb("start", [P, NE]), sb("countdown", [P, NE])
        cmp, eb, tn = sb("compare", [P, NBLK - NE, NE]), sb("block_e", [P, NBLK]), sb("turns", [P, 2])
        logits, ranks, turned, taken, expd, chain, scattered = sems(
            nc, st, f"route{layer}", ["logits", "ranks", "turned", "taken", "exp", "chain", "scattered"])
        with nc.Block(no_gpsimd_drain=True) as block:
            mark = {}

            @block.vector
            def _(dve):
                n = 0

                def link(ins):
                    nonlocal n
                    n += 1
                    ins.then_inc(chain, 1)
                    dve.wait_ge(chain, n)

                def over(x, n=NE):
                    return x.unsqueeze(2).to_broadcast([P, NT, n])

                def tiles(x, n=NE):
                    return x.unsqueeze(1).to_broadcast([P, NT, n])

                def first_best(one, values, n):
                    link(dve.tensor_reduce(top[:, :], values, AX.X, ALU.max))
                    link(dve.tensor_tensor(one, values, over(top[:, :], n), ALU.is_equal))
                    link(dve.tensor_tensor(one, one, tiles(down[:, NE - n:NE], n), ALU.mult))
                    link(dve.tensor_reduce(top[:, :], one, AX.X, ALU.max))
                    link(dve.tensor_tensor(one, one, over(top[:, :], n), ALU.is_equal))

                link(dve.tensor_scalar(down[:, :], c.base["iota16"], -1.0, float(NE), ALU.mult, ALU.add))
                dve.wait_ge(expd, 1)
                link(dve.tensor_scalar(s[:, :, :], s[:, :, :], 1.0, None, ALU.add))
                link(dve.reciprocal(s[:, :, :], s[:, :, :]))
                link(dve.tensor_tensor(gr[:, :, :], s[:, :, :], tiles(c.router_b[:, :]), ALU.add))
                m = gr[:, :, :].rearrange("p t (g e) -> p (t g) e", e=EG)
                link(dve.tensor_tensor(pair[:, 0, :], m[:, :, 0], m[:, :, 1], ALU.add))
                for a in range(EG):
                    for b in range(max(a + 1, 2), EG):
                        link(dve.tensor_tensor(pair[:, 1, :], m[:, :, a], m[:, :, b], ALU.add))
                        link(dve.tensor_tensor(pair[:, 0, :], pair[:, 0, :], pair[:, 1, :], ALU.max))
                first_best(keep[:, :, :], pair[:, 0, :].rearrange("p (t g) -> p t g", t=NT), NG)
                link(dve.tensor_scalar(off[:, :, :], keep[:, :, :], -1.0, BIG, ALU.add, ALU.mult))
                for x, op in ((keep, ALU.mult), (off, ALU.add)):
                    link(dve.tensor_tensor(msk[:, :, :].rearrange("p t (g e) -> p (t g) e", e=EG), m if x is keep else
                                           msk[:, :, :].rearrange("p t (g e) -> p (t g) e", e=EG),
                                           x[:, :, :].rearrange("p t g -> p (t g)").unsqueeze(2).to_broadcast([P, G, EG]), op))
                first_best(o1[:, :, :], msk[:, :, :], NE)
                link(dve.scalar_tensor_tensor(out=msk[:, :, :], in0=o1[:, :, :], scalar=-BIG, in1=msk[:, :, :],
                                              op0=ALU.mult, op1=ALU.add))
                first_best(o2[:, :, :], msk[:, :, :], NE)
                link(dve.tensor_tensor(on[:, :, :], o1[:, :, :], o2[:, :, :], ALU.add))
                mark["onehot"] = n
                for k, o in enumerate((o1, o2)):
                    link(dve.tensor_tensor(tmp[:, :, :], o[:, :, :], s[:, :, :], ALU.mult))
                    link(dve.tensor_reduce(c.w12[:, k, :], tmp[:, :, :], AX.X, ALU.add))
                link(dve.tensor_tensor(wsum[:, :], c.w12[:, 0, :], c.w12[:, 1, :], ALU.add))
                link(dve.reciprocal(wsum[:, :], wsum[:, :]))
                for k in range(2):
                    link(dve.tensor_tensor(c.w12[:, k, :], c.w12[:, k, :], wsum[:, :], ALU.mult))
                dve.wait_ge(ranks, 1)
                count = ps[:, 1, NT * NE:(NT + 1) * NE]
                link(dve.tensor_scalar(nb[:, :], count, float(P), None, ALU.is_gt))
                for b in range(2, NT):
                    link(dve.scalar_tensor_tensor(out=nb[:, :], in0=count, scalar=float(b * P), in1=nb[:, :],
                                                  op0=ALU.is_gt, op1=ALU.add))
                link(dve.tensor_copy(cs[:, 0, :], nb[:, :]))
                a = 0
                for sh in (1, 2, 4, 8):
                    link(dve.tensor_copy(cs[:, 1 - a, 0:sh], cs[:, a, 0:sh]))
                    link(dve.tensor_tensor(cs[:, 1 - a, sh:NE], cs[:, a, sh:NE], cs[:, a, 0:NE - sh], ALU.add))
                    a = 1 - a
                link(dve.tensor_tensor(start[:, :], cs[:, a, :], nb[:, :], ALU.subtract))
                link(dve.tensor_tensor(start[:, :], start[:, :], c.base["iota16"], ALU.subtract))
                link(dve.tensor_scalar(start[:, :], start[:, :], float(NE - 1), float(P), ALU.add, ALU.mult))
                rank = ps[:, 1, 0:NT * NE].rearrange("p (t e) -> p t e", t=NT)
                link(dve.tensor_scalar(past[:, :, :], rank, float(P), None, ALU.is_ge))
                link(dve.tensor_tensor(past[:, :, :], past[:, :, :], tiles(start[:, :]), ALU.mult))
                link(dve.tensor_tensor(tmp[:, :, :], past[:, :, :], rank, ALU.add))
                link(dve.scalar_tensor_tensor(out=tmp[:, :, :], in0=tiles(c.base["iota16"]), scalar=float(P), in1=tmp[:, :, :],
                                              op0=ALU.mult, op1=ALU.add))
                for k, o in enumerate((o1, o2)):
                    link(dve.tensor_tensor(o[:, :, :], o[:, :, :], tmp[:, :, :], ALU.mult))
                    link(dve.tensor_reduce(dst[:, k, :], o[:, :, :], AX.X, ALU.add))
                link(dve.tensor_copy(c.dest[:, :, :], dst[:, :, :]))
                mark["dest"] = n
                link(dve.tensor_tensor(cmp[:, :, :], cs[:, a, :].unsqueeze(1).to_broadcast([P, NBLK - NE, NE]),
                                       c.base["iotab"][:, 0:NBLK - NE].unsqueeze(2).to_broadcast([P, NBLK - NE, NE]), ALU.is_le))
                link(dve.tensor_copy(eb[:, 0:NE], c.base["iota16"]))
                link(dve.tensor_reduce(eb[:, NE:NBLK], cmp[:, :, :], AX.X, ALU.add))
                link(dve.tensor_scalar(c.blk_e[:, :], eb[:, :], float(NE - 1), None, ALU.min))
                link(dve.tensor_scalar(cmp[:, :, 0], c.base["iotab"][:, 0:NBLK - NE], 2.0, None, ALU.mult))
                link(dve.tensor_tensor(cmp[:, :, 1], cmp[:, :, 0], cs[:, a, NE - 1:NE].to_broadcast([P, NBLK - NE]), ALU.is_lt))
                link(dve.tensor_reduce(tn[:, 0:1], cmp[:, :, 1], AX.X, ALU.add))
                for less in range(3):
                    link(dve.tensor_scalar(c.turns[:, less:less + 1], tn[:, 0:1], float(NE // 2 - less), None, ALU.add))

            @block.tensor
            def _(pe):
                for t in range(NT):
                    for k in range(KD):
                        mm = pe.matmul(ps[:, 0, t * NE:(t + 1) * NE], c.h[:, k, t * P:(t + 1) * P], c.router[:, k, :],
                                       start=(k == 0), stop=(k == KD - 1))
                mm.then_inc(logits, 1)
                for g in range(2 * NT):
                    if g >= 4:
                        pe.wait_ge(taken, g - 3)
                    for k in range(4):
                        mm = pe.transpose(ps[:, 2 + g % 4, k * P:(k + 1) * P],
                                          c.h[:, 4 * (g % 2) + k, (g // 2) * P:(g // 2 + 1) * P], c.base["ident"])
                    mm.then_inc(turned, 1)
                pe.wait_ge(chain, mark["onehot"])
                for t in range(NT + 1):
                    for u in range(min(t + 1, NT)):
                        mm = pe.matmul(ps[:, 1, t * NE:(t + 1) * NE], c.base["before"] if u == t else c.base["ones"],
                                       on[:, u, :], start=(u == 0), stop=(u == min(t, NT - 1)))
                mm.then_inc(ranks, 1)

            @block.scalar
            def _(act):
                act.wait_ge(logits, 1)
                nc.scalar.activation(s[:, :, :], ps[:, 0, 0:NT * NE].rearrange("p (t e) -> p t e", t=NT), ACT.Exp,
                                     scale=-1.0).then_inc(expd, 1)
                for g in range(2 * NT):
                    act.wait_ge(turned, g + 1)
                    nc.scalar.copy(rows[:, g // 2, 512 * (g % 2):512 * (g % 2 + 1)], ps[:, 2 + g % 4, :]).then_inc(taken, 1)

            @block.gpsimd
            def _(pool):
                pool.wait_ge(chain, mark["dest"])
                for t in range(NT):
                    pool.wait_ge(taken, 2 * t + 2)
                    for k in range(TOPK):
                        pool.indirect_dma_start(c.xs, bass.IndirectOffsetOnAxis(c.dest[:, k, t:t + 1], 0),
                                                rows[:, t, :], None).then_inc(scattered, 16)
                pool.wait_ge(scattered, 16 * NT * TOPK)


def expert_slots(c):
    return [[c.slot(3 * u).rearrange("p (k n) -> p k n", k=KD), c.slot(3 * u + 1).rearrange("p (k n) -> p k n", k=KD),
             c.slot(3 * u + 2).rearrange("p (k n) -> p k n", k=4)] for u in range(2)]


def load_expert(c, sp, layer, e, u, w):
    src = c.ops[("moe_w_gate", "moe_w_up", "moe_w_down")[w]][layer].rearrange("e (k p) n -> e p k n", p=P)
    sp.dma_start(expert_slots(c)[u][w], src[bass.ds(e, 1)].rearrange("a p k n -> (a p) k n")).then_inc(c.moe_full[layer][3 * u + w], 16)


def experts(c, layer):
    nc, ops, ps = c.nc, c.ops, c.ps
    UN, BUF = 12, 4
    flat = c.h[:, :, :].rearrange("p k n -> p (k n)")
    xr = flat[:, 0:2 * D].rearrange("p (u n) -> p u n", u=2)
    y = flat[:, 2 * D:4 * D].rearrange("p (u n) -> p u n", u=2)
    with ExitStack() as st:
        def sb(name, shape, dt=F32):
            return st.enter_context(nc.sbuf_tensor(f"moe{layer}_" + name, shape, dt))

        whi, wlo = sb("w_hi", [P, BUF, 1024], F32R), sb("w_lo", [P, BUF, 1024], F32R)
        xhi, xlo = sb("rows_t_hi", [P, 2, KD, P], F32R), sb("rows_t_lo", [P, 2, KD, P], F32R)
        hhi, hlo = sb("hidden_t_hi", [P, 4, P], F32R), sb("hidden_t_lo", [P, 4, P], F32R)
        sil, hid = sb("silu", [P, FE]), sb("hidden", [P, FE])
        xfull = sems(nc, st, f"moe{layer}", ["x_full0", "x_full1"])
        wfull = c.moe_full[layer]
        stored = sems(nc, st, f"moe{layer}", ["stored0", "stored1"])
        turned, used, hturned, w_hi, w_lo, x_hi, x_lo, silued, hidden, h_hi, h_lo, ya, yv = sems(
            nc, st, f"moe{layer}", ["x_turned", "w_used", "h_turned", "w_hi", "w_lo", "x_hi", "x_lo", "silu", "hidden",
                                    "h_hi", "h_lo", "y_act", "y_dve"])
        wslot = expert_slots(c)

        def part(u, x):
            w = wslot[u][x // 4]
            return w[:, 2 * (x % 4):2 * (x % 4) + 2, :].rearrange("p k n -> p (k n)") if x < 8 else w[:, x - 8, :]

        def turns(eng, less=0):
            return eng.value_load(c.turns[0:1, less:less + 1], min_val=NE // 2 - less, max_val=NBLK // 2 - less)

        def at(i, d):
            return (i * 2 + d, d % 2, i + d // 2)

        GATE, UP, DOWN = 0, 4, 8

        with nc.Block(no_gpsimd_drain=True) as block:
            @block.gpsimd
            def _(pool):
                def load_rows(blk):
                    b, u, _ = blk
                    pool.dma_start(xr[:, u, :], c.xs.rearrange("(b p) d -> b p d", p=P)[bass.ds(b, 1)].rearrange("a p d -> (a p) d"))\
                        .then_inc(xfull[u], 16)

                def refill_rows(blk):
                    pool.wait_ge(turned, blk[0] - 1)
                    load_rows(blk)

                load_rows(at(0, 0))
                load_rows(at(0, 1))
                pen = turns(pool, 2)
                refill_rows(at(0, 2))
                refill_rows(at(0, 3))
                with pool.Fori(0, pen) as i:
                    for d in (1, 2):
                        refill_rows(at(i, d + 3))
                for u in range(2):
                    pool.wait_ge(stored[u], pen * 16 + 48)

            @block.sync
            def _(sp):
                def expert(blk):
                    return sp.value_load(c.blk_e[0:1, bass.ds(blk[0], 1)], min_val=0, max_val=NE - 1)

                def refill(step, unit, e, u, w):
                    sp.wait_ge(w_lo, step * UN + (unit + 4))
                    load_expert(c, sp, layer, e, u, w)

                def refill_after(s, before, now, after):
                    if before:
                        refill(s, 0, expert(before), before[1], 2)
                    refill(s, 4, expert(now), now[1], 1)
                    if after:
                        refill(s, 8, expert(after), after[1], 0)

                pen = turns(sp, 2)
                sp.wait_ge(w_lo, 4)
                load_expert(c, sp, layer, expert(at(0, 2)), 0, 0)
                refill_after(0, None, at(0, 2), at(0, 3))
                with sp.Fori(0, pen) as i:
                    for d in (3, 4):
                        refill_after(i * 2 + (d - 2), at(i, d - 1), at(i, d), at(i, d + 1))
                refill_after(pen * 2 + 1, at(pen, 2), at(pen, 3), None)
                refill(pen * 2 + 2, 0, expert(at(pen, 3)), 1, 2)

            @block.tensor
            def _(pe):
                def turn_rows(blk):
                    b, u, i = blk
                    pe.wait_ge(xfull[u], i * 16 + 16)
                    pe.wait_ge(x_lo, b + 1)
                    for k in range(KD):
                        mm = pe.transpose(ps[:, k // 4, (k % 4) * P:(k % 4 + 1) * P], xr[:, u, k * P:(k + 1) * P], c.base["ident"])
                    mm.then_inc(turned, 1)

                def turn_hidden(blk):
                    pe.wait_ge(hidden, blk[0] + 2)
                    pe.wait_ge(h_lo, blk[0] + 1)
                    for k in range(4):
                        mm = pe.transpose(ps[:, 4, k * P:(k + 1) * P], hid[:, k * P:(k + 1) * P], c.base["ident"])
                    mm.then_inc(hturned, 1)

                def three(out, hi, lo, first, last):
                    for x, (lhs, rhs) in enumerate(((hi[0], hi[1]), (hi[0], lo[1]), (lo[0], hi[1]))):
                        mm = pe.matmul(out, lhs, rhs, start=(first and x == 0), stop=(last and x == 2))
                    return mm

                def gate_or_up(blk, bank, step, unit, x):
                    u = blk[1]
                    pe.wait_ge(w_lo, step * UN + (unit + x + 1))
                    for k in range(2):
                        kk, cols = 2 * x + k, slice(k * 512, (k + 1) * 512)
                        mm = three(ps[:, bank, :], (xhi[:, u, kk, :], whi[:, x, cols]),
                                   (xlo[:, u, kk, :], wlo[:, x, cols]), kk == 0, kk == KD - 1)
                    mm.then_inc(used, 1)

                def gate(blk, step, unit, xs):
                    if xs[0] == 0:
                        pe.wait_ge(x_lo, blk[0] + 2)
                        pe.wait_ge(silued, blk[0] + 1)
                    for x in xs:
                        gate_or_up(blk, 2, step, unit, x)

                def up(blk):
                    pe.wait_ge(x_lo, blk[0] + 2)
                    pe.wait_ge(hidden, blk[0] + 1)
                    for x in range(4):
                        gate_or_up(blk, 3, blk[0], 4, x)

                def down(blk, step, unit):
                    pe.wait_ge(h_lo, blk[0] + 2)
                    pe.wait_ge(ya, blk[0] + 1)
                    pe.wait_ge(yv, blk[0] + 1)
                    for k in range(4):
                        pe.wait_ge(w_lo, step * UN + (unit + k + 1))
                        for n in range(2):
                            cols = slice(n * 512, (n + 1) * 512)
                            mm = three(ps[:, 5 + n, :], (hhi[:, k, :], whi[:, k, cols]),
                                       (hlo[:, k, :], wlo[:, k, cols]), k == 0, k == 3)
                        mm.then_inc(used, 1)

                def up_and_gate(now, after):
                    turn_rows(after)
                    up(now)
                    gate(after, now[0], 8, (0, 1))
                    turn_hidden(now)
                    gate(after, now[0], 8, (2, 3))

                pe.sem_inc(hturned, 1)
                pe.sem_inc(used, BUF)
                last = turns(pe, 1)
                turn_rows(at(0, 0))
                gate(at(0, 0), 0, 0, (0, 1, 2, 3))
                up_and_gate(at(0, 0), at(0, 1))
                with pe.Fori(0, last) as i:
                    for d in (1, 2):
                        down(at(i, d - 1), i * 2 + d, 0)
                        up_and_gate(at(i, d), at(i, d + 1))
                down(at(last, 0), last * 2 + 1, 0)
                up(at(last, 1))
                turn_hidden(at(last, 1))
                down(at(last, 1), last * 2 + 1, 8)

            @block.scalar
            def _(act):
                def split(blk, w, step, unit, xs=range(4)):
                    _, u, i = blk
                    for x in xs:
                        act.wait_ge(wfull[3 * u + w // 4], i * 16 + 16)
                        act.wait_ge(used, step * UN + (unit + x + 1))
                        nc.scalar.activation(whi[:, x, :], part(u, w + x), ACT.Identity).then_inc(w_hi, 1)

                def take_x(blk):
                    act.wait_ge(turned, blk[0] + 1)
                    nc.scalar.activation(xhi[:, blk[1], :, :], ps[:, 0:2, :].rearrange("p a (k n) -> p (a k) n", k=4), ACT.Identity).then_inc(x_hi, 1)

                def take_hidden(blk):
                    act.wait_ge(hturned, blk[0] + 2)
                    nc.scalar.activation(hhi[:, :, :], ps[:, 4, :].rearrange("p (k n) -> p k n", k=4), ACT.Identity).then_inc(h_hi, 1)

                def silu(blk, gate_made):
                    act.wait_ge(used, gate_made)
                    act.wait_ge(hidden, blk[0] + 1)
                    nc.scalar.activation(sil[:, :], ps[:, 2, :], ACT.Silu).then_inc(silued, 1)

                def take_y(blk, down_made):
                    b, u, i = blk
                    act.wait_ge(used, down_made)
                    act.wait_ge(stored[u], i * 16 + 16)
                    nc.scalar.copy(y[:, u, 0:512], ps[:, 5, :]).then_inc(ya, 1)

                def store(blk):
                    b, u, _ = blk
                    act.wait_ge(ya, b + 2)
                    act.wait_ge(yv, b + 2)
                    act.dma_start(c.ys.rearrange("(b p) d -> b p d", p=P)[bass.ds(b, 1)].rearrange("a p d -> (a p) d"), y[:, u, :])\
                        .then_inc(stored[u], 16)

                def step(before, now, after):
                    s = now[0]
                    split(before, DOWN, s, 0, (0, 1))
                    take_hidden(before)
                    split(before, DOWN, s, 0, (2, 3))
                    silu(now, s * UN + BUF)
                    split(now, UP, s, 4)
                    if after:
                        take_x(after)
                        split(after, GATE, s, 8, (0,))
                        take_y(before, s * UN + (4 + BUF))
                        split(after, GATE, s, 8, (1, 2, 3))
                    else:
                        take_y(before, s * UN + (4 + BUF))
                    store(before)

                for ahead in (silued, ya):
                    act.sem_inc(ahead, 1)
                for ahead in stored:
                    act.sem_inc(ahead, 16)
                last = turns(act, 1)
                take_x(at(0, 0))
                split(at(0, 0), GATE, 0, 0)
                split(at(0, 0), UP, 0, 4)
                silu(at(0, 0), 4 + BUF)
                take_x(at(0, 1))
                split(at(0, 1), GATE, 0, 8)
                with act.Fori(0, last) as i:
                    for d in (1, 2):
                        step(at(i, d - 1), at(i, d), at(i, d + 1))
                step(at(last, 0), at(last, 1), None)
                split(at(last, 1), DOWN, last * 2 + 1, 8)
                take_hidden(at(last, 1))
                take_y(at(last, 1), last * (2 * UN) + (2 * UN + BUF))
                store(at(last, 1))

            @block.vector
            def _(dve):
                def split(blk, w, step, unit, xs=range(4)):
                    for x in xs:
                        dve.wait_ge(w_hi, step * UN + (unit + x + 1))
                        dve.tensor_tensor(wlo[:, x, :], part(blk[1], w + x), whi[:, x, :].bitcast(F32), ALU.subtract).then_inc(w_lo, 1)

                def take_x(blk):
                    b, u, _ = blk
                    dve.wait_ge(x_hi, b + 1)
                    dve.tensor_tensor(xlo[:, u, :, :], ps[:, 0:2, :].rearrange("p a (k n) -> p (a k) n", k=4),
                                      xhi[:, u, :, :].bitcast(F32), ALU.subtract).then_inc(x_lo, 1)

                def take_hidden(blk):
                    dve.wait_ge(h_hi, blk[0] + 1)
                    dve.tensor_tensor(hlo[:, :, :], ps[:, 4, :].rearrange("p (k n) -> p k n", k=4), hhi[:, :, :].bitcast(F32),
                                      ALU.subtract).then_inc(h_lo, 1)

                def make_hidden(blk):
                    b = blk[0]
                    dve.wait_ge(silued, b + 2)
                    dve.wait_ge(used, b * UN + (8 + BUF))
                    dve.wait_ge(hturned, b + 1)
                    dve.tensor_tensor(hid[:, :], sil[:, :], ps[:, 3, :], ALU.mult).then_inc(hidden, 1)

                def take_y(blk, down_made):
                    b, u, i = blk
                    dve.wait_ge(used, down_made)
                    dve.wait_ge(stored[u], i * 16 + 16)
                    dve.tensor_copy(y[:, u, 512:1024], ps[:, 6, :]).then_inc(yv, 1)

                def step(before, now, after):
                    s = now[0]
                    split(before, DOWN, s, 0, (0, 1))
                    take_hidden(before)
                    split(before, DOWN, s, 0, (2, 3))
                    split(now, UP, s, 4)
                    if after:
                        take_x(after)
                        split(after, GATE, s, 8, (0,))
                        take_y(before, s * UN + (4 + BUF))
                        split(after, GATE, s, 8, (1, 2, 3))
                        make_hidden(now)
                    else:
                        take_y(before, s * UN + (4 + BUF))

                for ahead in (x_lo, hidden, h_lo, yv):
                    dve.sem_inc(ahead, 1)
                last = turns(dve, 1)
                take_x(at(0, 0))
                split(at(0, 0), GATE, 0, 0)
                split(at(0, 0), UP, 0, 4)
                take_x(at(0, 1))
                split(at(0, 1), GATE, 0, 8)
                make_hidden(at(0, 0))
                with dve.Fori(0, last) as i:
                    for d in (1, 2):
                        step(at(i, d - 1), at(i, d), at(i, d + 1))
                step(at(last, 0), at(last, 1), None)
                split(at(last, 1), DOWN, last * 2 + 1, 8)
                make_hidden(at(last, 1))
                take_hidden(at(last, 1))
                take_y(at(last, 1), last * (2 * UN) + (2 * UN + BUF))


def combine(c, layer):
    nc, ps = c.nc, c.ps
    gate = c.mod[:, layer, 40:48, :]
    with ExitStack() as st:
        y = st.enter_context(nc.sbuf_tensor(f"comb{layer}_rows", [P, 2, TOPK, D], F32))
        got = sems(nc, st, f"comb{layer}", [f"got{u}{k}" for u in range(2) for k in range(2)])
        weighed, summed, turned, added = sems(nc, st, f"comb{layer}", ["weighed", "summed", "turned", "added"])
        with nc.Block(no_gpsimd_drain=True) as block:
            @block.gpsimd
            def _(pool):
                for t in range(NT):
                    if t >= 2:
                        pool.wait_ge(turned, t - 1)
                    for k in range(TOPK):
                        pool.indirect_dma_start(y[:, t % 2, k, :], None, c.ys,
                                                bass.IndirectOffsetOnAxis(c.dest[:, k, t:t + 1], 0)).then_inc(got[2 * (t % 2) + k], 16)

            @block.tensor
            def _(pe):
                for t in range(NT):
                    pe.wait_ge(summed, t + 1)
                    if t >= 4:
                        pe.wait_ge(added, (t - 3) * KD)
                    for k in range(KD):
                        mm = pe.transpose(ps[:, 2 * (t % 4) + k // 4, (k % 4) * P:(k % 4 + 1) * P],
                                          y[:, t % 2, 0, k * P:(k + 1) * P], c.base["ident"])
                    mm.then_inc(turned, 1)

            @block.vector
            def _(dve):
                for t in range(NT):
                    dve.wait_ge(got[2 * (t % 2)], 16 * (t // 2 + 1))
                    dve.wait_ge(got[2 * (t % 2) + 1], 16 * (t // 2 + 1))
                    dve.tensor_scalar(y[:, t % 2, 0, :], y[:, t % 2, 0, :], c.w12[:, 0, t:t + 1], None, ALU.mult).then_inc(weighed, 1)
                    dve.wait_ge(weighed, t + 1)
                    dve.scalar_tensor_tensor(out=y[:, t % 2, 0, :], in0=y[:, t % 2, 1, :], scalar=c.w12[:, 1, t:t + 1],
                                             in1=y[:, t % 2, 0, :], op0=ALU.mult, op1=ALU.add).then_inc(summed, 1)
                    dve.wait_ge(turned, t + 1)
                    jc = 0 if t == 0 else 1
                    for k in range(KD):
                        cols = slice(t * P, (t + 1) * P)
                        dve.scalar_tensor_tensor(out=c.x[:, k, cols], in0=ps[:, 2 * (t % 4) + k // 4, (k % 4) * P:(k % 4 + 1) * P],
                                                 scalar=gate[:, k, jc:jc + 1], in1=c.x[:, k, cols],
                                                 op0=ALU.mult, op1=ALU.add).then_inc(added, 1)


def write_out(c):
    nc, ops, ps = c.nc, c.ops, c.ps
    with ExitStack() as st:
        rows = st.enter_context(nc.sbuf_tensor("out_rows", [P, NT, D], F32))
        turned, taken, taken_v, out_s = sems(nc, st, "out", ["turned", "act", "dve", "stored"])
        with nc.Block(no_gpsimd_drain=True) as block:
            @block.tensor
            def _(pe):
                for g in range(2 * NT):
                    if g >= 8:
                        pe.wait_ge(taken, (g - 8) // 2 + 1)
                        pe.wait_ge(taken_v, (g - 8) // 2 + 1)
                    for k in range(4):
                        mm = pe.transpose(ps[:, g % 8, k * P:(k + 1) * P],
                                          c.h[:, 4 * (g % 2) + k, (g // 2) * P:(g // 2 + 1) * P], c.base["ident"])
                    mm.then_inc(turned, 1)

            @block.scalar
            def _(act):
                for g in range(0, 2 * NT, 2):
                    act.wait_ge(turned, g + 1)
                    nc.scalar.copy(rows[:, g // 2, 0:512], ps[:, g % 8, :]).then_inc(taken, 1)

            @block.vector
            def _(dve):
                for g in range(1, 2 * NT, 2):
                    dve.wait_ge(turned, g + 1)
                    dve.tensor_copy(rows[:, g // 2, 512:1024], ps[:, g % 8, :]).then_inc(taken_v, 1)

            @block.sync
            def _(sp):
                for t in range(NT):
                    sp.wait_ge(taken, t + 1)
                    sp.wait_ge(taken_v, t + 1)
                    dst = ops["y_prompt"][0] if t == 0 else ops["y_sample"][0, (t - 1) * P:t * P]
                    sp.dma_start(dst, rows[:, t, :]).then_inc(out_s, 16)
                sp.wait_ge(out_s, 16 * NT)


def trunk_step(nc, ops):
    with ExitStack() as stack:
        c = Chip(nc, stack, ops)

        def load_mla(sp, split, per, n):
            for s, load in ((4, lambda: load_mla_in(c, sp, 0)), (0, lambda: load_mla_q(c, sp, 0, 0)),
                            (1, lambda: load_mla_kv(c, sp, 0, 0)), (2, lambda: load_mla_o(c, sp, 0, 0))):
                last = max(x for x in range(n) if x % NSLOT == s)
                sp.wait_ge(split, per * (last + 1))
                load()

        with ExitStack() as st:
            cond4 = st.enter_context(nc.sbuf_tensor("cond_parts", [P, KD, 4], F32R))
            setup(c, cond4)
            modulation(c, cond4, load_mla)
        counters = [0, 0]
        for layer in range(DEPTH):
            kind = layer % 3
            norm(c, 2 * layer, c.amp[:, layer, 0], c.mod[:, layer, 0:8, :])
            (mla, retention)[kind](c, layer, counters[kind])
            counters[kind] += 1
            norm(c, 2 * layer + 1, c.amp[:, layer, 1], c.mod[:, layer, 24:32, :],
                 lambda sp: [load_expert(c, sp, layer, u, u, w) for u, w in ((0, 0), (0, 1), (1, 0), (0, 2), (1, 1), (1, 2))])
            route(c, layer)
            experts(c, layer)
            combine(c, layer)
        norm(c, 2 * DEPTH, c.fin2, c.zero2)
        write_out(c)


_INS = ["x_prompt", "x_sample", "cache_mla", "state_ret", "c", "c_ctx", "norm1_g", "norm2_g", "ada_w", "ada_b",
        "final_norm_g", "mla_w_in", "mla_q_norm_g", "mla_kv_norm_g", "mla_w_uq", "mla_w_ukv", "mla_w_o",
        "ret_w_in", "ret_decay_f", "ret_decay_b", "ret_w_o", "router_w", "router_b",
        "moe_w_gate", "moe_w_up", "moe_w_down"]
_CONSTS = ["base_consts", "mla_consts", "ret_consts", "trig_consts"]
_OUTS = {"y_prompt": (1, SEQ, D), "y_sample": (1, LAT, D), "new_cache": (1, 1, SEQ, KVL + ROPE),
         "new_state": (1, 1, 2, RH, DK, DV)}


def kernel(**inputs):
    import concourse.bacc as bacc
    from concourse.bass_utils import run_bass_kernel_spmd

    nc = bacc.Bacc("TRN2", target_bir_lowering=False, num_devices=1)
    arrays, ops = {}, {}
    for name, a in [(n, inputs[n]) for n in _INS] + list(zip(_CONSTS, shape_constants())):
        a = np.ascontiguousarray(a)
        arrays["in_" + name] = a
        ops[name] = nc.dram_tensor("in_" + name, a.shape, F32, kind="ExternalInput").ap()
    for name, shape in _OUTS.items():
        ops[name] = nc.dram_tensor("out_" + name, shape, F32, kind="ExternalOutput").ap()
    for name, blocks in (("rows_in", NBLK), ("rows_out", NBLK)):
        ops[name] = nc.dram_tensor(name, (blocks * P, D), F32, kind="Internal").ap()
    trunk_step(nc, ops)
    r = run_bass_kernel_spmd(nc, [arrays], core_ids=[0])
    return tuple(r.results[0]["out_" + name] for name in _OUTS)
```

```python
from contextlib import ExitStack

import numpy as np

import concourse.bass as bass
import concourse.mybir as mybir
from concourse.alu_op_type import AluOpType as ALU

F32 = mybir.dt.float32
F32R = mybir.dt.float32r
I32 = mybir.dt.int32
ACT = mybir.ActivationFunctionType
AX = mybir.AxisListType

P = 128
D = 1024
KD = D // P
SEQ, LAT, PAST = 128, 512, 128
T = SEQ + LAT
NT = T // P
RANGES = ((0, SEQ, 0), (SEQ, LAT, 1))
DEPTH = 2
EPS = 1e-6
GRID_W = 64
BASE = 10000.0

QL, KVL, ROPE, NOPE, VD, HEADS = 384, 256, 64, 128, 128, 8
KEYS = T + PAST
NKT = KEYS // P
LKEYS = LAT + PAST
PAIRS = HEADS // 2
UQ = NOPE + ROPE
MLA_SCALE = float(UQ) ** -0.5

RH, DK, DV = 4, 256, 512
KSCALE = float(DK) ** -0.5

NE, NG, EG, FE = 16, 4, 4, 512
TOPK = 2
ASSIGNED = T * TOPK
NOVER = (ASSIGNED - NE) // P
NBLK = (NE + NOVER + 1) // 2 * 2
BIG = 3.0e38

SLOT = 4096
NSLOT = 6


class Steps:

    def __init__(self, sem, names, ahead=0):
        self.sem, self.per, self.ahead = sem, len(names), ahead
        self.pos = {n: i + 1 for i, n in enumerate(names)}
        assert len(self.pos) == len(names)

    def value(self, name, i=0):
        return i * self.per + (self.pos[name] + self.ahead)

    def before(self, i):
        assert self.ahead
        return i * self.per + self.ahead


BASE_COLS = {"ident": P, "ones": P, "before": P, "iota16": NE, "iota4": NG, "iotab": NBLK, "pick": 2}
MLA_COLS = {"swap": P, "rcos": LAT, "rsin": LAT}
RET_COLS = {"relf": LAT, "relb": LAT, "trif": P, "trib": P, "kf": 1, "kb": 1}
TRIG_COLS = {"cos": LAT, "sin": LAT, "idxf": LAT}


def _width(cols):
    return sum(cols.values())


def _views(tile, cols):
    at, out = 0, {}
    for n, w in cols.items():
        out[n] = tile[:, at:at + w]
        at += w
    return out


def shape_constants():
    f = np.float32
    p, m = np.arange(P)[:, None], np.arange(P)[None, :]
    n = np.arange(LAT)[None, :]
    one = np.ones((P, 1), f)
    base = [np.eye(P), np.ones((P, P)), p < m, one * np.arange(NE), one * np.arange(NG),
            one * np.arange(NBLK), p % 2 == np.arange(2)]
    d = np.arange(P) % ROPE
    inv = (f(BASE) ** (-np.arange(0, ROPE // 2, 2, dtype=f) / f(ROPE // 2))).astype(f)[d % 16]
    where = np.where((d < 32)[:, None], n // GRID_W, n % GRID_W).astype(f)
    ang = (where * inv[:, None]).astype(f)
    sign = np.where(d % 32 < 16, -1.0, 1.0)[:, None]
    partner = (p // 32) * 32 + (p % 32 + 16) % 32
    mla = [partner == m, np.cos(ang), np.sin(ang) * sign]
    rel_f, rel_b = n - p, p + (LAT - P) - n
    ret = [np.maximum(rel_f, 0), np.maximum(rel_b, 0), m >= p, m <= p, P - 1 - p, p]
    inv = (f(BASE) ** (-np.linspace(0.0, 1.0, DK // 2, dtype=f))).astype(f)
    ang = (n.astype(f) * inv[:, None]).astype(f)
    trig = [np.cos(ang), np.sin(ang), one * (n + 1)]
    return [np.concatenate([np.asarray(a, f) for a in g], axis=1) for g in (base, mla, ret, trig)]


class Chip:

    def __init__(self, nc, stack, ops):
        self.nc, self.ops = nc, ops

        def sb(name, shape, dt=F32):
            return stack.enter_context(nc.sbuf_tensor(name, shape, dt))

        self.ps = stack.enter_context(nc.psum_tensor("ps", [P, 8, 512], F32))
        self.x = sb("x_resid", [P, KD, T])
        self.h = sb("h_normed", [P, KD, T])
        self.ring = sb("weight_ring", [P, NSLOT * SLOT])
        self.base_tile = sb("base_consts", [P, _width(BASE_COLS)])
        self.base = _views(self.base_tile, BASE_COLS)
        self.mod = sb("modulation", [P, DEPTH, 48, 2])
        self.amp = sb("norm_amplitude", [P, DEPTH, 2, KD, 2])
        self.cols_a = sb("norm_gain_and_ada_bias", [P, P])
        self.cols_b = sb("other_columns", [P, 32])
        self.zero2 = sb("no_shift", [P, KD, 2])
        self.fin2 = sb("final_gain", [P, KD, 2])
        self.router = sb("router_w", [P, KD, NE])
        self.router_b = sb("router_b", [P, NE])
        self.eps = sb("eps", [P, 1])
        self.log_decay = sb("log_decays", [P, RH, 2])
        self.w12 = sb("route_weights", [P, TOPK, NT])
        self.dest = sb("route_rows", [P, TOPK, NT], I32)
        self.blk_e = sb("block_expert", [P, NBLK], I32)
        self.turns = sb("block_pairs", [P, 3], I32)
        self.norm_sems = sems(nc, stack, "norm", ["squared", "summed", "rooted", "inverted", "scaled", "shifted"])
        self.ada_full = sems(nc, stack, "ada", [f"full{i}" for i in range(NSLOT)])
        self.moe_full = [sems(nc, stack, f"moe{l}", [f"{n}_full{u}" for u in range(2) for n in "gud"]) for l in range(DEPTH)]
        self.w_in_full, self.wq_full, self.wkv_full, self.wo_full = sems(nc, stack, "mla", ["w_in", "wq_full", "wkv_full", "wo_full"])
        self.ret_full = sems(nc, stack, "ret", [f"full{s}" for s in range(4)])
        self.xs = ops["rows_in"]
        self.ys = ops["rows_out"]

    def slot(self, s, width=SLOT):
        return self.ring[:, s * SLOT:s * SLOT + width]


def sems(nc, stack, stage, names):
    return [stack.enter_context(nc.semaphore(f"{stage}_{n}")) for n in names]


def setup(c, cond4):
    nc, ops, ps = c.nc, c.ops, c.ps
    with ExitStack() as st:
        xt = st.enter_context(nc.sbuf_tensor("x_rows", [P, NT, D], F32))
        rows_a = st.enter_context(nc.sbuf_tensor("vector_rows_a", [P, P], F32))
        rows_b = st.enter_context(nc.sbuf_tensor("vector_rows_b", [P, P], F32))
        cond = st.enter_context(nc.sbuf_tensor("silu_cond", [P, KD, 2], F32))
        raw, lt1, lt2 = (st.enter_context(nc.sbuf_tensor(n, [P, 2, RH], F32)) for n in ("logits", "log_tmp1", "log_tmp2"))
        silued, logit_in, absolute, logged = sems(nc, st, "setup", ["silu", "logits", "absolute", "logged"])
        consts_in, rows_in, x_in, small_in, turned, taken_a, taken_v, memsets = sems(
            nc, st, "setup", ["consts", "rows", "x", "small", "turned", "act", "dve", "memset"])
        with nc.Block(no_gpsimd_drain=True) as block:
            @block.sync
            def _(sp):
                sp.dma_start(c.base_tile[:, :], ops["base_consts"]).then_inc(consts_in, 16)
                sp.dma_start(raw[:, 0, :], ops["ret_decay_f"].broadcast_to([P, RH])).then_inc(logit_in, 16)
                sp.dma_start(raw[:, 1, :], ops["ret_decay_b"].broadcast_to([P, RH])).then_inc(logit_in, 16)
                sp.dma_start(xt[:, 0, :], ops["x_prompt"][0]).then_inc(x_in, 16)
                sp.dma_start(xt[:, 1:NT, :], ops["x_sample"][0].rearrange("(t p) d -> p t d", p=P)).then_inc(x_in, 16)
                sp.dma_start(c.router[:, :, :], ops["router_w"].rearrange("(k p) e -> p k e", p=P)).then_inc(small_in, 16)
                sp.dma_start(c.router_b[:, :], ops["router_b"].rearrange("(a e) -> a e", a=1).broadcast_to([P, NE])).then_inc(small_in, 16)
                for n in range(NSLOT):
                    load_ada(c, sp, n)
                sp.wait_ge(small_in, 32)

            @block.gpsimd
            def _(pool):
                pool.memset(c.eps[:, :], EPS).then_inc(memsets, 1)
                pool.memset(c.zero2[:, :, :], 0.0).then_inc(memsets, 1)
                pool.memset(rows_b[:, :], 0.0).then_inc(memsets, 1)

            @block.scalar
            def _(act):
                act.dma_start(rows_a[0:16, :], ops["norm1_g"].rearrange("l (k p) -> (l k) p", p=P)).then_inc(rows_in, 16)
                act.dma_start(rows_a[16:32, :], ops["norm2_g"].rearrange("l (k p) -> (l k) p", p=P)).then_inc(rows_in, 16)
                act.dma_start(rows_a[32:128, :], ops["ada_b"].rearrange("l (k p) -> (l k) p", p=P)).then_inc(rows_in, 16)
                act.wait_ge(memsets, 3)
                for r, n in ((0, "c_ctx"), (8, "c"), (16, "final_norm_g"), (24, "mla_q_norm_g"), (27, "mla_kv_norm_g")):
                    v = ops[n] if len(ops[n].shape) == 1 else ops[n].rearrange("a n -> (a n)")
                    w = v.shape[0] // P
                    act.dma_start(rows_b[r:r + w, :], v.rearrange("(k p) -> k p", p=P)).then_inc(rows_in, 16)
                act.wait_ge(absolute, 2)
                nc.scalar.activation(lt1[:, :, :], lt1[:, :, :], ACT.Exp, scale=-1.0).then_inc(logged, 1)
                act.wait_ge(logged, 1)
                nc.scalar.activation(lt1[:, :, :], lt1[:, :, :], ACT.Ln, bias=1.0).then_inc(logged, 1)
                for g in range(1, 2 * NT, 2):
                    act.wait_ge(turned, g + 3)
                    nc.scalar.copy(c.x[:, 4:8, (g // 2) * P:(g // 2 + 1) * P],
                                   ps[:, 2 + g % 6, :].rearrange("p (k n) -> p k n", k=4)).then_inc(taken_a, 1)
                act.wait_ge(taken_v, 3)
                for j in range(2):
                    nc.scalar.activation(cond[:, :, j], c.cols_b[:, 8 * j:8 * j + 8], ACT.Silu).then_inc(silued, 1)
                act.wait_ge(silued, 2)
                nc.scalar.activation(cond4[:, :, 0:2], cond[:, :, :], ACT.Identity).then_inc(silued, 1)

            @block.tensor
            def _(pe):
                pe.wait_ge(consts_in, 16)
                pe.wait_ge(rows_in, 16 * 8)
                pe.wait_ge(memsets, 3)
                pe.transpose(ps[:, 0, 0:P], rows_a[:, :], c.base["ident"]).then_inc(turned, 1)
                pe.transpose(ps[:, 1, 0:P], rows_b[:, :], c.base["ident"]).then_inc(turned, 1)
                pe.wait_ge(x_in, 32)
                for g in range(2 * NT):
                    if g >= 6:
                        pe.wait_ge(taken_v, 3 + (g - 6) // 2 + 1)
                        pe.wait_ge(taken_a, (g - 6) // 2 + 1)
                    for k in range(4):
                        mm = pe.transpose(ps[:, 2 + g % 6, k * P:(k + 1) * P],
                                          xt[:, g // 2, (4 * (g % 2) + k) * P:(4 * (g % 2) + k + 1) * P], c.base["ident"])
                    mm.then_inc(turned, 1)

            @block.vector
            def _(dve):
                dve.wait_ge(logit_in, 32)
                dve.tensor_scalar(lt2[:, :, :], raw[:, :, :], -1.0, None, ALU.mult).then_inc(absolute, 1)
                dve.wait_ge(absolute, 1)
                dve.tensor_tensor(lt1[:, :, :], raw[:, :, :], lt2[:, :, :], ALU.max).then_inc(absolute, 1)
                dve.wait_ge(absolute, 2)
                dve.tensor_scalar(lt2[:, :, :], raw[:, :, :], 0.0, None, ALU.min).then_inc(absolute, 1)
                dve.wait_ge(absolute, 3)
                dve.wait_ge(logged, 2)
                dve.tensor_tensor(c.log_decay[:, :, :].rearrange("p h f -> p f h"), lt2[:, :, :], lt1[:, :, :],
                                  ALU.subtract).then_inc(absolute, 1)
                dve.wait_ge(turned, 1)
                dve.tensor_copy(c.cols_a[:, :], ps[:, 0, 0:P]).then_inc(taken_v, 1)
                dve.wait_ge(turned, 2)
                dve.tensor_copy(c.cols_b[:, :], ps[:, 1, 0:32]).then_inc(taken_v, 1)
                dve.wait_ge(taken_v, 2)
                dve.tensor_copy(c.fin2[:, :, 0], c.cols_b[:, 16:24]).then_inc(taken_v, 1)
                for g in range(0, 2 * NT, 2):
                    dve.wait_ge(turned, g + 3)
                    dve.tensor_copy(c.x[:, 0:4, (g // 2) * P:(g // 2 + 1) * P],
                                    ps[:, 2 + g % 6, :].rearrange("p (k n) -> p k n", k=4)).then_inc(taken_v, 1)
                dve.tensor_copy(c.fin2[:, :, 1], c.cols_b[:, 16:24]).then_inc(taken_v, 1)
                dve.wait_ge(silued, 3)
                dve.tensor_tensor(cond4[:, :, 2:4], cond[:, :, :], cond4[:, :, 0:2].bitcast(F32), ALU.subtract).then_inc(taken_v, 1)


ADA_CH = 6 * D // 512


def load_ada(c, sp, n):
    src = c.ops["ada_w"].rearrange("l (k p) (g n) -> l g p k n", p=P, n=512)[n // ADA_CH, n % ADA_CH]
    sp.dma_start(c.slot(n % NSLOT).rearrange("p (k n) -> p k n", k=KD), src).then_inc(c.ada_full[n % NSLOT], 16)


def modulation(c, cond4, prefetch):
    nc, ops, ps = c.nc, c.ops, c.ps
    N = DEPTH * ADA_CH
    UN = 4
    with ExitStack() as st:
        whi = st.enter_context(nc.sbuf_tensor("ada_w_hi", [P, 4, 2, 512], F32R))
        wlo = st.enter_context(nc.sbuf_tensor("ada_w_lo", [P, 4, 2, 512], F32R))
        rows = st.enter_context(nc.sbuf_tensor("ada_rows", [4, 2, 512], F32))
        hi_s, lo_s, used, rowed, turned, biased, amp = sems(nc, st, "ada", ["w_hi", "w_lo", "used", "rows", "turned", "biased", "amp"])

        def part(n, x):
            return c.slot(n % NSLOT).rearrange("p (k n) -> p k n", k=KD)[:, 2 * x:2 * x + 2, :]

        with nc.Block(no_gpsimd_drain=True) as block:
            @block.sync
            def _(sp):
                for n in range(NSLOT, N):
                    sp.wait_ge(lo_s, UN * (n - NSLOT + 1))
                    load_ada(c, sp, n)
                prefetch(sp, lo_s, UN, N)

            @block.scalar
            def _(act):
                for n in range(N):
                    act.wait_ge(c.ada_full[n % NSLOT], 16 * (n // NSLOT + 1))
                    for x in range(UN):
                        if UN * n + x >= 4:
                            act.wait_ge(used, UN * n + x - 3)
                        nc.scalar.activation(whi[:, x], part(n, x), ACT.Identity).then_inc(hi_s, 1)

            @block.tensor
            def _(pe):
                def turn(n):
                    pe.wait_ge(rowed, n + 1)
                    for b in range(4):
                        col = 2 * ((n % ADA_CH) * 4 + b)
                        mm = pe.matmul(ps[:, 4 + n // ADA_CH, col:col + 2], rows[:, n % 2, b * P:(b + 1) * P],
                                       c.base["pick"][0:4, :], start=True, stop=True)
                    mm.then_inc(turned, 1)

                for n in range(N):
                    if n >= 4:
                        pe.wait_ge(rowed, n - 3)
                    for x in range(UN):
                        pe.wait_ge(lo_s, UN * n + x + 1)
                        for k in range(2):
                            for w in (whi, wlo):
                                mm = pe.matmul(ps[0:4, n % 4, :], cond4[:, 2 * x + k, :], w[:, x, k, :],
                                               start=(x == 0 and k == 0 and w is whi), stop=(x == UN - 1 and k == 1 and w is wlo))
                        mm.then_inc(used, 1)
                    if n:
                        turn(n - 1)
                turn(N - 1)

            @block.vector
            def _(dve):
                def take_rows(n):
                    dve.wait_ge(used, UN * (n + 1))
                    if n >= 2:
                        dve.wait_ge(turned, n - 1)
                    dve.tensor_copy(rows[:, n % 2, :], ps[0:4, n % 4, :]).then_inc(rowed, 1)

                for n in range(N):
                    for x in range(UN):
                        dve.wait_ge(hi_s, UN * n + x + 1)
                        dve.tensor_tensor(wlo[:, x], part(n, x), whi[:, x].bitcast(F32), ALU.subtract).then_inc(lo_s, 1)
                    if n:
                        take_rows(n - 1)
                take_rows(N - 1)
                for layer in range(DEPTH):
                    dve.wait_ge(turned, (layer + 1) * ADA_CH)
                    bias = c.cols_a[:, 32 + 48 * layer:32 + 48 * layer + 48]
                    for j in range(2):
                        dve.tensor_tensor(c.mod[:, layer, :, j],
                                          ps[:, 4 + layer, 0:96].rearrange("p (m j) -> p m j", j=2)[:, :, j],
                                          bias, ALU.add).then_inc(biased, 1)
                    dve.wait_ge(biased, 2 * layer + 2)
                    for n, m in ((0, 1), (1, 4)):
                        gain = c.cols_a[:, 16 * n + 8 * layer:16 * n + 8 * layer + 8]
                        for j in range(2):
                            dve.scalar_tensor_tensor(out=c.amp[:, layer, n, :, j],
                                                     in0=c.mod[:, layer, 8 * m:8 * m + 8, j], scalar=1.0,
                                                     in1=gain, op0=ALU.add, op1=ALU.mult).then_inc(amp, 1)


def norm(c, call, amp, shift, prefetch=None, parts=None):
    nc, ps = c.nc, c.ps
    with ExitStack() as st:
        rstd = st.enter_context(nc.sbuf_tensor(f"norm{call}_rstd", [P, T], F32))
        squared, summed, rooted, inverted, scaled, shifted = c.norm_sems
        before2, before8, before16 = 2 * call, KD * call, 2 * KD * call
        with nc.Block(no_gpsimd_drain=True) as block:
            if prefetch:
                @block.sync
                def _(sp):
                    prefetch(sp)

            @block.scalar
            def _(act):
                for k in range(KD):
                    nc.scalar.activation(c.h[:, k, :], c.x[:, k, :], ACT.Square).then_inc(squared, 1)
                for r, (a, n, j) in enumerate(RANGES):
                    act.wait_ge(summed, before2 + r + 1)
                    nc.scalar.activation(rstd[:, a:a + n], ps[:, r, 0:n], ACT.Sqrt, bias=c.eps[:, :], scale=1.0 / D).then_inc(rooted, 1)
                i = 0
                for k in range(KD):
                    for a, n, j in RANGES:
                        i += 1
                        act.wait_ge(scaled, before16 + i)
                        nc.scalar.activation((parts[0] if parts else c.h)[:, k, a:a + n], c.h[:, k, a:a + n], ACT.Identity,
                                             bias=shift[:, k, j:j + 1]).then_inc(shifted, 1)

            @block.tensor
            def _(pe):
                for k in range(KD):
                    pe.wait_ge(squared, before8 + k + 1)
                    for r, (a, n, j) in enumerate(RANGES):
                        mm = pe.matmul(ps[:, r, 0:n], c.base["ones"], c.h[:, k, a:a + n],
                                       start=(k == 0), stop=(k == KD - 1))
                        if k == KD - 1:
                            mm.then_inc(summed, 1)

            @block.vector
            def _(dve):
                for r, (a, n, j) in enumerate(RANGES):
                    dve.wait_ge(rooted, before2 + r + 1)
                    dve.reciprocal(rstd[:, a:a + n], rstd[:, a:a + n]).then_inc(inverted, 1)
                dve.wait_ge(inverted, before2 + 2)
                for k in range(KD):
                    for a, n, j in RANGES:
                        dve.scalar_tensor_tensor(out=c.h[:, k, a:a + n], in0=c.x[:, k, a:a + n],
                                                 scalar=amp[:, k, j:j + 1], in1=rstd[:, a:a + n],
                                                 op0=ALU.mult, op1=ALU.mult).then_inc(scaled, 1)
                i = 0
                for k in range(KD if parts else 0):
                    for a, n, j in RANGES:
                        i += 1
                        dve.wait_ge(shifted, before16 + i)
                        dve.scalar_tensor_tensor(out=parts[1][:, k, a:a + n], in0=c.h[:, k, a:a + n],
                                                 scalar=shift[:, k, j:j + 1], in1=parts[0][:, k, a:a + n].bitcast(F32),
                                                 op0=ALU.add, op1=ALU.subtract)


def mla(c, layer, j):
    nc = c.nc
    with ExitStack() as st:
        def sb(name, shape):
            return st.enter_context(nc.sbuf_tensor("mla_" + name, shape, F32))

        m = {"consts": sb("consts", [P, _width(MLA_COLS)]), "cq": sb("cq", [P, 3, T]),
             "ckv": sb("ckv", [P, 2, KEYS]), "kpe": sb("kpe", [P, KEYS])}
        m.update(_views(m["consts"], MLA_COLS))
        mla_project(c, m, j)
        mla_pairs(c, m, layer, j)


def mla_project(c, m, j):
    nc, ops, ps = c.nc, c.ops, c.ps
    W = QL + KVL + ROPE
    w_in = c.ring[:, 3 * SLOT:3 * SLOT + KD * W].rearrange("p (k n) -> p k n", k=KD)
    cq, ckv, kpe = m["cq"], m["ckv"], m["kpe"]
    with ExitStack() as st:
        sq = st.enter_context(nc.sbuf_tensor("mla_squares", [P, 5, T], F32))
        rq = st.enter_context(nc.sbuf_tensor("mla_rstd", [P, 2, T], F32))
        cache = st.enter_context(nc.sbuf_tensor("mla_cache_rows", [P, 3 * P], F32))
        w_kpe2 = st.enter_context(nc.sbuf_tensor("mla_w_kpe_twice", [P, KD, P], F32))
        rows = st.enter_context(nc.sbuf_tensor("mla_new_cache", [P, 3 * P], F32))
        rope = st.enter_context(nc.sbuf_tensor("mla_rope_parts", [P, 2, LAT], F32))
        loaded = c.w_in_full
        zero_s, zeros_out = sems(nc, st, "mlap", ["zero", "zeros_out"])
        zeros = st.enter_context(nc.sbuf_tensor("zero_rows", [P, D], F32))
        const_in, cache_in, done, act_s, dve_s, out_s, dup_s = sems(
            nc, st, "mlap", ["consts", "cache_in", "products", "act", "dve", "out", "dup"])
        Z_BANKS, SUM_BANKS = (0, 2, 4, 0, 2, 2), (4, 0)
        prod = Steps(done, [f"z{b}" for b in range(5)] + ["cache", "sq", "skv", "z5", "swap", "rows"])
        act_n = Steps(act_s, [f"{n}{b}{r}" for b in range(5) for n, r in (("z", 0), ("z", 1), ("s", ""))]
                      + ["cacheT"] + [f"root{g}{r}" for g in range(2) for r in range(2)] + ["z50", "z51"])
        dve_n = Steps(dve_s, ["cachepe", "inv0"] + [f"n{b}{r}" for b in range(3) for r in range(2)]
                      + ["inv1"] + [f"n{b}{r}" for b in range(3, 5) for r in range(2)] + ["rc", "rs", "rot", "rows"])
        with nc.Block(no_gpsimd_drain=True) as block:
            @block.sync
            def _(sp):
                sp.dma_start(cache[:, 0:KVL + ROPE], ops["cache_mla"][0, j]).then_inc(cache_in, 16)
                sp.dma_start(cache[:, KVL + ROPE:3 * P], ops["cache_mla"][0, j, :, KVL:KVL + ROPE]).then_inc(cache_in, 16)
                sp.dma_start(m["consts"][:, :], ops["mla_consts"]).then_inc(const_in, 16)
                sp.wait_ge(zero_s, 1)
                for b in range(NBLK):
                    sp.dma_start(c.xs[b * P:(b + 1) * P, :], zeros[:, :]).then_inc(zeros_out, 16)
                for b in range(NE, NBLK):
                    sp.dma_start(c.ys[b * P:(b + 1) * P, :], zeros[:, :]).then_inc(zeros_out, 16)
                sp.wait_ge(zeros_out, 16 * (NBLK + NBLK - NE))
                sp.wait_ge(dve_n.sem, dve_n.value("rows"))
                sp.dma_start(ops["new_cache"][0, j], rows[:, 0:KVL + ROPE]).then_inc(out_s, 16)
                sp.wait_ge(out_s, 16)

            @block.tensor
            def _(pe):
                pe.wait_ge(loaded, 16)
                pe.wait_ge(dup_s, 2)
                def project(b):
                    for r, (a, n, _) in enumerate(RANGES):
                        for k in range(KD):
                            lhs = w_in[:, k, b * P:(b + 1) * P] if b < 5 else w_kpe2[:, k, :]
                            mm = pe.matmul(ps[:, Z_BANKS[b] + r, 0:n], lhs, c.h[:, k, a:a + n],
                                           start=(k == 0), stop=(k == KD - 1))
                    mm.then_inc(done, 1)

                for b in range(5):
                    if b >= 3:
                        pe.wait_ge(act_n.sem, act_n.value(f"z{b - 3}1"))
                    project(b)
                pe.wait_ge(cache_in, 32)
                for b in range(3):
                    mm = pe.transpose(ps[:, 6 + b // 2, (b % 2) * P:(b % 2 + 1) * P], cache[:, b * P:(b + 1) * P], c.base["ident"])
                mm.then_inc(done, 1)
                for g, blocks in ((0, (0, 1, 2)), (1, (3, 4))):
                    pe.wait_ge(act_n.sem, act_n.value(f"s{blocks[-1]}"))
                    for r, (a, n, _) in enumerate(RANGES):
                        for b in blocks:
                            mm = pe.matmul(ps[:, SUM_BANKS[g] + r, 0:n], c.base["ones"], sq[:, b, a:a + n],
                                           start=(b == blocks[0]), stop=(b == blocks[-1]))
                    mm.then_inc(done, 1)
                project(5)
                pe.wait_ge(act_n.sem, act_n.value("z51"))
                pe.wait_ge(const_in, 16)
                pe.matmul(ps[:, 5, :], m["swap"], kpe[:, SEQ:T], start=True, stop=True).then_inc(done, 1)
                pe.wait_ge(dve_n.sem, dve_n.value("n41"))
                for b in range(2):
                    pe.transpose(ps[:, 7, b * P:(b + 1) * P], ckv[:, b, 0:P], c.base["ident"])
                pe.transpose(ps[:, 7, 2 * P:3 * P], kpe[:, 0:P], c.base["ident"]).then_inc(done, 1)

            @block.scalar
            def _(act):
                def take(b):
                    act.wait_ge(prod.sem, prod.value(f"z{b}"))
                    for r, (a, n, _) in enumerate(RANGES):
                        dst = cq[:, b] if b < 3 else ckv[:, b - 3] if b < 5 else kpe
                        nc.scalar.copy(dst[:, a:a + n], ps[:, Z_BANKS[b] + r, 0:n]).then_inc(act_s, 1)

                for b in range(5):
                    take(b)
                    src = cq[:, b, :] if b < 3 else ckv[:, b - 3, 0:T]
                    act.wait_ge(act_n.sem, act_n.value(f"z{b}1"))
                    nc.scalar.activation(sq[:, b, :], src, ACT.Square).then_inc(act_s, 1)
                act.wait_ge(prod.sem, prod.value("cache"))
                nc.scalar.copy(ckv[:, :, T:KEYS], ps[:, 6, 0:2 * P].rearrange("p (b n) -> p b n", b=2)).then_inc(act_s, 1)
                for g, width in ((0, QL), (1, KVL)):
                    act.wait_ge(prod.sem, prod.value("sq" if g == 0 else "skv"))
                    for r, (a, n, _) in enumerate(RANGES):
                        nc.scalar.activation(rq[:, g, a:a + n], ps[:, SUM_BANKS[g] + r, 0:n], ACT.Sqrt,
                                             bias=c.eps[:, :], scale=1.0 / width).then_inc(act_s, 1)
                take(5)

            @block.gpsimd
            def _(pool):
                pool.memset(zeros[:, :], 0.0).then_inc(zero_s, 1)

            @block.vector
            def _(dve):
                dve.wait_ge(loaded, 16)
                for i in range(2):
                    dve.tensor_copy(w_kpe2[:, :, i * ROPE:(i + 1) * ROPE], w_in[:, :, QL + KVL:W]).then_inc(dup_s, 1)
                dve.wait_ge(prod.sem, prod.value("cache"))
                dve.tensor_copy(kpe[:, T:KEYS], ps[:, 7, 0:P]).then_inc(dve_s, 1)
                for b in range(5):
                    g = b // 3
                    if b in (0, 3):
                        dve.wait_ge(act_n.sem, act_n.value(f"root{g}1"))
                        dve.reciprocal(rq[:, g, :], rq[:, g, :]).then_inc(dve_s, 1)
                        dve.wait_ge(dve_n.sem, dve_n.value(f"inv{g}"))
                    for a, n, _ in RANGES:
                        t = cq[:, b, a:a + n] if b < 3 else ckv[:, b - 3, a:a + n]
                        dve.scalar_tensor_tensor(out=t, in0=t, scalar=c.cols_b[:, 24 + b:25 + b],
                                                 in1=rq[:, b // 3, a:a + n], op0=ALU.mult, op1=ALU.mult).then_inc(dve_s, 1)
                dve.wait_ge(const_in, 16)
                dve.wait_ge(act_n.sem, act_n.value("z51"))
                dve.tensor_tensor(rope[:, 0, :], kpe[:, SEQ:T], m["rcos"], ALU.mult).then_inc(dve_s, 1)
                dve.wait_ge(prod.sem, prod.value("swap"))
                dve.tensor_tensor(rope[:, 1, :], ps[:, 5, :], m["rsin"], ALU.mult).then_inc(dve_s, 1)
                dve.wait_ge(dve_n.sem, dve_n.value("rs"))
                dve.tensor_tensor(kpe[:, SEQ:T], rope[:, 0, :], rope[:, 1, :], ALU.add).then_inc(dve_s, 1)
                dve.wait_ge(prod.sem, prod.value("rows"))
                dve.tensor_copy(rows[:, :], ps[:, 7, 0:3 * P]).then_inc(dve_s, 1)


def mla_slots(c):
    wq = c.slot(0, 3 * 2 * UQ).rearrange("p (k n) -> p k n", k=3)
    wkv = c.slot(1, 2 * 512).rearrange("p (k h n) -> p k h n", k=2, h=2)
    wo = c.slot(2, 2 * D).rearrange("p (h n) -> p h n", h=2)
    return wq, wkv, wo


def load_mla_in(c, sp, j):
    W = QL + KVL + ROPE
    sp.dma_start(c.ring[:, 3 * SLOT:3 * SLOT + KD * W].rearrange("p (k n) -> p k n", k=KD),
                 c.ops["mla_w_in"][j].rearrange("(k p) n -> p k n", p=P)).then_inc(c.w_in_full, 16)


def load_mla_q(c, sp, j, i):
    wq = mla_slots(c)[0]
    src = c.ops["mla_w_uq"][j].rearrange("(k p) (g h n) -> g p k h n", p=P, h=2, n=UQ)
    for first, width, at in ((0, NOPE, 0), (NOPE, ROPE, 2 * NOPE)):
        for hd in range(2):
            sp.dma_start(wq[:, :, at + hd * width:at + (hd + 1) * width],
                         src[bass.ds(i, 1), :, :, hd, first:first + width].rearrange("a p k n -> (a p) k n"))\
              .then_inc(c.wq_full, 16)


def load_mla_kv(c, sp, j, i):
    sp.dma_start(c.slot(1, 2 * 512).rearrange("p (k n) -> p k n", k=2),
                 c.ops["mla_w_ukv"][j].rearrange("(k p) (g n) -> g p k n", p=P, n=512)[bass.ds(i, 1)]
                 .rearrange("a p k n -> (a p) k n")).then_inc(c.wkv_full, 16)


def load_mla_o(c, sp, j, i):
    sp.dma_start(mla_slots(c)[2], c.ops["mla_w_o"][j].rearrange("(g h p) n -> g p h n", p=P, h=2)[bass.ds(i, 1)]
                 .rearrange("a p h n -> (a p) h n")).then_inc(c.wo_full, 16)


def mla_pairs(c, m, layer, j):
    nc, ops, ps = c.nc, c.ops, c.ps
    cq, ckv, kpe = m["cq"], m["ckv"], m["kpe"]
    UNITS = [(hd, t) for hd in range(2) for t in range(NT)]
    NU = len(UNITS)
    order = ["q0", "q1", "qp", "k0", "qs", "k1", "S0", "S1", "v0", "v1", "v2"]
    for u in range(NU):
        order += ([f"S{u + 2}"] if u + 2 < NU else []) + [f"T{u}"] + (["O0"] if u == NU - 2 else [])
    order += ["O1"] + [f"w{d}" for d in range(KD)]
    bank = {n: 2 * (i % 4) for i, n in enumerate(order)}
    wq, wkv, wo = mla_slots(c)
    act_names = ["q00", "q01", "q10", "q11", "qp0", "qp1", "k0", "k1"]
    for u, (hd, t) in enumerate(UNITS):
        act_names += [f"e{u}"] + {0: ["v0", "v1"], 1: ["v2"]}.get(u, []) + ([f"T{u - 1}"] if u else [])
    act_names += [f"T{NU - 1}"]
    dve_names = ["rc", "rs", "rot"]
    for u, (hd, t) in enumerate(UNITS):
        dve_names += [f"m{u}", f"b{u}"] + ([f"i{u - 1}", f"p{u - 1}"] if u else [])
        dve_names += [f"t{u - 1}"] if u and UNITS[u - 1][1] else []
    dve_names += [f"i{NU - 1}", f"p{NU - 1}", f"t{NU - 1}", "o00", "o01", "o10", "o11"] + [f"x{d}{r}" for d in range(KD) for r in range(2)]
    last = {"q0": ("a", "q01"), "q1": ("a", "q11"), "qp": ("a", "qp1"), "qs": ("v", "rs"), "k0": ("a", "k0"), "k1": ("a", "k1"),
            "v0": ("a", "v0"), "v1": ("a", "v1"), "v2": ("a", "v2"), "O0": ("v", "o01"), "O1": ("v", "o11")}
    last |= {f"S{u}": ("a", f"e{u}") for u in range(NU)}
    last |= {f"w{d}": ("v", f"x{d}1") for d in range(KD)}
    with ExitStack() as st:
        def sb(name, shape):
            return st.enter_context(nc.sbuf_tensor("mla_" + name, shape, F32))

        q, qpe, qraw = sb("q", [P, 2, T]), sb("qpe", [P, T]), sb("qraw", [P, LAT])
        rope = sb("qrope", [P, 2, LAT])
        k, v = sb("k", [P, 2, KEYS]), sb("v", [P, NKT, 2 * VD])
        prob = sb("prob", [P, 3, LKEYS])
        pt = c.h[:, :, :].rearrange("p k n -> p (k n)").rearrange("p (h x n) -> p h x n", h=2, x=5)
        ptc = sb("prob_t_ctx", [P, 2, P])
        o = sb("o", [P, 2, T])
        mx, bias, den, inv = (sb(n, [P, NU]) for n in ("max", "bias", "den", "inv"))
        fq, fkv, fo = c.wq_full, c.wkv_full, c.wo_full
        done, act_s, dve_s = sems(nc, st, "mla", ["products", "act", "dve"])
        prod = Steps(done, order)
        act_n, dve_n = Steps(act_s, act_names, 1), Steps(dve_s, dve_names, 5)
        by = {"a": act_n, "v": dve_n}
        gate = c.mod[:, layer, 16:24, :]
        with nc.Block(no_gpsimd_drain=True) as block:
            @block.sync
            def _(sp):
                with sp.Fori(0, PAIRS - 1) as i:
                    sp.wait_ge(prod.sem, prod.value("qp", i))
                    load_mla_q(c, sp, j, i + 1)
                    sp.wait_ge(prod.sem, prod.value("v2", i))
                    load_mla_kv(c, sp, j, i + 1)
                    sp.wait_ge(prod.sem, prod.value(f"w{KD - 1}", i))
                    load_mla_o(c, sp, j, i + 1)

            @block.tensor
            def _(pe):
                def two_ranges(name, mms, i):
                    for r, (a, n, _) in enumerate(RANGES):
                        for x, (lhs, rhs) in enumerate(mms):
                            mm = pe.matmul(ps[:, bank[name] + r, 0:n], lhs, rhs[:, a:a + n],
                                           start=(x == 0), stop=(x == len(mms) - 1))
                    mm.then_inc(done, 1)

                def free(name, i):
                    g = order.index(name) - 4
                    if g >= 0:
                        old = order[g]
                        if old[0] == "T":
                            u = int(old[1:])
                            pe.wait_ge(act_n.sem, act_n.value(f"T{u}", i))
                            if UNITS[u][1]:
                                pe.wait_ge(dve_n.sem, dve_n.value(f"t{u}", i))
                        else:
                            e, s = last[old]
                            pe.wait_ge(by[e].sem, by[e].value(s, i))

                def scores(u, i):
                    hd, t = UNITS[u]
                    free(f"S{u}", i)
                    b = bank[f"S{u}"]
                    half = slice(hd * ROPE, (hd + 1) * ROPE)
                    cols = slice(t * P, (t + 1) * P)
                    spans = [(0, SEQ)] if t == 0 else [(SEQ, LKEYS // 2), (SEQ + LKEYS // 2, LKEYS // 2)]
                    for r, (a, n) in enumerate(spans):
                        pe.matmul(ps[:, b + r, 0:n], q[:, hd, cols], k[:, hd, a:a + n], start=True, stop=False)
                        mm = pe.matmul(ps[:, b + r, 0:n], qpe[half, cols], kpe[half, a:a + n], start=False, stop=True)
                    mm.then_inc(done, 1)

                def turn(u, i):
                    hd, t = UNITS[u]
                    free(f"T{u}", i)
                    b = bank[f"T{u}"]
                    pe.wait_ge(dve_n.sem, dve_n.value(f"p{u}", i))
                    for x in range(1 if t == 0 else 5):
                        mm = pe.transpose(ps[:, b + x // 4, (x % 4) * P:(x % 4 + 1) * P],
                                          prob[:, u % 3, x * P:(x + 1) * P], c.base["ident"])
                    mm.then_inc(done, 1)

                def attend(hd, i):
                    free(f"O{hd}", i)
                    b, u = bank[f"O{hd}"], hd * NT + NT - 1
                    pe.wait_ge(act_n.sem, act_n.value(f"T{u}", i))
                    pe.wait_ge(dve_n.sem, dve_n.value(f"t{u}", i))
                    vh = slice(hd * VD, (hd + 1) * VD)
                    pe.matmul(ps[:, b, 0:P], v[:, 0, vh], ptc[:, hd, :], start=True, stop=True)
                    for x in range(5):
                        mm = pe.matmul(ps[:, b + 1, :], v[:, 1 + x, vh], pt[:, hd, x, :], start=(x == 0), stop=(x == 4))
                    mm.then_inc(done, 1)

                with pe.Fori(0, PAIRS) as i:
                    pe.wait_ge(fq, (i + 1) * 64)
                    pe.wait_ge(act_n.sem, act_n.before(i))
                    for hd in range(2):
                        pe.wait_ge(dve_n.sem, dve_n.before(i) - (4 - 2 * hd))
                        two_ranges(f"q{hd}", [(wq[:, b, hd * NOPE:(hd + 1) * NOPE], cq[:, b, :]) for b in range(3)], i)
                    pe.wait_ge(dve_n.sem, dve_n.before(i))
                    two_ranges("qp", [(wq[:, b, 2 * NOPE:2 * UQ], cq[:, b, :]) for b in range(3)], i)
                    pe.wait_ge(fkv, (i + 1) * 16)

                    def keys(hd):
                        for r in range(2):
                            for b in range(2):
                                mm = pe.matmul(ps[:, bank[f"k{hd}"] + r, 0:KEYS // 2], wkv[:, b, hd, 0:NOPE],
                                               ckv[:, b, r * KEYS // 2:(r + 1) * KEYS // 2], start=(b == 0), stop=(b == 1))
                        mm.then_inc(done, 1)

                    keys(0)
                    pe.wait_ge(act_n.sem, act_n.value("qp1", i))
                    pe.matmul(ps[:, bank["qs"], :], m["swap"], qraw[:, :], start=True, stop=True).then_inc(done, 1)
                    free("k1", i)
                    keys(1)
                    pe.wait_ge(act_n.sem, act_n.value("k1", i))
                    scores(0, i)
                    pe.wait_ge(dve_n.sem, dve_n.value("rot", i))
                    scores(1, i)
                    for g in range(3):
                        free(f"v{g}", i)
                        for r in range(2):
                            t = 2 * g + r
                            for b in range(2):
                                mm = pe.matmul(ps[:, bank[f"v{g}"] + r, 0:2 * VD], ckv[:, b, t * P:(t + 1) * P],
                                               wkv[:, b, :, NOPE:2 * NOPE], start=(b == 0), stop=(b == 1))
                        mm.then_inc(done, 1)
                    for u in range(NU):
                        if u + 2 < NU:
                            scores(u + 2, i)
                        turn(u, i)
                        if u == NU - 2:
                            attend(0, i)
                    attend(1, i)
                    pe.wait_ge(fo, (i + 1) * 16)
                    for d in range(KD):
                        if d == 0:
                            pe.wait_ge(act_n.sem, act_n.value(f"T{NU - 2}", i))
                        else:
                            free(f"w{d}", i)
                        for hd in range(2):
                            if d == 0:
                                pe.wait_ge(dve_n.sem, dve_n.value(f"o{hd}1", i))
                            for r, (a, n, _) in enumerate(RANGES):
                                mm = pe.matmul(ps[:, bank[f"w{d}"] + r, 0:n], wo[:, hd, d * P:(d + 1) * P], o[:, hd, a:a + n],
                                               start=(hd == 0), stop=(hd == 1))
                        mm.then_inc(done, 1)

            @block.scalar
            def _(act):
                def take_turned(u, i):
                    hd, t = UNITS[u]
                    act.wait_ge(prod.sem, prod.value(f"T{u}", i))
                    b = bank[f"T{u}"]
                    if t == 0:
                        nc.scalar.copy(ptc[:, hd, :], ps[:, b, 0:P]).then_inc(act_s, 1)
                    else:
                        nc.scalar.copy(pt[:, hd, 0:4, (t - 1) * P:t * P],
                                       ps[:, b, :].rearrange("p (x n) -> p x n", x=4)).then_inc(act_s, 1)

                act.sem_inc(act_s, 1)
                with act.Fori(0, PAIRS) as i:
                    for hd in range(2):
                        act.wait_ge(prod.sem, prod.value(f"q{hd}", i))
                        for r, (a, n, _) in enumerate(RANGES):
                            nc.scalar.copy(q[:, hd, a:a + n], ps[:, bank[f"q{hd}"] + r, 0:n]).then_inc(act_s, 1)
                    act.wait_ge(prod.sem, prod.value("qp", i))
                    nc.scalar.copy(qpe[:, 0:SEQ], ps[:, bank["qp"], 0:SEQ]).then_inc(act_s, 1)
                    nc.scalar.copy(qraw[:, :], ps[:, bank["qp"] + 1, :]).then_inc(act_s, 1)
                    for hd in range(2):
                        act.wait_ge(prod.sem, prod.value(f"k{hd}", i))
                        nc.scalar.copy(k[:, hd, :].rearrange("p (r n) -> p r n", r=2),
                                       ps[:, bank[f"k{hd}"]:bank[f"k{hd}"] + 2, 0:KEYS // 2]).then_inc(act_s, 1)

                    def take_v(g):
                        act.wait_ge(prod.sem, prod.value(f"v{g}", i))
                        nc.scalar.copy(v[:, 2 * g:2 * g + 2, :],
                                       ps[:, bank[f"v{g}"]:bank[f"v{g}"] + 2, 0:2 * VD]).then_inc(act_s, 1)

                    for u, (hd, t) in enumerate(UNITS):
                        b = bank[f"S{u}"]
                        act.wait_ge(dve_n.sem, dve_n.value(f"b{u}", i))
                        if u >= 3:
                            act.wait_ge(prod.sem, prod.value(f"T{u - 3}", i))
                        src = ps[:, b, 0:SEQ] if t == 0 else ps[:, b:b + 2, 0:LKEYS // 2]
                        dst = prob[:, u % 3, 0:SEQ] if t == 0 else prob[:, u % 3, :].rearrange("p (r n) -> p r n", r=2)
                        nc.scalar.activation(dst, src, ACT.Exp, bias=bias[:, u:u + 1], scale=MLA_SCALE,
                                             accum_out=den[:, u:u + 1]).then_inc(act_s, 1)
                        for g in {0: (0, 1), 1: (2,)}.get(u, ()):
                            take_v(g)
                        if u:
                            take_turned(u - 1, i)
                    take_turned(NU - 1, i)

            @block.vector
            def _(dve):
                def normalise(u, i):
                    hd, t = UNITS[u]
                    n = SEQ if t == 0 else LKEYS
                    dve.wait_ge(act_n.sem, act_n.value(f"e{u}", i))
                    dve.reciprocal(inv[:, u:u + 1], den[:, u:u + 1]).then_inc(dve_s, 1)
                    dve.wait_ge(dve_n.sem, dve_n.value(f"i{u}", i))
                    dve.tensor_scalar(prob[:, u % 3, 0:n], prob[:, u % 3, 0:n], inv[:, u:u + 1], None,
                                      ALU.mult).then_inc(dve_s, 1)

                def take_last(u, i):
                    hd, t = UNITS[u]
                    dve.wait_ge(prod.sem, prod.value(f"T{u}", i))
                    dve.tensor_copy(pt[:, hd, 4, (t - 1) * P:t * P], ps[:, bank[f"T{u}"] + 1, 0:P]).then_inc(dve_s, 1)

                def take_o(hd, i):
                    dve.wait_ge(prod.sem, prod.value(f"O{hd}", i))
                    for r, (a, n, _) in enumerate(RANGES):
                        dve.tensor_copy(o[:, hd, a:a + n], ps[:, bank[f"O{hd}"] + r, 0:n]).then_inc(dve_s, 1)

                dve.sem_inc(dve_s, 5)
                with dve.Fori(0, PAIRS) as i:
                    dve.wait_ge(act_n.sem, act_n.value("qp1", i))
                    dve.tensor_tensor(rope[:, 0, :], qraw[:, :], m["rcos"], ALU.mult).then_inc(dve_s, 1)
                    dve.wait_ge(prod.sem, prod.value("qs", i))
                    dve.tensor_tensor(rope[:, 1, :], ps[:, bank["qs"], :], m["rsin"], ALU.mult).then_inc(dve_s, 1)
                    dve.wait_ge(dve_n.sem, dve_n.value("rs", i))
                    dve.tensor_tensor(qpe[:, SEQ:T], rope[:, 0, :], rope[:, 1, :], ALU.add).then_inc(dve_s, 1)
                    for u, (hd, t) in enumerate(UNITS):
                        b = bank[f"S{u}"]
                        dve.wait_ge(prod.sem, prod.value(f"S{u}", i))
                        if t == 0:
                            dve.tensor_reduce(mx[:, u:u + 1], ps[:, b, 0:SEQ], AX.X, ALU.max).then_inc(dve_s, 1)
                        else:
                            dve.tensor_reduce(mx[:, u:u + 1], ps[:, b:b + 2, 0:LKEYS // 2], AX.XY, ALU.max).then_inc(dve_s, 1)
                        dve.wait_ge(dve_n.sem, dve_n.value(f"m{u}", i))
                        dve.tensor_scalar(bias[:, u:u + 1], mx[:, u:u + 1], -MLA_SCALE, None, ALU.mult).then_inc(dve_s, 1)
                        if u:
                            normalise(u - 1, i)
                            if UNITS[u - 1][1]:
                                take_last(u - 1, i)
                    normalise(NU - 1, i)
                    take_last(NU - 1, i)
                    take_o(0, i)
                    take_o(1, i)
                    for d in range(KD):
                        dve.wait_ge(prod.sem, prod.value(f"w{d}", i))
                        for r, (a, n, jc) in enumerate(RANGES):
                            dve.scalar_tensor_tensor(out=c.x[:, d, a:a + n], in0=ps[:, bank[f"w{d}"] + r, 0:n],
                                                     scalar=gate[:, d, jc:jc + 1], in1=c.x[:, d, a:a + n],
                                                     op0=ALU.mult, op1=ALU.add).then_inc(dve_s, 1)


QK, V, F, B = 0, KD, 2 * KD, 3 * KD
RET_FULL = {QK: (0, 48, 32), F: (0, 48, 48), V: (1, 32, 16), B: (1, 32, 32)}


def ret_slots(c):
    w_in = [c.slot(s).rearrange("p (k n) -> p k n", k=KD) for s in range(2)]
    w_out = c.slot(2).rearrange("p (b n) -> p b n", b=4)
    states = c.ring[:, 3 * SLOT:3 * SLOT + 2048].rearrange("p (f b n) -> p f b n", f=2, b=2)
    trig = c.ring[:, 3 * SLOT + 2048:3 * SLOT + 2048 + 3 * LAT]
    expo = c.ring[:, 3 * SLOT + 2048 + 3 * LAT:4 * SLOT]
    return w_in, w_out, states, trig, expo


def load_ret_in(c, sp, j, sweep, i):
    s = RET_FULL[sweep][0]
    w = ret_slots(c)[0][s]
    w3 = c.ops["ret_w_in"][j].rearrange("(k p) n -> p k n", p=P)
    if sweep == QK:
        for x in range(2):
            sp.dma_start(w[:, :, x * DK:(x + 1) * DK], w3[:, :, bass.ds(i * DK + x * RH * DK, DK)]).then_inc(c.ret_full[s], 16)
    else:
        first = 2 * RH * DK + {V: 0, F: 1, B: 2}[sweep] * RH * DV
        sp.dma_start(w, w3[:, :, bass.ds(i * DV + first, DV)]).then_inc(c.ret_full[s], 16)


def load_ret_state(c, sp, j, i):
    src = c.ops["state_ret"][0, j].rearrange("f h (b p) n -> h f b p n", p=P)
    for f in range(2):
        for b in range(2):
            sp.dma_start(ret_slots(c)[2][:, f, b, :], src[bass.ds(i, 1), f, b].rearrange("a p n -> (a p) n")).then_inc(c.ret_full[3], 16)


def load_ret_out(c, sp, j, i):
    sp.dma_start(ret_slots(c)[1], c.ops["ret_w_o"][j].rearrange("(h b p) n -> h p b n", p=P, b=4)[bass.ds(i, 1)]
                 .rearrange("a p b n -> (a p) b n")).then_inc(c.ret_full[2], 16)


def load_ret_first(c, sp, j, consts):
    load_ret_in(c, sp, j, QK, 0)
    sp.dma_start(consts, c.ops["ret_consts"]).then_inc(c.ret_full[3], 16)
    sp.dma_start(ret_slots(c)[3], c.ops["trig_consts"]).then_inc(c.ret_full[3], 16)
    load_ret_in(c, sp, j, V, 0)
    load_ret_state(c, sp, j, 0)
    load_ret_out(c, sp, j, 0)


def retention(c, layer, j, consts, hh, hl):
    nc, ops, ps = c.nc, c.ops, c.ps
    UN, BUF = 4 * KD, 2
    HALF = T // 2
    V_BANKS, KC_BANK, F_BANKS, B_BANKS, STATE_BANKS = (0, 1, 2, 3, 4), 7, (5, 6, 0, 1, 2), (3, 4, 5, 6, 0), (1, 2)
    paired = ["sc", "s0", "s1", "s2", "s3"]
    paired += [f"o{t}" for t in range(NT)] + [f"y{t}" for t in range(NT)] + [f"w{d}" for d in range(KD)]
    order = ["kc", "fs", "bs"] + paired
    order.insert(order.index("y3"), "wc")

    def bank(name, r=0):
        return (1 + 2 * (paired.index(name) % 4) + r) % 8

    last = {"sc": ("v", "scb")}
    last |= {f"s{x}": ("v", f"s{x}b") for x in range(4)}
    last |= {f"o{t}": ("v", f"o{t}b") for t in range(NT)}
    last |= {f"y{t}": ("a", f"y{t}") for t in range(NT)}
    last |= {f"w{d}": ("v", f"x{d}") for d in range(KD)}
    before_paired = {"sc": ("v", "bs"), "s0": ("a", "b0"), "s1": ("a", "b2"), "s2": ("v", "kb")}
    act_names = ["df", "db", "kdf", "kdb", "ef", "eb", "q00", "q01", "q10", "q11", "k00", "k01", "k10", "k11"]
    act_names += [f"{g}{t}" for g in "fb" for t in range(NT)]
    act_names += [f"o{t}{r}" for t in range(NT) for r in "fb"] + [f"y{t}" for t in range(NT)]
    dve_names = ["lg", "idxb", "tf", "tb"] + [f"q{x}" for x in range(6)] + ["qf0", "qf1"]
    dve_names += ["v0", "v1", "v2", "v3", "v4", "kf", "kb", "fs", "bs", "scf", "scb"]
    dve_names += [f"s{x}{r}" for x in range(3) for r in "fb"] + ["qb0", "qb1", "s3f", "s3b"]
    for t in range(NT + 1):
        if t < NT:
            dve_names += [f"m{t}"]
        if t:
            dve_names += [f"o{t - 1}f", f"o{t - 1}b", f"y{t - 1}"]
    dve_names += [f"xc{d}" for d in range(KD)] + [f"x{d}" for d in range(KD)]
    pool_names = [f"k{x}" for x in range(6)] + [f"r{t}" for t in range(NT)]
    with ExitStack() as st:
        def sb(name, shape, dt=F32):
            return st.enter_context(nc.sbuf_tensor("ret_" + name, shape, dt))

        m = _views(consts, RET_COLS)
        win, wo, s0, trig, expo = ret_slots(c)
        m.update(_views(trig, TRIG_COLS))
        at = 4 * SLOT

        def results(*shape):
            nonlocal at
            n, at = int(np.prod(shape)), at + int(np.prod(shape))
            assert at <= 6 * SLOT
            flat = c.ring[:, at - n:at]
            return flat.rearrange("p (a n) -> p a n", a=shape[0]) if len(shape) == 2 else flat

        v, q, k, ss = results(NT, DV), results(2, T), results(2, T), results(4, T)
        idxb = results(LAT)
        junk = idxb
        flat_h = c.h[:, :, :].rearrange("p k n -> p (k n)")
        gf, gb = (flat_h[:, f * NT * DV:(f + 1) * NT * DV].rearrange("p (t n) -> p t n", t=NT) for f in range(2))
        yt = v[:, :, :].rearrange("p t n -> p (t n)").rearrange("p (b n) -> p b n", b=4)
        whi, wlo = sb("w_hi", [P, BUF, 512], F32R), sb("w_lo", [P, BUF, 512], F32R)
        dec = sb("decay", [P, 2, LAT])
        kc = sb("k_ctx_rows", [P, 2, DK])
        sctx = kc[:, :, 0:P]
        stage = sb("new_state", [P, 2, DV])
        qd = sb("q_decayed", [P, 2, LAT])
        kd, lg = sb("k_decay", [P, 2]), sb("log_decay", [P, 2])
        sumsq, mean, rs, half = sb("sumsq", [P, NT, 2]), sb("meansq", [P, NT, 2]), sb("rstd", [P, NT, 2]), sb("minus_half", [P, 2])
        tmp = ss[:, :, :].rearrange("p t n -> p (t n)")[:, 0:4 * LAT].rearrange("p (x n) -> p x n", x=4)
        full = c.ret_full
        w_hi, w_lo, used = sems(nc, st, "ret", ["w_hi", "w_lo", "w_used"])
        prep, done, act_s, dve_s, pool_s, store_s = sems(nc, st, "ret", ["minus_half", "products", "act", "dve", "pool", "stored"])
        prod, act_n, dve_n, pool_n = Steps(done, order), Steps(act_s, act_names, 1), Steps(dve_s, dve_names, 4), Steps(pool_s, pool_names)
        by = {"a": act_n, "v": dve_n}
        gate = c.mod[:, layer, 16:24, :]
        with nc.Block(no_gpsimd_drain=True) as block:
            @block.sync
            def _(sp):
                def split_done(sweep, i):
                    sp.wait_ge(w_lo, i * UN + (sweep + KD))

                def store_state(f, i):
                    sp.wait_ge(dve_n.sem, dve_n.value(("fs", "bs")[f], i))
                    dst = ops["new_state"][0, j, f].rearrange("h (b p) n -> h p b n", p=P)
                    sp.dma_start(dst[bass.ds(i, 1)].rearrange("a p b n -> (a p) b n"), stage[:, :, :]).then_inc(store_s, 16)

                sp.sem_inc(store_s, 16)
                with sp.Fori(0, RH - 1) as i:
                    split_done(QK, i)
                    load_ret_in(c, sp, j, F, i)
                    split_done(V, i)
                    load_ret_in(c, sp, j, B, i)
                    split_done(F, i)
                    load_ret_in(c, sp, j, QK, i + 1)
                    store_state(0, i)
                    store_state(1, i)
                    split_done(B, i)
                    load_ret_in(c, sp, j, V, i + 1)
                    sp.wait_ge(prod.sem, prod.value(f"o{NT - 1}", i))
                    load_ret_state(c, sp, j, i + 1)
                    sp.wait_ge(prod.sem, prod.value(f"w{KD - 1}", i))
                    load_ret_out(c, sp, j, i + 1)
                split_done(QK, RH - 1)
                load_ret_in(c, sp, j, F, RH - 1)
                split_done(V, RH - 1)
                load_ret_in(c, sp, j, B, RH - 1)
                store_state(0, RH - 1)
                store_state(1, RH - 1)
                sp.wait_ge(store_s, RH * 32 + 16)

            @block.gpsimd
            def _(pool):
                pool.memset(half[:, :], -0.5).then_inc(prep, 1)
                pool.wait_ge(full[3], 96)
                with pool.Fori(0, RH) as i:
                    pool.wait_ge(act_n.sem, act_n.value("k11", i))
                    k1, k2 = k[:, 0, SEQ:T], k[:, 1, SEQ:T]
                    pool.tensor_tensor(tmp[:, 0, :], k1, m["sin"], ALU.mult).then_inc(pool_s, 1)
                    pool.tensor_tensor(tmp[:, 1, :], k2, m["sin"], ALU.mult).then_inc(pool_s, 1)
                    pool.wait_ge(pool_n.sem, pool_n.value("k1", i))
                    pool.tensor_tensor(k1, k1, m["cos"], ALU.mult).then_inc(pool_s, 1)
                    pool.tensor_tensor(k2, k2, m["cos"], ALU.mult).then_inc(pool_s, 1)
                    pool.wait_ge(pool_n.sem, pool_n.value("k3", i))
                    pool.tensor_tensor(k1, k1, tmp[:, 1, :], ALU.subtract).then_inc(pool_s, 1)
                    pool.tensor_tensor(k2, k2, tmp[:, 0, :], ALU.add).then_inc(pool_s, 1)
                    for t in range(NT):
                        pool.wait_ge(prep, 1)
                        pool.wait_ge(dve_n.sem, dve_n.value(f"m{t}", i))
                        pool.tensor_tensor(rs[:, t, :], mean[:, t, :], half[:, :], ALU.pow).then_inc(pool_s, 1)

            @block.tensor
            def _(pe):
                def free(name, i):
                    g = paired.index(name) - 4
                    e, s = before_paired[name] if g < 0 else last[paired[g]]
                    pe.wait_ge(by[e].sem, by[e].value(s, i))

                def three(out, hi, lo, k):
                    for x, (lhs, rhs) in enumerate(((hi[0], hi[1]), (hi[0], lo[1]), (lo[0], hi[1]))):
                        mm = pe.matmul(out, lhs, rhs, start=(k == 0 and x == 0), stop=(k == KD - 1 and x == 2))
                    return mm

                def rows_of(sweep, banks, taken, i, ks=range(KD)):
                    for k in ks:
                        w = (sweep + k) % BUF
                        pe.wait_ge(w_lo, i * UN + (sweep + k + 1))
                        for t in range(NT):
                            if k == 0:
                                e, s = taken[t]
                                pe.wait_ge(by[e].sem, by[e].value(s, i))
                            cols = slice(t * P, (t + 1) * P)
                            mm = three(ps[:, banks[t], :], (hh[:, k, cols], whi[:, w, :]), (hl[:, k, cols], wlo[:, w, :]), k)
                        mm.then_inc(used, 1)

                pe.sem_inc(used, BUF)
                with pe.Fori(0, RH) as i:
                    pe.wait_ge(act_n.sem, act_n.before(i))
                    for kk in range(KD):
                        w = (QK + kk) % BUF
                        pe.wait_ge(w_lo, i * UN + (QK + kk + 1))
                        for x in range(4):
                            cols = slice(x * P, (x + 1) * P)
                            for r in range(2):
                                if kk == 0 and r == 1:
                                    pe.wait_ge(dve_n.sem, dve_n.before(i) - (2, 1, 0, 0)[x])
                                half_t = slice(r * HALF, (r + 1) * HALF)
                                mm = three(ps[:, 2 * x + r, 0:HALF], (whi[:, w, cols], hh[:, kk, half_t]),
                                           (wlo[:, w, cols], hl[:, kk, half_t]), kk)
                        mm.then_inc(used, 1)
                    rows_of(V, V_BANKS, [("a", n) for n in ("q00", "q01", "q10", "q11", "k00")], i)
                    pe.wait_ge(act_n.sem, act_n.value("k11", i))
                    for b in range(2):
                        mm = pe.transpose(ps[:, KC_BANK, b * P:(b + 1) * P], k[:, b, 0:P], c.base["ident"])
                    mm.then_inc(done, 1)
                    rows_of(F, F_BANKS, [("a", "k01"), ("a", "k10"), ("v", "v0"), ("v", "v1"), ("v", "v2")], i)

                    def new_state(f, name, taken):
                        e, s = taken
                        pe.wait_ge(by[e].sem, by[e].value(s, i))
                        for b in range(2):
                            mm = pe.matmul(ps[:, STATE_BANKS[b], :], kc[:, f, b * P:(b + 1) * P], v[:, 0, :], start=True, stop=True)
                        mm.then_inc(done, 1)

                    b_taken = [("v", "v3"), ("v", "v4"), ("a", "f0"), ("a", "f1"), ("a", "f2")]
                    rows_of(B, B_BANKS, b_taken, i, range(0, 2))
                    pe.wait_ge(dve_n.sem, dve_n.value("kb", i))
                    new_state(0, "fs", ("a", "f4"))
                    rows_of(B, B_BANKS, b_taken, i, range(2, 6))
                    new_state(1, "bs", ("v", "fs"))
                    rows_of(B, B_BANKS, b_taken, i, range(6, KD))
                    free("sc", i)
                    for b in range(2):
                        mm = pe.matmul(ps[:, bank("sc"), 0:P], k[:, b, 0:P], q[:, b, 0:P], start=(b == 0), stop=(b == 1))
                    mm.then_inc(done, 1)
                    pe.wait_ge(pool_n.sem, pool_n.value("k5", i))
                    pe.wait_ge(dve_n.sem, dve_n.value("q5", i))
                    for x in range(4):
                        free(f"s{x}", i)
                        for b in range(2):
                            mm = pe.matmul(ps[:, bank(f"s{x}"), :], k[:, b, SEQ + x * P:SEQ + (x + 1) * P], q[:, b, SEQ:T],
                                           start=(b == 0), stop=(b == 1))
                        mm.then_inc(done, 1)
                    pe.wait_ge(full[3], i * 64 + 96)
                    for t in range(NT):
                        free(f"o{t}", i)
                        pe.wait_ge(act_n.sem, act_n.value(("b1", "b3", "b4", "b4", "b4")[t], i))
                        pe.wait_ge(dve_n.sem, dve_n.value("s3b" if t else "scb", i))
                        for f in range(2):
                            out = ps[:, bank(f"o{t}", f), :]
                            if t == 0:
                                mm = pe.matmul(out, sctx[:, f, :], v[:, 0, :], start=True, stop=True)
                                continue
                            n = t - 1
                            mms = [(ss[:, x, (n + 1 - f) * P:(n + 2 - f) * P], v[:, 1 + x, :])
                                   for x in (range(n + 1) if f == 0 else range(n, 4))]
                            qq = qd if f == 0 else q[:, :, SEQ:T]
                            mms += [(qq[:, b, n * P:(n + 1) * P], s0[:, f, b, :]) for b in range(2)]
                            for x, (lhs, rhs) in enumerate(mms):
                                mm = pe.matmul(out, lhs, rhs, start=(x == 0), stop=(x == len(mms) - 1))
                        mm.then_inc(done, 1)
                    def turn_y(t):
                        free(f"y{t}", i)
                        pe.wait_ge(dve_n.sem, dve_n.value(f"y{t}", i))
                        for b in range(4):
                            mm = pe.transpose(ps[:, bank(f"y{t}"), b * P:(b + 1) * P], gf[:, t, b * P:(b + 1) * P], c.base["ident"])
                        mm.then_inc(done, 1)

                    for t in range(3):
                        turn_y(t)
                    pe.wait_ge(full[2], (i + 1) * 16)
                    pe.wait_ge(act_n.sem, act_n.value("y0", i))
                    for d in range(KD):
                        for b in range(4):
                            mm = pe.matmul(ps[:, bank(f"y{d // 4}", 1), (d % 4) * P:(d % 4 + 1) * P], wo[:, b, d * P:(d + 1) * P],
                                           yt[:, b, 0:SEQ], start=(b == 0), stop=(b == 3))
                    mm.then_inc(done, 1)
                    turn_y(3)
                    turn_y(4)
                    pe.wait_ge(act_n.sem, act_n.value(f"y{NT - 1}", i))
                    for d in range(KD):
                        free(f"w{d}", i)
                        for b in range(4):
                            mm = pe.matmul(ps[:, bank(f"w{d}"), :], wo[:, b, d * P:(d + 1) * P], yt[:, b, SEQ:T],
                                           start=(b == 0), stop=(b == 3))
                        mm.then_inc(done, 1)

            @block.scalar
            def _(act):
                act.wait_ge(full[3], 96)
                act.sem_inc(act_s, 1)
                with act.Fori(0, RH) as i:
                    def split(sweep, *ks):
                        s, per, count = RET_FULL[sweep]
                        for k in ks:
                            n = sweep + k
                            act.wait_ge(full[s], i * per + count)
                            act.wait_ge(used, i * UN + (n + 1))
                            nc.scalar.activation(whi[:, n % BUF, :], win[s][:, k, :], ACT.Identity).then_inc(w_hi, 1)

                    def take(name, x, r):
                        half_t = slice(r * HALF, (r + 1) * HALF)
                        nc.scalar.activation((q, k)[x // 2][:, x % 2, half_t], ps[:, 2 * x + r, 0:HALF], ACT.Identity,
                                             scale=1.0 if x < 2 else KSCALE).then_inc(act_s, 1)

                    def gates(g, banks, ts):
                        for t in ts:
                            nc.scalar.activation(g[:, t, :], ps[:, banks[t], :], ACT.Silu).then_inc(act_s, 1)

                    split(QK, 0, 1)
                    act.wait_ge(dve_n.sem, dve_n.value("lg", i))
                    nc.scalar.activation(dec[:, 0, :], m["relf"], ACT.Exp, scale=lg[:, 0:1]).then_inc(act_s, 1)
                    nc.scalar.activation(dec[:, 1, :], m["relb"], ACT.Exp, scale=lg[:, 1:2]).then_inc(act_s, 1)
                    nc.scalar.activation(kd[:, 0:1], m["kf"], ACT.Exp, scale=lg[:, 0:1]).then_inc(act_s, 1)
                    nc.scalar.activation(kd[:, 1:2], m["kb"], ACT.Exp, scale=lg[:, 1:2]).then_inc(act_s, 1)
                    nc.scalar.activation(expo, m["idxf"], ACT.Exp, scale=lg[:, 0:1]).then_inc(act_s, 1)
                    act.wait_ge(dve_n.sem, dve_n.value("idxb", i))
                    nc.scalar.activation(idxb, idxb, ACT.Exp, scale=lg[:, 1:2]).then_inc(act_s, 1)
                    split(QK, *range(2, KD))
                    split(V, 0)
                    act.wait_ge(used, i * UN + (QK + KD + BUF))
                    take("q0", 0, 0)
                    take("q0", 0, 1)
                    take("q1", 1, 0)
                    take("q1", 1, 1)
                    take("k0", 2, 0)
                    split(V, 1)
                    take("k0", 2, 1)
                    take("k1", 3, 0)
                    take("k1", 3, 1)
                    split(V, *range(2, KD))
                    split(F, *range(KD))
                    split(B, 0)
                    act.wait_ge(used, i * UN + (F + KD + BUF))
                    gates(gf, F_BANKS, (0, 1, 2))
                    split(B, 1)
                    gates(gf, F_BANKS, (3, 4))
                    split(B, *range(2, KD))
                    act.wait_ge(used, i * UN + (B + KD + BUF))
                    gates(gb, B_BANKS, range(NT))
                    act.wait_ge(dve_n.sem, dve_n.value("qb1", i))
                    for t in range(NT):
                        act.wait_ge(prod.sem, prod.value(f"o{t}", i))
                        for f in range(2):
                            act.wait_ge(act_n.sem, act_n.value(f"o{t}f", i) - 1 + f)
                            nc.scalar.activation(junk, ps[:, bank(f"o{t}", f), :], ACT.Square,
                                                 accum_out=sumsq[:, t, f:f + 1]).then_inc(act_s, 1)
                    for t in range(NT):
                        act.wait_ge(prod.sem, prod.value(f"y{t}", i))
                        nc.scalar.copy(yt[:, :, t * P:(t + 1) * P],
                                       ps[:, bank(f"y{t}"), :].rearrange("p (b n) -> p b n", b=4)).then_inc(act_s, 1)

            @block.vector
            def _(dve):
                dve.wait_ge(full[3], 96)
                dve.sem_inc(dve_s, 4)
                with dve.Fori(0, RH) as i:
                    def split(sweep, *ks):
                        s = RET_FULL[sweep][0]
                        for k in ks:
                            n = sweep + k
                            dve.wait_ge(w_hi, i * UN + (n + 1))
                            dve.tensor_tensor(wlo[:, n % BUF, :], win[s][:, k, :], whi[:, n % BUF, :].bitcast(F32),
                                              ALU.subtract).then_inc(w_lo, 1)

                    def take_state(n, f):
                        dve.wait_ge(prod.sem, prod.value(n, i))
                        dve.wait_ge(store_s, i * 32 + 16 * (f + 1))
                        dve.tensor_copy(stage[:, :, :], ps[:, STATE_BANKS[0]:STATE_BANKS[0] + 2, :]).then_inc(dve_s, 1)

                    def take_scores(x):
                        s = ps[:, bank(f"s{x}"), :]
                        dve.tensor_tensor(ss[:, x, (x + 1) * P:T], s[:, x * P:LAT], dec[:, 0, 0:LAT - x * P], ALU.mult).then_inc(dve_s, 1)
                        dve.tensor_tensor(ss[:, x, 0:(x + 1) * P], s[:, 0:(x + 1) * P], dec[:, 1, LAT - (x + 1) * P:LAT],
                                          ALU.mult).then_inc(dve_s, 1)

                    split(QK, 0)
                    dve.wait_ge(act_n.sem, act_n.before(i))
                    dve.tensor_copy(lg[:, :], c.log_decay[:, bass.ds(i, 1), :].rearrange("p a f -> p (a f)")).then_inc(dve_s, 1)
                    dve.tensor_scalar(idxb, m["idxf"], -1.0, float(LAT + 1), ALU.mult, ALU.add).then_inc(dve_s, 1)
                    split(QK, 1)
                    dve.wait_ge(act_n.sem, act_n.value("db", i))
                    dve.tensor_tensor(dec[:, 0, 0:P], dec[:, 0, 0:P], m["trif"], ALU.mult).then_inc(dve_s, 1)
                    dve.tensor_tensor(dec[:, 1, LAT - P:LAT], dec[:, 1, LAT - P:LAT], m["trib"], ALU.mult).then_inc(dve_s, 1)
                    split(QK, *range(2, KD))
                    split(V, 0, 1, 2)
                    q1, q2 = q[:, 0, SEQ:T], q[:, 1, SEQ:T]
                    dve.wait_ge(act_n.sem, act_n.value("q11", i))
                    dve.tensor_tensor(tmp[:, 2, :], q1, m["sin"], ALU.mult).then_inc(dve_s, 1)
                    dve.tensor_tensor(tmp[:, 3, :], q2, m["sin"], ALU.mult).then_inc(dve_s, 1)
                    split(V, 3)
                    dve.wait_ge(dve_n.sem, dve_n.value("q1", i))
                    dve.tensor_tensor(q1, q1, m["cos"], ALU.mult).then_inc(dve_s, 1)
                    dve.tensor_tensor(q2, q2, m["cos"], ALU.mult).then_inc(dve_s, 1)
                    split(V, 4)
                    dve.wait_ge(dve_n.sem, dve_n.value("q3", i))
                    dve.tensor_tensor(q1, q1, tmp[:, 3, :], ALU.subtract).then_inc(dve_s, 1)
                    dve.tensor_tensor(q2, q2, tmp[:, 2, :], ALU.add).then_inc(dve_s, 1)
                    split(V, 5)
                    dve.wait_ge(act_n.sem, act_n.value("ef", i))
                    dve.wait_ge(dve_n.sem, dve_n.value("q5", i))
                    for b in range(2):
                        dve.tensor_tensor(qd[:, b, :], q[:, b, SEQ:T], expo, ALU.mult).then_inc(dve_s, 1)
                    split(V, 6, 7)
                    split(F, 0)
                    dve.wait_ge(used, i * UN + (V + KD + BUF))
                    for t in range(3):
                        dve.tensor_copy(v[:, t, :], ps[:, V_BANKS[t], :]).then_inc(dve_s, 1)
                    split(F, 1)
                    for t in range(3, NT):
                        dve.tensor_copy(v[:, t, :], ps[:, V_BANKS[t], :]).then_inc(dve_s, 1)
                    dve.wait_ge(prod.sem, prod.value("kc", i))
                    dve.wait_ge(act_n.sem, act_n.value("kdb", i))
                    for f in range(2):
                        dve.tensor_scalar(kc[:, f, :], ps[:, KC_BANK, 0:DK], kd[:, f:f + 1], None, ALU.mult).then_inc(dve_s, 1)
                    split(F, *range(2, KD))
                    split(B, *range(0, 4))
                    take_state("fs", 0)
                    split(B, *range(4, KD))
                    take_state("bs", 1)
                    dve.wait_ge(prod.sem, prod.value("sc", i))
                    dve.wait_ge(dve_n.sem, dve_n.value("tb", i))
                    dve.tensor_tensor(sctx[:, 0, :], ps[:, bank("sc"), 0:P], dec[:, 0, 0:P], ALU.mult).then_inc(dve_s, 1)
                    dve.tensor_tensor(sctx[:, 1, :], ps[:, bank("sc"), 0:P], dec[:, 1, LAT - P:LAT], ALU.mult).then_inc(dve_s, 1)
                    for x in range(3):
                        dve.wait_ge(prod.sem, prod.value(f"s{x}", i))
                        take_scores(x)
                    dve.wait_ge(prod.sem, prod.value("s3", i))
                    dve.wait_ge(act_n.sem, act_n.value("eb", i))
                    for b in range(2):
                        dve.tensor_tensor(q[:, b, SEQ:T], q[:, b, SEQ:T], idxb, ALU.mult).then_inc(dve_s, 1)
                    take_scores(3)
                    for t in range(NT + 1):
                        if t < NT:
                            dve.wait_ge(act_n.sem, act_n.value(f"o{t}b", i))
                            dve.tensor_scalar(mean[:, t, :], sumsq[:, t, :], 1.0 / DV, EPS, ALU.mult, ALU.add).then_inc(dve_s, 1)
                        if t:
                            n = t - 1
                            dve.wait_ge(pool_n.sem, pool_n.value(f"r{n}", i))
                            for f, g in enumerate((gf, gb)):
                                dve.scalar_tensor_tensor(out=g[:, n, :], in0=ps[:, bank(f"o{n}", f), :], scalar=rs[:, n, f:f + 1],
                                                         in1=g[:, n, :], op0=ALU.mult, op1=ALU.mult).then_inc(dve_s, 1)
                            dve.wait_ge(dve_n.sem, dve_n.value(f"o{n}b", i))
                            dve.tensor_tensor(gf[:, n, :], gf[:, n, :], gb[:, n, :], ALU.add).then_inc(dve_s, 1)
                    def add(d, a, n, jc, src):
                        dve.scalar_tensor_tensor(out=c.x[:, d, a:a + n], in0=src, scalar=gate[:, d, jc:jc + 1], in1=c.x[:, d, a:a + n],
                                                 op0=ALU.mult, op1=ALU.add).then_inc(dve_s, 1)

                    dve.wait_ge(prod.sem, prod.value("wc", i))
                    for d in range(KD):
                        add(d, *RANGES[0], ps[:, bank(f"y{d // 4}", 1), (d % 4) * P:(d % 4 + 1) * P])
                    for d in range(KD):
                        dve.wait_ge(prod.sem, prod.value(f"w{d}", i))
                        add(d, *RANGES[1], ps[:, bank(f"w{d}"), :])


def route(c, layer):
    nc, ps = c.nc, c.ps
    G = NT * NG
    with ExitStack() as st:
        def sb(name, shape, dt=F32):
            return st.enter_context(nc.sbuf_tensor(f"route{layer}_" + name, shape, dt))

        rows = sb("rows", [P, NT, D])
        s, gr, msk, o1, o2, on, tmp, past = (sb(n, [P, NT, NE]) for n in
                                             ("scores", "biased", "masked", "one1", "one2", "both", "tmp", "past"))
        pair, keep, off = sb("pair", [P, 2, G]), sb("keep", [P, NT, NG]), sb("off", [P, NT, NG])
        top = sb("top", [P, NT])
        wsum, dst = sb("wsum", [P, NT]), sb("dst", [P, 2, NT])
        nb, cs, start, down = sb("more_blocks", [P, NE]), sb("cumulated", [P, 2, NE]), sb("start", [P, NE]), sb("countdown", [P, NE])
        cmp, eb, tn = sb("compare", [P, NBLK - NE, NE]), sb("block_e", [P, NBLK]), sb("turns", [P, 2])
        logits_t = sb("logits_t", [NE, T])
        by_expert, copied, logits, ranks, turned, taken, expd, chain, scattered = sems(
            nc, st, f"route{layer}", ["by_expert", "copied", "logits", "ranks", "turned", "taken", "exp", "chain", "scattered"])
        with nc.Block(no_gpsimd_drain=True) as block:
            mark = {}

            @block.vector
            def _(dve):
                n = 0

                def link(ins):
                    nonlocal n
                    n += 1
                    ins.then_inc(chain, 1)
                    dve.wait_ge(chain, n)

                def over(x, n=NE):
                    return x.unsqueeze(2).to_broadcast([P, NT, n])

                def tiles(x, n=NE):
                    return x.unsqueeze(1).to_broadcast([P, NT, n])

                def first_best(one, values, n):
                    link(dve.tensor_reduce(top[:, :], values, AX.X, ALU.max))
                    link(dve.tensor_tensor(one, values, over(top[:, :], n), ALU.is_equal))
                    link(dve.tensor_tensor(one, one, tiles(down[:, NE - n:NE], n), ALU.mult))
                    link(dve.tensor_reduce(top[:, :], one, AX.X, ALU.max))
                    link(dve.tensor_tensor(one, one, over(top[:, :], n), ALU.is_equal))

                link(dve.tensor_scalar(down[:, :], c.base["iota16"], -1.0, float(NE), ALU.mult, ALU.add))
                dve.wait_ge(expd, 1)
                link(dve.tensor_scalar(s[:, :, :], s[:, :, :], 1.0, None, ALU.add))
                link(dve.reciprocal(s[:, :, :], s[:, :, :]))
                link(dve.tensor_tensor(gr[:, :, :], s[:, :, :], tiles(c.router_b[:, :]), ALU.add))
                m = gr[:, :, :].rearrange("p t (g e) -> p (t g) e", e=EG)
                link(dve.tensor_tensor(pair[:, 0, :], m[:, :, 0], m[:, :, 1], ALU.add))
                for a in range(EG):
                    for b in range(max(a + 1, 2), EG):
                        link(dve.tensor_tensor(pair[:, 1, :], m[:, :, a], m[:, :, b], ALU.add))
                        link(dve.tensor_tensor(pair[:, 0, :], pair[:, 0, :], pair[:, 1, :], ALU.max))
                first_best(keep[:, :, :], pair[:, 0, :].rearrange("p (t g) -> p t g", t=NT), NG)
                link(dve.tensor_scalar(off[:, :, :], keep[:, :, :], -1.0, BIG, ALU.add, ALU.mult))
                for x, op in ((keep, ALU.mult), (off, ALU.add)):
                    link(dve.tensor_tensor(msk[:, :, :].rearrange("p t (g e) -> p (t g) e", e=EG), m if x is keep else
                                           msk[:, :, :].rearrange("p t (g e) -> p (t g) e", e=EG),
                                           x[:, :, :].rearrange("p t g -> p (t g)").unsqueeze(2).to_broadcast([P, G, EG]), op))
                first_best(o1[:, :, :], msk[:, :, :], NE)
                link(dve.scalar_tensor_tensor(out=msk[:, :, :], in0=o1[:, :, :], scalar=-BIG, in1=msk[:, :, :],
                                              op0=ALU.mult, op1=ALU.add))
                first_best(o2[:, :, :], msk[:, :, :], NE)
                link(dve.tensor_tensor(on[:, :, :], o1[:, :, :], o2[:, :, :], ALU.add))
                mark["onehot"] = n
                for k, o in enumerate((o1, o2)):
                    link(dve.tensor_tensor(tmp[:, :, :], o[:, :, :], s[:, :, :], ALU.mult))
                    link(dve.tensor_reduce(c.w12[:, k, :], tmp[:, :, :], AX.X, ALU.add))
                link(dve.tensor_tensor(wsum[:, :], c.w12[:, 0, :], c.w12[:, 1, :], ALU.add))
                link(dve.reciprocal(wsum[:, :], wsum[:, :]))
                for k in range(2):
                    link(dve.tensor_tensor(c.w12[:, k, :], c.w12[:, k, :], wsum[:, :], ALU.mult))
                dve.wait_ge(ranks, 1)
                count = ps[:, 6, 0:NE]
                link(dve.tensor_scalar(nb[:, :], count, float(P), None, ALU.is_gt))
                for b in range(2, NT):
                    link(dve.scalar_tensor_tensor(out=nb[:, :], in0=count, scalar=float(b * P), in1=nb[:, :],
                                                  op0=ALU.is_gt, op1=ALU.add))
                link(dve.tensor_copy(cs[:, 0, :], nb[:, :]))
                a = 0
                for sh in (1, 2, 4, 8):
                    link(dve.tensor_copy(cs[:, 1 - a, 0:sh], cs[:, a, 0:sh]))
                    link(dve.tensor_tensor(cs[:, 1 - a, sh:NE], cs[:, a, sh:NE], cs[:, a, 0:NE - sh], ALU.add))
                    a = 1 - a
                link(dve.tensor_tensor(start[:, :], cs[:, a, :], nb[:, :], ALU.subtract))
                link(dve.tensor_tensor(start[:, :], start[:, :], c.base["iota16"], ALU.subtract))
                link(dve.tensor_scalar(start[:, :], start[:, :], float(NE - 1), float(P), ALU.add, ALU.mult))
                rank = ps[:, 1, 0:NT * NE].rearrange("p (t e) -> p t e", t=NT)
                link(dve.tensor_scalar(past[:, :, :], rank, float(P), None, ALU.is_ge))
                link(dve.tensor_tensor(past[:, :, :], past[:, :, :], tiles(start[:, :]), ALU.mult))
                link(dve.tensor_tensor(tmp[:, :, :], past[:, :, :], rank, ALU.add))
                link(dve.scalar_tensor_tensor(out=tmp[:, :, :], in0=tiles(c.base["iota16"]), scalar=float(P), in1=tmp[:, :, :],
                                              op0=ALU.mult, op1=ALU.add))
                for k, o in enumerate((o1, o2)):
                    link(dve.tensor_tensor(o[:, :, :], o[:, :, :], tmp[:, :, :], ALU.mult))
                    link(dve.tensor_reduce(dst[:, k, :], o[:, :, :], AX.X, ALU.add))
                link(dve.tensor_copy(c.dest[:, :, :], dst[:, :, :]))
                mark["dest"] = n
                link(dve.tensor_tensor(cmp[:, :, :], cs[:, a, :].unsqueeze(1).to_broadcast([P, NBLK - NE, NE]),
                                       c.base["iotab"][:, 0:NBLK - NE].unsqueeze(2).to_broadcast([P, NBLK - NE, NE]), ALU.is_le))
                link(dve.tensor_copy(eb[:, 0:NE], c.base["iota16"]))
                link(dve.tensor_reduce(eb[:, NE:NBLK], cmp[:, :, :], AX.X, ALU.add))
                link(dve.tensor_scalar(c.blk_e[:, :], eb[:, :], float(NE - 1), None, ALU.min))
                link(dve.tensor_scalar(cmp[:, :, 0], c.base["iotab"][:, 0:NBLK - NE], 2.0, None, ALU.mult))
                link(dve.tensor_tensor(cmp[:, :, 1], cmp[:, :, 0], cs[:, a, NE - 1:NE].to_broadcast([P, NBLK - NE]), ALU.is_lt))
                link(dve.tensor_reduce(tn[:, 0:1], cmp[:, :, 1], AX.X, ALU.add))
                for less in range(3):
                    link(dve.tensor_scalar(c.turns[:, less:less + 1], tn[:, 0:1], float(NE // 2 - less), None, ALU.add))

            @block.tensor
            def _(pe):
                for r, (a, n, _) in enumerate(RANGES):
                    for k in range(KD):
                        mm = pe.matmul(ps[0:NE, 6 + r, 0:n], c.router[:, k, :], c.h[:, k, a:a + n],
                                       start=(k == 0), stop=(k == KD - 1))
                    mm.then_inc(by_expert, 1)
                pe.wait_ge(copied, 2)
                for t in range(NT):
                    mm = pe.transpose(ps[:, 0, t * NE:(t + 1) * NE], logits_t[:, t * P:(t + 1) * P], c.base["ident"][0:NE, 0:NE])
                mm.then_inc(logits, 1)
                for g in range(2 * NT):
                    if g >= 4:
                        pe.wait_ge(taken, g - 3)
                    for k in range(4):
                        mm = pe.transpose(ps[:, 2 + g % 4, k * P:(k + 1) * P],
                                          c.h[:, 4 * (g % 2) + k, (g // 2) * P:(g // 2 + 1) * P], c.base["ident"])
                    mm.then_inc(turned, 1)
                pe.wait_ge(chain, mark["onehot"])
                flat = on[:, :, :].rearrange("p t e -> p (t e)")
                pe.matmul(ps[:, 1, 0:NT * NE], c.base["before"], flat, start=True, stop=False)
                for back in range(1, NT):
                    pe.matmul(ps[:, 1, back * NE:NT * NE], c.base["ones"], flat[:, 0:(NT - back) * NE],
                              start=False, stop=(back == NT - 1))
                for t in range(NT):
                    mm = pe.matmul(ps[:, 6, 0:NE], c.base["ones"], on[:, t, :], start=(t == 0), stop=(t == NT - 1))
                mm.then_inc(ranks, 1)

            @block.scalar
            def _(act):
                for r, (a, n, _) in enumerate(RANGES):
                    act.wait_ge(by_expert, r + 1)
                    nc.scalar.copy(logits_t[:, a:a + n], ps[0:NE, 6 + r, 0:n]).then_inc(copied, 1)
                act.wait_ge(logits, 1)
                nc.scalar.activation(s[:, :, :], ps[:, 0, 0:NT * NE].rearrange("p (t e) -> p t e", t=NT), ACT.Exp,
                                     scale=-1.0).then_inc(expd, 1)
                for g in range(2 * NT):
                    act.wait_ge(turned, g + 1)
                    nc.scalar.copy(rows[:, g // 2, 512 * (g % 2):512 * (g % 2 + 1)], ps[:, 2 + g % 4, :]).then_inc(taken, 1)

            @block.gpsimd
            def _(pool):
                pool.wait_ge(chain, mark["dest"])
                for t in range(NT):
                    pool.wait_ge(taken, 2 * t + 2)
                    for k in range(TOPK):
                        pool.indirect_dma_start(c.xs, bass.IndirectOffsetOnAxis(c.dest[:, k, t:t + 1], 0),
                                                rows[:, t, :], None).then_inc(scattered, 16)
                pool.wait_ge(scattered, 16 * NT * TOPK)


def expert_slots(c):
    return [[c.slot(3 * u).rearrange("p (k n) -> p k n", k=KD), c.slot(3 * u + 1).rearrange("p (k n) -> p k n", k=KD),
             c.slot(3 * u + 2).rearrange("p (k n) -> p k n", k=4)] for u in range(2)]


def load_expert(c, sp, layer, e, u, w):
    src = c.ops[("moe_w_gate", "moe_w_up", "moe_w_down")[w]][layer].rearrange("e (k p) n -> e p k n", p=P)
    sp.dma_start(expert_slots(c)[u][w], src[bass.ds(e, 1)].rearrange("a p k n -> (a p) k n")).then_inc(c.moe_full[layer][3 * u + w], 16)


def experts(c, layer):
    nc, ops, ps = c.nc, c.ops, c.ps
    UN, BUF = 12, 4
    flat = c.h[:, :, :].rearrange("p k n -> p (k n)")
    xr = flat[:, 0:2 * D].rearrange("p (u n) -> p u n", u=2)
    y = flat[:, 2 * D:4 * D].rearrange("p (u n) -> p u n", u=2)
    with ExitStack() as st:
        def sb(name, shape, dt=F32):
            return st.enter_context(nc.sbuf_tensor(f"moe{layer}_" + name, shape, dt))

        whi, wlo = sb("w_hi", [P, BUF, 1024], F32R), sb("w_lo", [P, BUF, 1024], F32R)
        xhi, xlo = sb("rows_t_hi", [P, 2, KD, P], F32R), sb("rows_t_lo", [P, 2, KD, P], F32R)
        hhi, hlo = sb("hidden_t_hi", [P, 4, P], F32R), sb("hidden_t_lo", [P, 4, P], F32R)
        sil, hid = sb("silu", [P, FE]), sb("hidden", [P, FE])
        xfull = sems(nc, st, f"moe{layer}", ["x_full0", "x_full1"])
        wfull = c.moe_full[layer]
        stored = sems(nc, st, f"moe{layer}", ["stored0", "stored1"])
        turned, used, hturned, w_hi, w_lo, x_hi, x_lo, silued, hidden, h_hi, h_lo, ya, yv = sems(
            nc, st, f"moe{layer}", ["x_turned", "w_used", "h_turned", "w_hi", "w_lo", "x_hi", "x_lo", "silu", "hidden",
                                    "h_hi", "h_lo", "y_act", "y_dve"])
        wslot = expert_slots(c)

        def part(u, x):
            w = wslot[u][x // 4]
            return w[:, 2 * (x % 4):2 * (x % 4) + 2, :].rearrange("p k n -> p (k n)") if x < 8 else w[:, x - 8, :]

        def turns(eng, less=0):
            return eng.value_load(c.turns[0:1, less:less + 1], min_val=NE // 2 - less, max_val=NBLK // 2 - less)

        def at(i, d):
            return (i * 2 + d, d % 2, i + d // 2)

        GATE, UP, DOWN = 0, 4, 8

        with nc.Block(no_gpsimd_drain=True) as block:
            @block.gpsimd
            def _(pool):
                def load_rows(blk):
                    b, u, _ = blk
                    pool.dma_start(xr[:, u, :], c.xs.rearrange("(b p) d -> b p d", p=P)[bass.ds(b, 1)].rearrange("a p d -> (a p) d"))\
                        .then_inc(xfull[u], 16)

                def refill_rows(blk):
                    pool.wait_ge(turned, blk[0] - 1)
                    load_rows(blk)

                load_rows(at(0, 0))
                load_rows(at(0, 1))
                pen = turns(pool, 2)
                refill_rows(at(0, 2))
                refill_rows(at(0, 3))
                with pool.Fori(0, pen) as i:
                    for d in (1, 2):
                        refill_rows(at(i, d + 3))
                for u in range(2):
                    pool.wait_ge(stored[u], pen * 16 + 48)

            @block.sync
            def _(sp):
                def expert(blk):
                    return sp.value_load(c.blk_e[0:1, bass.ds(blk[0], 1)], min_val=0, max_val=NE - 1)

                def refill(step, unit, e, u, w):
                    sp.wait_ge(w_lo, step * UN + (unit + 4))
                    load_expert(c, sp, layer, e, u, w)

                def refill_after(s, before, now, after):
                    if before:
                        refill(s, 0, expert(before), before[1], 2)
                    refill(s, 4, expert(now), now[1], 1)
                    if after:
                        refill(s, 8, expert(after), after[1], 0)

                pen = turns(sp, 2)
                sp.wait_ge(w_lo, 4)
                load_expert(c, sp, layer, expert(at(0, 2)), 0, 0)
                refill_after(0, None, at(0, 2), at(0, 3))
                with sp.Fori(0, pen) as i:
                    for d in (3, 4):
                        refill_after(i * 2 + (d - 2), at(i, d - 1), at(i, d), at(i, d + 1))
                refill_after(pen * 2 + 1, at(pen, 2), at(pen, 3), None)
                refill(pen * 2 + 2, 0, expert(at(pen, 3)), 1, 2)

            @block.tensor
            def _(pe):
                def turn_rows(blk):
                    b, u, i = blk
                    pe.wait_ge(xfull[u], i * 16 + 16)
                    pe.wait_ge(x_lo, b + 1)
                    for k in range(KD):
                        mm = pe.transpose(ps[:, k // 4, (k % 4) * P:(k % 4 + 1) * P], xr[:, u, k * P:(k + 1) * P], c.base["ident"])
                    mm.then_inc(turned, 1)

                def turn_hidden(blk):
                    pe.wait_ge(hidden, blk[0] + 2)
                    pe.wait_ge(h_lo, blk[0] + 1)
                    for k in range(4):
                        mm = pe.transpose(ps[:, 4, k * P:(k + 1) * P], hid[:, k * P:(k + 1) * P], c.base["ident"])
                    mm.then_inc(hturned, 1)

                def three(out, hi, lo, first, last):
                    for x, (lhs, rhs) in enumerate(((hi[0], hi[1]), (hi[0], lo[1]), (lo[0], hi[1]))):
                        mm = pe.matmul(out, lhs, rhs, start=(first and x == 0), stop=(last and x == 2))
                    return mm

                def gate_or_up(blk, bank, step, unit, x):
                    u = blk[1]
                    pe.wait_ge(w_lo, step * UN + (unit + x + 1))
                    for k in range(2):
                        kk, cols = 2 * x + k, slice(k * 512, (k + 1) * 512)
                        mm = three(ps[:, bank, :], (xhi[:, u, kk, :], whi[:, x, cols]),
                                   (xlo[:, u, kk, :], wlo[:, x, cols]), kk == 0, kk == KD - 1)
                    mm.then_inc(used, 1)

                def gate(blk, step, unit, xs):
                    if xs[0] == 0:
                        pe.wait_ge(x_lo, blk[0] + 2)
                        pe.wait_ge(silued, blk[0] + 1)
                    for x in xs:
                        gate_or_up(blk, 2, step, unit, x)

                def up(blk):
                    pe.wait_ge(x_lo, blk[0] + 2)
                    pe.wait_ge(hidden, blk[0] + 1)
                    for x in range(4):
                        gate_or_up(blk, 3, blk[0], 4, x)

                def down(blk, step, unit):
                    pe.wait_ge(h_lo, blk[0] + 2)
                    pe.wait_ge(ya, blk[0] + 1)
                    pe.wait_ge(yv, blk[0] + 1)
                    for k in range(4):
                        pe.wait_ge(w_lo, step * UN + (unit + k + 1))
                        for n in range(2):
                            cols = slice(n * 512, (n + 1) * 512)
                            mm = three(ps[:, 5 + n, :], (hhi[:, k, :], whi[:, k, cols]),
                                       (hlo[:, k, :], wlo[:, k, cols]), k == 0, k == 3)
                        mm.then_inc(used, 1)

                def up_and_gate(now, after):
                    turn_rows(after)
                    up(now)
                    gate(after, now[0], 8, (0, 1))
                    turn_hidden(now)
                    gate(after, now[0], 8, (2, 3))

                pe.sem_inc(hturned, 1)
                pe.sem_inc(used, BUF)
                last = turns(pe, 1)
                turn_rows(at(0, 0))
                gate(at(0, 0), 0, 0, (0, 1, 2, 3))
                up_and_gate(at(0, 0), at(0, 1))
                with pe.Fori(0, last) as i:
                    for d in (1, 2):
                        down(at(i, d - 1), i * 2 + d, 0)
                        up_and_gate(at(i, d), at(i, d + 1))
                down(at(last, 0), last * 2 + 1, 0)
                up(at(last, 1))
                turn_hidden(at(last, 1))
                down(at(last, 1), last * 2 + 1, 8)

            @block.scalar
            def _(act):
                def split(blk, w, step, unit, xs=range(4)):
                    _, u, i = blk
                    for x in xs:
                        act.wait_ge(wfull[3 * u + w // 4], i * 16 + 16)
                        act.wait_ge(used, step * UN + (unit + x + 1))
                        nc.scalar.activation(whi[:, x, :], part(u, w + x), ACT.Identity).then_inc(w_hi, 1)

                def take_x(blk):
                    act.wait_ge(turned, blk[0] + 1)
                    nc.scalar.activation(xhi[:, blk[1], :, :], ps[:, 0:2, :].rearrange("p a (k n) -> p (a k) n", k=4), ACT.Identity).then_inc(x_hi, 1)

                def take_hidden(blk):
                    act.wait_ge(hturned, blk[0] + 2)
                    nc.scalar.activation(hhi[:, :, :], ps[:, 4, :].rearrange("p (k n) -> p k n", k=4), ACT.Identity).then_inc(h_hi, 1)

                def silu(blk, gate_made):
                    act.wait_ge(used, gate_made)
                    act.wait_ge(hidden, blk[0] + 1)
                    nc.scalar.activation(sil[:, :], ps[:, 2, :], ACT.Silu).then_inc(silued, 1)

                def take_y(blk, down_made):
                    b, u, i = blk
                    act.wait_ge(used, down_made)
                    act.wait_ge(stored[u], i * 16 + 16)
                    nc.scalar.copy(y[:, u, 0:512], ps[:, 5, :]).then_inc(ya, 1)

                def store(blk):
                    b, u, _ = blk
                    act.wait_ge(ya, b + 2)
                    act.wait_ge(yv, b + 2)
                    act.dma_start(c.ys.rearrange("(b p) d -> b p d", p=P)[bass.ds(b, 1)].rearrange("a p d -> (a p) d"), y[:, u, :])\
                        .then_inc(stored[u], 16)

                def step(before, now, after):
                    s = now[0]
                    split(before, DOWN, s, 0, (0, 1))
                    take_hidden(before)
                    split(before, DOWN, s, 0, (2, 3))
                    silu(now, s * UN + BUF)
                    split(now, UP, s, 4)
                    if after:
                        take_x(after)
                        split(after, GATE, s, 8, (0,))
                        take_y(before, s * UN + (4 + BUF))
                        split(after, GATE, s, 8, (1, 2, 3))
                    else:
                        take_y(before, s * UN + (4 + BUF))
                    store(before)

                for ahead in (silued, ya):
                    act.sem_inc(ahead, 1)
                for ahead in stored:
                    act.sem_inc(ahead, 16)
                last = turns(act, 1)
                split(at(0, 0), GATE, 0, 0)
                take_x(at(0, 0))
                split(at(0, 0), UP, 0, 4)
                silu(at(0, 0), 4 + BUF)
                take_x(at(0, 1))
                split(at(0, 1), GATE, 0, 8)
                with act.Fori(0, last) as i:
                    for d in (1, 2):
                        step(at(i, d - 1), at(i, d), at(i, d + 1))
                step(at(last, 0), at(last, 1), None)
                split(at(last, 1), DOWN, last * 2 + 1, 8)
                take_hidden(at(last, 1))
                take_y(at(last, 1), last * (2 * UN) + (2 * UN + BUF))
                store(at(last, 1))

            @block.vector
            def _(dve):
                def split(blk, w, step, unit, xs=range(4)):
                    for x in xs:
                        dve.wait_ge(w_hi, step * UN + (unit + x + 1))
                        dve.tensor_tensor(wlo[:, x, :], part(blk[1], w + x), whi[:, x, :].bitcast(F32), ALU.subtract).then_inc(w_lo, 1)

                def take_x(blk):
                    b, u, _ = blk
                    dve.wait_ge(x_hi, b + 1)
                    dve.tensor_tensor(xlo[:, u, :, :], ps[:, 0:2, :].rearrange("p a (k n) -> p (a k) n", k=4),
                                      xhi[:, u, :, :].bitcast(F32), ALU.subtract).then_inc(x_lo, 1)

                def take_hidden(blk):
                    dve.wait_ge(h_hi, blk[0] + 1)
                    dve.tensor_tensor(hlo[:, :, :], ps[:, 4, :].rearrange("p (k n) -> p k n", k=4), hhi[:, :, :].bitcast(F32),
                                      ALU.subtract).then_inc(h_lo, 1)

                def make_hidden(blk):
                    b = blk[0]
                    dve.wait_ge(silued, b + 2)
                    dve.wait_ge(used, b * UN + (8 + BUF))
                    dve.wait_ge(hturned, b + 1)
                    dve.tensor_tensor(hid[:, :], sil[:, :], ps[:, 3, :], ALU.mult).then_inc(hidden, 1)

                def take_y(blk, down_made):
                    b, u, i = blk
                    dve.wait_ge(used, down_made)
                    dve.wait_ge(stored[u], i * 16 + 16)
                    dve.tensor_copy(y[:, u, 512:1024], ps[:, 6, :]).then_inc(yv, 1)

                def step(before, now, after):
                    s = now[0]
                    split(before, DOWN, s, 0, (0, 1))
                    take_hidden(before)
                    split(before, DOWN, s, 0, (2, 3))
                    split(now, UP, s, 4)
                    if after:
                        take_x(after)
                        split(after, GATE, s, 8, (0,))
                        take_y(before, s * UN + (4 + BUF))
                        split(after, GATE, s, 8, (1, 2, 3))
                        make_hidden(now)
                    else:
                        take_y(before, s * UN + (4 + BUF))

                for ahead in (x_lo, hidden, h_lo, yv):
                    dve.sem_inc(ahead, 1)
                last = turns(dve, 1)
                split(at(0, 0), GATE, 0, 0)
                take_x(at(0, 0))
                split(at(0, 0), UP, 0, 4)
                take_x(at(0, 1))
                split(at(0, 1), GATE, 0, 8)
                make_hidden(at(0, 0))
                with dve.Fori(0, last) as i:
                    for d in (1, 2):
                        step(at(i, d - 1), at(i, d), at(i, d + 1))
                step(at(last, 0), at(last, 1), None)
                split(at(last, 1), DOWN, last * 2 + 1, 8)
                make_hidden(at(last, 1))
                take_hidden(at(last, 1))
                take_y(at(last, 1), last * (2 * UN) + (2 * UN + BUF))


def combine(c, layer):
    nc, ps = c.nc, c.ps
    gate = c.mod[:, layer, 40:48, :]
    with ExitStack() as st:
        y = st.enter_context(nc.sbuf_tensor(f"comb{layer}_rows", [P, NT, TOPK, D], F32))
        got = sems(nc, st, f"comb{layer}", [f"got{t}" for t in range(NT)])
        weighed, summed, turned, added = sems(nc, st, f"comb{layer}", ["weighed", "summed", "turned", "added"])
        with nc.Block(no_gpsimd_drain=True) as block:
            @block.gpsimd
            def _(pool):
                for t in range(NT):
                    for k in range(TOPK):
                        pool.indirect_dma_start(y[:, t, k, :], None, c.ys,
                                                bass.IndirectOffsetOnAxis(c.dest[:, k, t:t + 1], 0)).then_inc(got[t], 16)

            @block.scalar
            def _(act):
                for t in range(NT):
                    act.wait_ge(got[t], 16 * TOPK)
                    nc.scalar.activation(y[:, t, 0, :], y[:, t, 0, :], ACT.Identity, scale=c.w12[:, 0, t:t + 1]).then_inc(weighed, 1)

            @block.tensor
            def _(pe):
                for t in range(NT):
                    pe.wait_ge(summed, t + 1)
                    if t >= 4:
                        pe.wait_ge(added, (t - 3) * KD)
                    for k in range(KD):
                        mm = pe.transpose(ps[:, 2 * (t % 4) + k // 4, (k % 4) * P:(k % 4 + 1) * P],
                                          y[:, t, 0, k * P:(k + 1) * P], c.base["ident"])
                    mm.then_inc(turned, 1)

            @block.vector
            def _(dve):
                for t in range(NT + 1):
                    if t < NT:
                        dve.wait_ge(weighed, t + 1)
                        dve.scalar_tensor_tensor(out=y[:, t, 0, :], in0=y[:, t, 1, :], scalar=c.w12[:, 1, t:t + 1],
                                                 in1=y[:, t, 0, :], op0=ALU.mult, op1=ALU.add).then_inc(summed, 1)
                    if t:
                        n = t - 1
                        dve.wait_ge(turned, n + 1)
                        jc = 0 if n == 0 else 1
                        for k in range(KD):
                            cols = slice(n * P, (n + 1) * P)
                            dve.scalar_tensor_tensor(out=c.x[:, k, cols], in0=ps[:, 2 * (n % 4) + k // 4, (k % 4) * P:(k % 4 + 1) * P],
                                                     scalar=gate[:, k, jc:jc + 1], in1=c.x[:, k, cols],
                                                     op0=ALU.mult, op1=ALU.add).then_inc(added, 1)


def write_out(c):
    nc, ops, ps = c.nc, c.ops, c.ps
    with ExitStack() as st:
        rows = st.enter_context(nc.sbuf_tensor("out_rows", [P, NT, D], F32))
        turned, taken, taken_v, out_s = sems(nc, st, "out", ["turned", "act", "dve", "stored"])
        with nc.Block(no_gpsimd_drain=True) as block:
            @block.tensor
            def _(pe):
                for g in range(2 * NT):
                    if g >= 8:
                        pe.wait_ge(taken, (g - 8) // 2 + 1)
                        pe.wait_ge(taken_v, (g - 8) // 2 + 1)
                    for k in range(4):
                        mm = pe.transpose(ps[:, g % 8, k * P:(k + 1) * P],
                                          c.h[:, 4 * (g % 2) + k, (g // 2) * P:(g // 2 + 1) * P], c.base["ident"])
                    mm.then_inc(turned, 1)

            @block.scalar
            def _(act):
                for g in range(0, 2 * NT, 2):
                    act.wait_ge(turned, g + 1)
                    nc.scalar.copy(rows[:, g // 2, 0:512], ps[:, g % 8, :]).then_inc(taken, 1)

            @block.vector
            def _(dve):
                for g in range(1, 2 * NT, 2):
                    dve.wait_ge(turned, g + 1)
                    dve.tensor_copy(rows[:, g // 2, 512:1024], ps[:, g % 8, :]).then_inc(taken_v, 1)

            @block.sync
            def _(sp):
                for t in range(NT):
                    sp.wait_ge(taken, t + 1)
                    sp.wait_ge(taken_v, t + 1)
                    dst = ops["y_prompt"][0] if t == 0 else ops["y_sample"][0, (t - 1) * P:t * P]
                    sp.dma_start(dst, rows[:, t, :]).then_inc(out_s, 16)
                sp.wait_ge(out_s, 16 * NT)


def trunk_step(nc, ops):
    with ExitStack() as stack:
        c = Chip(nc, stack, ops)

        def load_mla(sp, split, per, n):
            for s, load in ((4, lambda: load_mla_in(c, sp, 0)), (0, lambda: load_mla_q(c, sp, 0, 0)),
                            (1, lambda: load_mla_kv(c, sp, 0, 0)), (2, lambda: load_mla_o(c, sp, 0, 0))):
                last = max(x for x in range(n) if x % NSLOT == s)
                sp.wait_ge(split, per * (last + 1))
                load()

        with ExitStack() as st:
            cond4 = st.enter_context(nc.sbuf_tensor("cond_parts", [P, KD, 4], F32R))
            setup(c, cond4)
            modulation(c, cond4, load_mla)
        counters = [0, 0]
        for layer in range(DEPTH):
            kind = layer % 3
            amp, shift = c.amp[:, layer, 0], c.mod[:, layer, 0:8, :]
            if kind == 0:
                norm(c, 2 * layer, amp, shift)
                mla(c, layer, counters[kind])
            else:
                with ExitStack() as st:
                    parts = [st.enter_context(nc.sbuf_tensor(f"h_{n}{layer}", [P, KD, T], F32R)) for n in ("hi", "lo")]
                    consts = st.enter_context(nc.sbuf_tensor("ret_consts", [P, _width(RET_COLS)], F32))[:, :]
                    norm(c, 2 * layer, amp, shift, lambda sp: load_ret_first(c, sp, counters[kind], consts), parts)
                    retention(c, layer, counters[kind], consts, *parts)
            counters[kind] += 1
            norm(c, 2 * layer + 1, c.amp[:, layer, 1], c.mod[:, layer, 24:32, :],
                 lambda sp: [load_expert(c, sp, layer, u, u, w) for u, w in ((0, 0), (0, 1), (1, 0), (0, 2), (1, 1), (1, 2))])
            route(c, layer)
            experts(c, layer)
            combine(c, layer)
        norm(c, 2 * DEPTH, c.fin2, c.zero2)
        write_out(c)


_INS = ["x_prompt", "x_sample", "cache_mla", "state_ret", "c", "c_ctx", "norm1_g", "norm2_g", "ada_w", "ada_b",
        "final_norm_g", "mla_w_in", "mla_q_norm_g", "mla_kv_norm_g", "mla_w_uq", "mla_w_ukv", "mla_w_o",
        "ret_w_in", "ret_decay_f", "ret_decay_b", "ret_w_o", "router_w", "router_b",
        "moe_w_gate", "moe_w_up", "moe_w_down"]
_CONSTS = ["base_consts", "mla_consts", "ret_consts", "trig_consts"]
_OUTS = {"y_prompt": (1, SEQ, D), "y_sample": (1, LAT, D), "new_cache": (1, 1, SEQ, KVL + ROPE),
         "new_state": (1, 1, 2, RH, DK, DV)}


def kernel(**inputs):
    import concourse.bacc as bacc
    from concourse.bass_utils import run_bass_kernel_spmd

    nc = bacc.Bacc("TRN2", target_bir_lowering=False, num_devices=1)
    arrays, ops = {}, {}
    for name, a in [(n, inputs[n]) for n in _INS] + list(zip(_CONSTS, shape_constants())):
        a = np.ascontiguousarray(a)
        arrays["in_" + name] = a
        ops[name] = nc.dram_tensor("in_" + name, a.shape, F32, kind="ExternalInput").ap()
    for name, shape in _OUTS.items():
        ops[name] = nc.dram_tensor("out_" + name, shape, F32, kind="ExternalOutput").ap()
    for name, blocks in (("rows_in", NBLK), ("rows_out", NBLK)):
        ops[name] = nc.dram_tensor(name, (blocks * P, D), F32, kind="Internal").ap()
    trunk_step(nc, ops)
    r = run_bass_kernel_spmd(nc, [arrays], core_ids=[0])
    return tuple(r.results[0]["out_" + name] for name in _OUTS)
```
